# Optimizing a Trainium2 kernel written in Bass

```python
import jax, jax.numpy as jnp
from jax import lax
import numpy as np

D_MODEL = 1024
BATCH = 1
SEQ = 512
DEPTH = 2

GRID_W = 64
CTX_LEN = 256
D_SSD = 1024
HEAD_DIM = 64
N_HEADS = D_SSD // HEAD_DIM
N_GROUPS = 4
HEADS_PER_GROUP = N_HEADS // N_GROUPS
D_STATE = 128
SSD_CONV = 5
CHUNK = 128
D_CONF = 1024
CONF_KERNEL = 31
D_MIX = D_SSD + D_CONF
XBC_DIM = D_SSD + 2 * N_GROUPS * D_STATE
SSD_IN_COLS = XBC_DIM + 2 * N_HEADS
Z_END = SSD_IN_COLS + D_SSD
IN_COLS = Z_END + 2 * D_CONF
N_EXPERTS = 16
CAPACITY_FACTOR = 2
D_EXPERT = 1408
EPS = 1e-6

kernel_name = 'hymba_ssd_conformer_ec_moe_dit'

def rms_norm(x, g):
    xf = x.astype(jnp.float32)
    y = xf * lax.rsqrt(jnp.mean(xf * xf, axis=-1, keepdims=True) + EPS)
    return (y * g.astype(jnp.float32)).astype(x.dtype)

def layer_norm(x, g, b):
    xf = x.astype(jnp.float32)
    xc = xf - jnp.mean(xf, axis=-1, keepdims=True)
    var = jnp.mean(xc * xc, axis=-1, keepdims=True)
    y = xc * lax.rsqrt(var + EPS) * g.astype(jnp.float32) + b.astype(jnp.float32)
    return y.astype(x.dtype)

def depthwise_conv(u, w, bias):
    k = w.shape[0]
    out = lax.conv_general_dilated(u, w[:, None, :].astype(u.dtype), window_strides=(1,),
                                   padding=[(k // 2, k // 2)],
                                   dimension_numbers=('NWC', 'WIO', 'NWC'),
                                   feature_group_count=u.shape[-1])
    return out + bias.astype(u.dtype)

def adaln(cond, ada_w, ada_b):
    return jnp.split(jax.nn.silu(cond) @ ada_w + ada_b, 6, axis=-1)

def _rev(t):
    return jnp.flip(t, axis=1)

def _ssd_prep(x, dt, a, bm):
    b, l = x.shape[:2]
    nc = l // CHUNK
    xdt = (x.astype(jnp.float32) * dt[..., None]).reshape(b, nc, CHUNK, N_GROUPS, HEADS_PER_GROUP, HEAD_DIM)
    bc = bm.astype(jnp.float32).reshape(b, nc, CHUNK, N_GROUPS, D_STATE)
    cum = jnp.cumsum((dt * a).reshape(b, nc, CHUNK, N_GROUPS, HEADS_PER_GROUP), axis=2)
    return xdt, bc, cum

def _ssd_inter_chunk(xdt, bc, cum, h0):
    to_end = jnp.exp(cum[:, :, -1:] - cum)
    states = jnp.einsum('bclgn,bclgr,bclgrp->bcgrpn', bc, to_end, xdt)
    chunk_decay = jnp.exp(cum[:, :, -1])

    def step(h, inp):
        st, dec = inp
        return dec[..., None, None] * h + st, h

    h_final, h_prev = lax.scan(step, h0, (jnp.moveaxis(states, 1, 0), jnp.moveaxis(chunk_decay, 1, 0)))
    return jnp.moveaxis(h_prev, 0, 1), h_final

def ssd_chunked(x, dt, a, bm, cm, h0):
    b, l = x.shape[:2]
    xdt, bc, cum = _ssd_prep(x, dt, a, bm)
    cc = cm.astype(jnp.float32).reshape(b, l // CHUNK, CHUNK, N_GROUPS, D_STATE)
    h_prev, h_final = _ssd_inter_chunk(xdt, bc, cum, h0)
    cum_t = jnp.moveaxis(cum, 2, -1)
    seg = cum_t[..., :, None] - cum_t[..., None, :]
    lower = jnp.tril(jnp.ones((CHUNK, CHUNK), dtype=bool))
    decay = jnp.exp(jnp.where(lower, seg, -jnp.inf))
    scores = jnp.einsum('bclgn,bcsgn->bcgls', cc, bc)
    y_diag = jnp.einsum('bcgrls,bcsgrp->bclgrp', scores[:, :, :, None] * decay, xdt)
    y_off = jnp.einsum('bclgn,bcgrpn,bclgr->bclgrp', cc, h_prev, jnp.exp(cum))
    return (y_diag + y_off).reshape(x.shape), h_final

def ssd_final_state(x, dt, a, bm, h0):
    xdt, bc, cum = _ssd_prep(x, dt, a, bm)
    return _ssd_inter_chunk(xdt, bc, cum, h0)[1]

def ssd_inputs(proj, conv_w, conv_b, dt_bias):
    b, l, _ = proj.shape
    xbc = jax.nn.silu(depthwise_conv(proj[..., :XBC_DIM], conv_w, conv_b))
    xs = xbc[..., :D_SSD].reshape(b, l, N_HEADS, HEAD_DIM)
    bm = xbc[..., D_SSD:D_SSD + N_GROUPS * D_STATE].reshape(b, l, N_GROUPS, D_STATE)
    cm = xbc[..., D_SSD + N_GROUPS * D_STATE:].reshape(b, l, N_GROUPS, D_STATE)
    dt_raw = proj[..., XBC_DIM:SSD_IN_COLS].astype(jnp.float32).reshape(b, l, 2, N_HEADS)
    dt = jax.nn.softplus(dt_raw + dt_bias.astype(jnp.float32))
    return xs, bm, cm, dt

def mixer_output(proj, xs, y, d_skip, ssd_norm_g, cm_dw_w, cm_dw_b, cm_ln_g, cm_ln_b, w_out):
    b, l, _ = proj.shape
    y = y + d_skip.astype(jnp.float32)[:, None] * xs.astype(jnp.float32)
    z = proj[..., SSD_IN_COLS:Z_END].astype(jnp.float32)
    y_ssd = rms_norm(y.reshape(b, l, D_SSD) * jax.nn.silu(z), ssd_norm_g).astype(proj.dtype)
    v = proj[..., Z_END:Z_END + D_CONF] * jax.nn.sigmoid(proj[..., Z_END + D_CONF:])
    v = jax.nn.silu(layer_norm(depthwise_conv(v, cm_dw_w, cm_dw_b), cm_ln_g, cm_ln_b))
    return jnp.concatenate([y_ssd, v.astype(proj.dtype)], axis=-1) @ w_out

def token_mixer(u_lat, u_ctx, w_in, conv_w, conv_b, dt_bias, a_log, d_skip, ssd_norm_g,
                cm_dw_w, cm_dw_b, cm_ln_g, cm_ln_b, w_out, with_ctx_out):
    b = u_lat.shape[0]
    a = -jnp.exp(a_log.astype(jnp.float32))
    h0 = jnp.zeros((b, N_GROUPS, HEADS_PER_GROUP, HEAD_DIM, D_STATE), jnp.float32)
    p_ctx = u_ctx @ (w_in if with_ctx_out else w_in[:, :SSD_IN_COLS])
    xs_c, bm_c, cm_c, dt_c = ssd_inputs(p_ctx, conv_w, conv_b, dt_bias)
    if with_ctx_out:
        yf_c, hf_c = ssd_chunked(xs_c, dt_c[:, :, 0], a[0], bm_c, cm_c, h0)
        yb_c, hb_c = ssd_chunked(_rev(xs_c), _rev(dt_c[:, :, 1]), a[1], _rev(bm_c), _rev(cm_c), h0)
        m_ctx = mixer_output(p_ctx, xs_c, yf_c + _rev(yb_c), d_skip, ssd_norm_g,
                             cm_dw_w, cm_dw_b, cm_ln_g, cm_ln_b, w_out)
    else:
        hf_c = ssd_final_state(xs_c, dt_c[:, :, 0], a[0], bm_c, h0)
        hb_c = ssd_final_state(_rev(xs_c), _rev(dt_c[:, :, 1]), a[1], _rev(bm_c), h0)
        m_ctx = None
    p_lat = u_lat @ w_in
    xs_l, bm_l, cm_l, dt_l = ssd_inputs(p_lat, conv_w, conv_b, dt_bias)
    yf_l, _ = ssd_chunked(xs_l, dt_l[:, :, 0], a[0], bm_l, cm_l, hf_c)
    yb_l, _ = ssd_chunked(_rev(xs_l), _rev(dt_l[:, :, 1]), a[1], _rev(bm_l), _rev(cm_l), hb_c)
    m_lat = mixer_output(p_lat, xs_l, yf_l + _rev(yb_l), d_skip, ssd_norm_g,
                         cm_dw_w, cm_dw_b, cm_ln_g, cm_ln_b, w_out)
    return m_lat, m_ctx

def expert_choice_ffn(u, router_w, w_gate, w_up, w_down):
    b, n, d = u.shape
    cap = max(1, CAPACITY_FACTOR * n // N_EXPERTS)
    affinity = jax.nn.softmax((u @ router_w).astype(jnp.float32), axis=-1)
    gate, idx = lax.top_k(jnp.swapaxes(affinity, 1, 2), cap)
    sel = jax.vmap(lambda ub, ib: ub[ib])(u, idx)
    hdn = jax.nn.silu(jnp.einsum('becd,edf->becf', sel, w_gate)) * jnp.einsum('becd,edf->becf', sel, w_up)
    out = jnp.einsum('becf,efd->becd', hdn, w_down) * gate[..., None]
    y = jax.vmap(lambda ib, ob: jnp.zeros((n, d), ob.dtype).at[ib.reshape(-1)].add(ob.reshape(-1, d)))(idx, out)
    return y.astype(u.dtype)

def setup_inputs(seed: int = 0) -> dict:
    key = jax.random.key(seed)
    ks = jax.random.split(key, 26)
    f32 = jnp.float32
    nrm = lambda k, shape, s: jax.random.normal(k, shape, f32) * s
    dt_init = jnp.exp(jax.random.uniform(ks[10], (DEPTH, 2, N_HEADS), f32, np.log(1e-3), np.log(1e-1)))
    return {
        'x': nrm(ks[0], (BATCH, SEQ, D_MODEL), 1.0),
        'c': nrm(ks[1], (BATCH, D_MODEL), 1.0),
        'ctx': nrm(ks[2], (BATCH, CTX_LEN, D_MODEL), 1.0),
        'c_ctx': nrm(ks[3], (D_MODEL,), 1.0),
        'ada_w': nrm(ks[4], (DEPTH, D_MODEL, 6 * D_MODEL), 0.5 * D_MODEL ** -0.5),
        'ada_b': nrm(ks[5], (DEPTH, 6 * D_MODEL), 0.01),
        'mix_pre_g': 1.0 + nrm(ks[6], (DEPTH, D_MODEL), 0.05),
        'w_in': nrm(ks[7], (DEPTH, D_MODEL, IN_COLS), D_MODEL ** -0.5),
        'conv_w': nrm(ks[8], (DEPTH, SSD_CONV, XBC_DIM), SSD_CONV ** -0.5),
        'conv_b': nrm(ks[9], (DEPTH, XBC_DIM), 0.01),
        'dt_bias': dt_init + jnp.log(-jnp.expm1(-dt_init)),
        'a_log': jnp.log(jax.random.uniform(ks[11], (DEPTH, 2, N_HEADS), f32, 1.0, 16.0)),
        'd_skip': 1.0 + nrm(ks[12], (DEPTH, N_HEADS), 0.1),
        'ssd_norm_g': 1.0 + nrm(ks[13], (DEPTH, D_SSD), 0.05),
        'cm_dw_w': nrm(ks[14], (DEPTH, CONF_KERNEL, D_CONF), CONF_KERNEL ** -0.5),
        'cm_dw_b': nrm(ks[15], (DEPTH, D_CONF), 0.01),
        'cm_ln_g': 1.0 + nrm(ks[16], (DEPTH, D_CONF), 0.05),
        'cm_ln_b': nrm(ks[17], (DEPTH, D_CONF), 0.01),
        'w_out': nrm(ks[18], (DEPTH, D_MIX, D_MODEL), D_MIX ** -0.5),
        'mix_post_g': 1.0 + nrm(ks[19], (DEPTH, D_MODEL), 0.05),
        'moe_pre_g': 1.0 + nrm(ks[20], (DEPTH, D_MODEL), 0.05),
        'router_w': nrm(ks[21], (DEPTH, D_MODEL, N_EXPERTS), D_MODEL ** -0.5),
        'exp_w_gate': nrm(ks[22], (DEPTH, N_EXPERTS, D_MODEL, D_EXPERT), D_MODEL ** -0.5),
        'exp_w_up': nrm(ks[23], (DEPTH, N_EXPERTS, D_MODEL, D_EXPERT), D_MODEL ** -0.5),
        'exp_w_down': nrm(ks[24], (DEPTH, N_EXPERTS, D_EXPERT, D_MODEL), D_EXPERT ** -0.5),
        'moe_post_g': 1.0 + nrm(ks[25], (DEPTH, D_MODEL), 0.05),
    }

def reference(x, c, ctx, c_ctx, ada_w, ada_b, mix_pre_g, w_in, conv_w, conv_b, dt_bias, a_log,
              d_skip, ssd_norm_g, cm_dw_w, cm_dw_b, cm_ln_g, cm_ln_b, w_out, mix_post_g,
              moe_pre_g, router_w, exp_w_gate, exp_w_up, exp_w_down, moe_post_g):
    for i in range(DEPTH):
        last = i == DEPTH - 1
        sh1, sc1, g1, sh2, sc2, g2 = [m[:, None, :] for m in adaln(c, ada_w[i], ada_b[i])]
        csh1, csc1, cg1, csh2, csc2, cg2 = adaln(c_ctx, ada_w[i], ada_b[i])
        u_lat = rms_norm(x, mix_pre_g[i]) * (1.0 + sc1) + sh1
        u_ctx = rms_norm(ctx, mix_pre_g[i]) * (1.0 + csc1) + csh1
        m_lat, m_ctx = token_mixer(u_lat, u_ctx, w_in[i], conv_w[i], conv_b[i], dt_bias[i], a_log[i],
                                   d_skip[i], ssd_norm_g[i], cm_dw_w[i], cm_dw_b[i], cm_ln_g[i],
                                   cm_ln_b[i], w_out[i], not last)
        x = x + g1 * rms_norm(m_lat, mix_post_g[i])
        u = rms_norm(x, moe_pre_g[i]) * (1.0 + sc2) + sh2
        x = x + g2 * rms_norm(expert_choice_ffn(u, router_w[i], exp_w_gate[i], exp_w_up[i], exp_w_down[i]), moe_post_g[i])
        if not last:
            ctx = ctx + cg1 * rms_norm(m_ctx, mix_post_g[i])
            uc = rms_norm(ctx, moe_pre_g[i]) * (1.0 + csc2) + csh2
            ctx = ctx + cg2 * rms_norm(expert_choice_ffn(uc, router_w[i], exp_w_gate[i], exp_w_up[i], exp_w_down[i]), moe_post_g[i])
    return x


_drawn_inputs = setup_inputs


def setup_inputs(seed=0):
    import zlib

    import numpy as np

    out = dict(_drawn_inputs(seed))
    spreads = {}
    factors = {'cm_dw_b': 5.902, 'cm_ln_b': 4.421}
    for name, (base, spread) in spreads.items():
        noise = np.random.default_rng([zlib.crc32(name.encode()), seed]).standard_normal(out[name].shape)
        drawn = base * np.exp(spread * noise) if base else spread * noise
        out[name] = __import__('jax').numpy.asarray(drawn.astype(out[name].dtype))
    for name, factor in factors.items():
        out[name] = (out[name] * factor).astype(out[name].dtype)
    return out
```

```python
from contextlib import ExitStack

import numpy as np
import concourse.bass as bass
from concourse import mybir
from concourse.alu_op_type import AluOpType as ALU

ACT = mybir.ActivationFunctionType
AX_X = mybir.AxisListType.X
F32 = mybir.dt.float32
U32 = mybir.dt.uint32

P = 128
D = 1024
KD = D // P
CTX, SEQ = 256, 512
T = CTX + SEQ
NT = T // P
NCT = CTX // P
DEPTH = 2
H, HD, G, R, NS = 16, 64, 4, 4, 128
XBC = 2048
SSD_IN = XBC + 2 * H
Z_END = SSD_IN + D
IN_COLS = Z_END + 2 * D
K5, K31 = 5, 31
NE, FE = 16, 1408
FB = [(0, 512), (512, 512), (1024, 384)]
JF = FE // P
CL, CC = 2 * SEQ // NE, 2 * CTX // NE
EPS = 1e-6
WS = 5
SEG = [(0, CTX), (CTX, SEQ)]

COL = {"conv_w": 0, "conv_b": 80, "dw_b": 96, "ln_g": 104, "ln_b": 112, "pre_g": 120,
       "dw_w": 128, "moe_g": 376, "ada_b": 384, "norm_g": 432, "c": 440, "c_ctx": 448}


GATES = (2, 5)


def first_jobs(main):
    jobs = []
    for s in range(6):
        jobs.append(("ada", s))
        if s >= 1 and s - 1 not in GATES:
            jobs.append(("adaT", s - 1))
    jobs += [("norm", t) for t in range(NT)]
    for j in range(KD):
        jobs += [("g", j), ("a", j)]
    jobs += [("dt", 0)] + [("z", t) for t in main] + [("dtT", 0)]
    jobs += [("cum", 0)]
    for j in range(XBC // P):
        jobs.append(("xbc", j))
        if 2 <= j < 14:
            jobs.append(("xT", j - 2))
    jobs += [("mean", 0)]
    return jobs


def weight_slots(jobs):
    out = []
    for kind, i in jobs:
        if kind == "ada":
            out += [("ada", i, q) for q in range(4)]
        elif kind == "g" and i % 2 == 0:
            out += [("g", i // 2, 0), ("a", i // 2, 0)]
        elif kind == "dt":
            out += [("dt", 0, 0)] + [("z", 0, q) for q in range(4)]
        elif kind == "xbc" and i % 2 == 0:
            out.append(("xbc", i // 2, 0))
    return out


def build(nc, x, c, ctx, c_ctx, ada_w, ada_b, mix_pre_g, w_in, conv_w, conv_b, dt_bias, a_log,
          d_skip, ssd_norm_g, cm_dw_w, cm_dw_b, cm_ln_g, cm_ln_b, w_out, mix_post_g, moe_pre_g,
          router_w, exp_w_gate, exp_w_up, exp_w_down, moe_post_g, out):
    base = (nc.sbuf_base + 63) // 64 * 64
    end = nc.sbuf_usable_end

    def at(name, shape, off, dt=F32):
        n = int(np.prod(shape[1:])) * 4
        assert base + off + n <= end, (name, off + n, end - base)
        return nc.alloc_sbuf_tensor_at(name, list(shape), dt, offset=base + off)

    o = 0

    def perm(name, shape, dt=F32):
        nonlocal o
        t = at(name, shape, o, dt)
        o += (int(np.prod(shape[1:])) * 4 + 31) // 32 * 32
        return t

    masks = perm("masks", [P, 6, P])
    IDN, LE, GE, GT, LT, AVG = range(6)
    ones = perm("ones", [P, P])
    par = perm("par", [P, 512])
    cstat = perm("cstat", [P, KD, 33])
    modc = perm("modc", [P, 6, 2, KD])
    scl = perm("scl", [P, 2, 2, KD])
    ss = perm("ss", [P, 16])
    rstd = perm("rstd", [P, 16])
    eps = perm("eps", [P, 2])
    hdrow = perm("hdrow", [P, 5, 2 * H])
    W0 = o = (o + 63) // 64 * 64
    wslot = at("wslot", [P, WS, 2048], W0)
    o = W0 + WS * 8192
    U0 = o
    uT = at("uT", [P, KD, T], U0)
    Y = at("Y", [P, NT, D], U0)
    o += KD * T * 4
    X0 = o
    xtok = at("xtok", [P, NT, D], X0)
    o += NT * D * 4
    btok = at("btok", [P, NT, G * NS], o)
    o += NT * G * NS * 4
    B0 = o
    g5 = K5 // 2
    W5 = T + g5
    bct = at("bct", [P, 2 * G, W5], B0)
    yT = at("yT", [P, KD, T], B0)
    brow = at("brow", [33, 4, D], B0)
    o += 2 * G * W5 * 4
    g31 = K31 // 2
    W31 = T + g31
    PAD31 = T + 3 * g31
    vT = at("vT", [P, KD, PAD31], o)
    o += KD * PAD31 * 4
    TMP = (o + 63) // 64 * 64
    room = (end - base - TMP) // 32 * 32

    def tmp(first, specs):
        off, got = first, []
        for name, shape in specs:
            got.append(at(name, shape, TMP + off))
            off += (int(np.prod(shape[1:])) * 4 + 31) // 32 * 32
        assert off <= room, (off, room)
        return got, off

    (prow,), _ = tmp(0, [("prow", [P, 4, P])])
    (xt, junk, arow), _ = tmp(2048, [("xt", [P, NT, D]), ("junk", [P, D]), ("arow", [33, 2, D])])
    (sg, asb, cacc, pre5, acc5, szt, dtT), _ = tmp(0, [
        ("sg", [P, T]), ("asb", [P, T]), ("cacc", [P, 2, W31]), ("pre5", [P, 2, W5 + 2 * g5]),
        ("acc5", [P, 3, W5]), ("szt", [P, 2, D]), ("dtT", [2 * H, T])])
    DTN = NT * 2 * H
    (dts, ), dt_end = tmp(room - 9 * DTN * 4 - 64, [("dts", [P, 9, DTN])])
    DTV, DA, EC, ER, ET, WDT, D1, D2, D3 = range(9)
    (mean, sqb, rs), ln_end = tmp(31 * 1024, [("mean", [P, W31]), ("sqb", [P, 2, W31]), ("rs", [P, W31])])
    assert TMP + ln_end <= TMP + room - 9 * DTN * 4 - 64
    (dAm, E, GA, GB, SUL, hst, xw, otmp), ssd_end = tmp(0, [
        ("dAm", [P, 2, 2, 512]), ("E", [P, 2, 512]), ("GA", [P, 512]), ("GB", [P, 2, 512]),
        ("SUL", [P, 2, P]), ("hst", [P, 2, D]), ("xw", [P, D]), ("otmp", [P, D])])
    (szl,), _ = tmp(0, [("szl", [P, 2, D])])
    (gpb, xres, xn2, u2T, rw, sm, aff), _ = tmp(0, [
        ("gpb", [P, 2, D]), ("xres", [P, 2, D]), ("xn2", [P, NT, D]), ("u2T", [P, KD, P]),
        ("rw", [P, KD, NE]), ("sm", [P, 4, NT]), ("aff", [P, NT, NE])])
    SL = CL + CC
    (affT, topv, topi, gi, idxT, gateT, idg, ids, gcur, sel, hs, hh, ob, zro), _ = tmp(0, [
        ("affT", [48, SEQ]), ("topv", [48, CL]), ("topi", [48, CL]), ("gi", [NE, 2, SL]),
        ("idxT", [SL, NE]), ("gateT", [SL, NE]), ("idg", [SL, 1]), ("ids", [SL, 2]), ("gcur", [SL, 2]),
        ("sel", [SL, D]), ("hs", [SL, 512]), ("hh", [SL, FE]), ("ob", [SL, 2, D]), ("zro", [P, D])])
    RING = 24
    wr = at("wr", [P, RING, FE], W0)
    o = W0 + RING * FE * 4
    selT = at("selT", [P, 2, KD, SL], o)
    o += 2 * KD * SL * 4
    hT = at("hT", [P, 2, JF, SL], o)
    o += 2 * JF * SL * 4
    assert o <= TMP
    topi_u, idg_u, ids_u, idxT_u = (b[:].bitcast(U32) for b in (topi, idg, ids, idxT))
    (yt, xr, junk3, gpb2), _ = tmp(0, [("yt", [P, 2, D]), ("xr", [P, 2, D]), ("junk3", [P, D]), ("gpb2", [P, 2, D])])
    PS = nc.alloc_psum_tensor("PS", [P, 8, 512], F32)

    def dram(name, shape):
        return nc.dram_tensor(name, shape, F32, kind="Internal").ap()

    x1_d, xn_d, y_d, sz_d = (dram(n, (T, D)) for n in ("x1_d", "xn_d", "y_d", "sz_d"))
    xl_d = dram("xl_d", (T, D))
    gp_d = dram("gp_d", (2, 2, D))

    sems = {}

    def sem(name):
        if name not in sems:
            sems[name] = nc.alloc_semaphore(name)
        return sems[name]

    LAYERS = []
    for L in range(DEPTH):
        main = list(range(NT)) if L < DEPTH - 1 else list(range(NCT, NT))
        jobs = first_jobs(main)
        LAYERS.append((L, main, jobs, weight_slots(jobs)))

    def seg_banks(unit, s):
        return PS[:, 2 * unit + s, 0:SEG[s][1]]

    def unit2(unit, rows=P):
        return PS[0:rows, 2 * unit:2 * unit + 2, :].rearrange("p b n -> p (b n)")

    def c5(t):
        return P * t + (g5 if t >= NCT else 0)

    def c31(t):
        return P * t + (g31 if t >= NCT else 0)

    def segs(main):
        return (0, 1) if main[0] == 0 else (1,)

    def pairs(main):
        return [main[i:i + 2] for i in range(0, len(main), 2)]

    def src_rows(L, t):
        if L:
            return xl_d[t * P:(t + 1) * P, :]
        return ctx[0, t * P:(t + 1) * P, :] if t < NCT else x[0, (t - NCT) * P:(t - NCT + 1) * P, :]

    def slot_free(L, jobs, slots, n):
        kind, i, q = slots[n]
        if kind == "ada" and q < 3:
            return counter(L)("ada_used", 3 * i + q + 1)
        last = {"ada": i, "g": 2 * i + 1, "a": 2 * i + 1, "xbc": 2 * i + 1, "dt": 0,
                "z": max((j[1] for j in jobs if j[0] == "z"))}[kind]
        return counter(L)("pe_job", jobs.index((kind, last)) + 1)

    def scan(d):
        ctx_first = list(range(NCT)) if d == 0 else list(range(NCT))[::-1]
        lat = list(range(NCT, NT)) if d == 0 else list(range(NCT, NT))[::-1]
        return ctx_first + lat

    STEPS = [(d, n, scan(d)[n]) for n in range(NT) for d in range(2)]

    def reads(main):
        return [s for s in STEPS if s[1] and s[2] in main]

    UPDATES = [s for s in STEPS if s[1] < NT - 1]

    units = NT * G
    TOTAL = {}

    def count(total, names):
        TOTAL.update({name: total for name in names.split()})

    count(1, "par_T par_taken x_rms x_rstd pads_ready sp_abs sp_exp sp_one sp_ln a_exp da_ready wdt_ready var_taken "
             "affT_done affT_taken gi_ready giT_done")
    count(2, "mod_ready")
    count(NT, "x_sq xn_ready y_init yz_ready y_sq y_rms y_rstd yn_ready ynT_done yT_ready m_sq m_rms m_taken x1_ready "
              "x1_sq x1_rms x1_rstd xn2_ready u2T_done u2_ready logit_ready lmax_ready lexp_ready aff_ready "
              "f_sq f_rms xf_ready")
    count(KD, "v_made conf_done vc_ready sq_ready sq_used vn_ready v_ready")
    count(XBC // P, "taps_done conv_done")
    count(units, "dam_ready arg_ready e_ready s_ready m_ready yd_ready yd_taken")
    count(2 * units, "sul_ready")
    count(len(reads(range(NT))), "o_ready o_taken")
    count(len(UPDATES), "xw_ready st_ready h_ready")
    count(len(LAYERS[0][2]), "pe_job act_job")
    count(18, "ada_used")
    count(4, "gp_ready")
    count(NT // 2 * KD, "wo_used")
    count(16 * 16, "par_in")
    count(16 * NT, "x_in")
    count(8 * 16, "brow_in")
    count(4 * 16, "gp_out")
    count(2 * 16, "gpb_in gpb2_in")
    count(16, "rw_in")
    count(16 * NT // 2, "out_stored0 out_stored1 sz_out0 sz_out1 szl_in0 szl_in1 x1_out0 x1_out1 xn_out0 xn_out1 "
                        "xr_in0 xr_in1 xres_in0 xres_in1 yt_in0 yt_in1")
    count(NE, "selT_done selT_act selT_dve hT_done hT_act hT_dve dn_used gate_cur idg_ready")
    count(NE + 1, "dn_free")
    count(2 * NE, "settled")
    count(3 * NE, "hs_ready h_rows")
    count(2 * KD * NE, "gu_used")
    count(16 * NE, "sel_in")
    count(16 * NE + 32, "scattered")
    pieces = len(LAYERS[0][3]) + NT // 2 * KD
    for i in range(WS):
        count(16 * len(range(i, pieces, WS)), f"w_in{i}")

    def counter(L):
        return lambda name, v: (sem(name), L * TOTAL[name] + v)

    def seg_cols(main, gap):
        return (0, T + gap) if main[0] == 0 else (CTX + gap, SEQ)

    def store_out(sp, L, main, n):
        t = main[n]
        dst = xl_d[t * P:(t + 1) * P, :] if L < DEPTH - 1 else out[0, (t - NCT) * P:(t - NCT + 1) * P, :]
        sp.wait_ge(*counter(L)("xf_ready", n + 1))
        sp.dma_start(dst, xr[:, n % 2, :]).then_inc(sem(f"out_stored{n % 2}"), 16)

    def store_x1(pool, L, main, n):
        t = main[n]
        pool.wait_ge(*counter(L)("x1_ready", n + 1))
        pool.dma_start(x1_d[t * P:(t + 1) * P, :], xres[:, n % 2, :]).then_inc(sem(f"x1_out{n % 2}"), 16)
        pool.wait_ge(*counter(L)("xn2_ready", n + 1))
        pool.dma_start(xn_d[t * P:(t + 1) * P, :], xn2[:, n, :]).then_inc(sem(f"xn_out{n % 2}"), 16)

    with nc.Block() as block:
        @block.sync
        def _(sp):
            for L, main, jobs, slots in LAYERS:
                S, W = sem, counter(L)
                if L:
                    for i in range(2):
                        sp.wait_ge(*counter(L - 1)(f"out_stored{i}", 16 * NT // 2))

                def rows(ap, n0, what):
                    ti, r = divmod(COL[what] + n0, P)
                    sp.dma_start(prow[r:r + ap.shape[0], ti, :], ap).then_inc(S("par_in"), 16)

                rows(conv_w[L].rearrange("k (t p) -> (k t) p", p=P), 0, "conv_w")
                for src, what in ((conv_b, "conv_b"), (cm_dw_b, "dw_b"), (cm_ln_g, "ln_g"), (cm_ln_b, "ln_b"),
                                  (mix_pre_g, "pre_g"), (moe_pre_g, "moe_g"), (ssd_norm_g, "norm_g"), (ada_b, "ada_b")):
                    rows(src[L].rearrange("(t p) -> t p", p=P), 0, what)
                dw = cm_dw_w[L].rearrange("k (t p) -> (k t) p", p=P)
                rows(dw[0:P], 0, "dw_w")
                rows(dw[P:K31 * KD], P, "dw_w")
                rows(c[0].rearrange("(t p) -> t p", p=P), 0, "c")
                rows(c_ctx.rearrange("(t p) -> t p", p=P), 0, "c_ctx")
                for i, src in enumerate((dt_bias[L].rearrange("a h -> (a h)"), a_log[L].rearrange("a h -> (a h)"), d_skip[L])):
                    sp.dma_start(hdrow[:, i, 0:src.shape[0]], src.partition_broadcast(P)).then_inc(S("par_in"), 16)
                for t in range(NT):
                    sp.dma_start(xt[:, t, :], src_rows(L, t)).then_inc(S("x_in"), 16)
                for gi_, s in enumerate(GATES):
                    for r in (0, 32):
                        sp.dma_start(brow[r:r + 1, 2 * gi_, :], ada_b[L:L + 1, s * D:(s + 1) * D]).then_inc(S("brow_in"), 16)
                        sp.dma_start(brow[r:r + 1, 2 * gi_ + 1, :], (mix_post_g, moe_post_g)[gi_][L:L + 1, :]).then_inc(
                            S("brow_in"), 16)
                win = w_in[L].rearrange("(k p) n -> p k n", p=P)
                aw = ada_w[L].rearrange("(k p) n -> p k n", p=P)
                for n, (kind, i, q) in enumerate(slots):
                    if n >= WS:
                        sp.wait_ge(*slot_free(L, jobs, slots, n - WS))
                    dst = wslot[:, n % WS, :]
                    if kind == "ada":
                        dst = dst.rearrange("p (k n) -> p k n", k=2)
                        src = aw[:, 2 * q:2 * q + 2, i * D:(i + 1) * D]
                    elif kind == "dt":
                        dst = dst[:, 0:KD * 32].rearrange("p (k n) -> p k n", k=KD)
                        src = win[:, :, XBC:SSD_IN]
                    else:
                        dst = dst.rearrange("p (k n) -> p k n", k=KD)
                        first = {"g": Z_END + D + i * 256, "a": Z_END + i * 256, "z": SSD_IN + q * 256,
                                 "xbc": i * 256}[kind]
                        src = win[:, :, first:first + 256]
                    sp.dma_start(dst, src).then_inc(S(f"w_in{n % WS}"), 16)
                wo = w_out[L].rearrange("(q b p) n -> q p b n", b=2, p=P)
                for m in range(len(pairs(main)) * KD):
                    n = len(slots) + m
                    if m >= WS:
                        sp.wait_ge(*W("wo_used", m - WS + 1))
                    else:
                        sp.wait_ge(*slot_free(L, jobs, slots, n - WS))
                    sp.dma_start(wslot[:, n % WS, :].rearrange("p (b n) -> p b n", b=2), wo[m % KD]).then_inc(
                        S(f"w_in{n % WS}"), 16)
                sp.wait_ge(*W("wo_used", len(pairs(main)) * KD))
                base_in = 16 * NE * L

                def load_gate_up(e, reuse=True):
                    for k in range(KD):
                        for mi, w in ((0, exp_w_gate), (1, exp_w_up)):
                            if reuse:
                                sp.wait_ge(*W("gu_used", (e - 1) * 16 + 2 * k + mi + 1))
                            sp.dma_start(wr[:, 2 * k + mi, :], w[L, bass.ds(e, 1), k * P:(k + 1) * P, :].rearrange(
                                "o p n -> (o p) n")).then_inc(sem(f"gu_in{2 * k + mi}"), 16)

                def load_down(e, reuse=True):
                    src = exp_w_down[L, bass.ds(e, 1), :, :].rearrange("o (p j) n -> (o p) (j n)", j=JF)
                    if reuse:
                        sp.wait_ge(*W("dn_used", e))
                    for q in range(8):
                        sp.dma_start(wr[:, 16 + q, :], src[:, q * FE:(q + 1) * FE]).then_inc(sem(f"dn_in{q}"), 16)

                load_gate_up(0, False)
                load_gate_up(1)
                load_down(0, False)
                with sp.Fori(2, NE) as e:
                    load_gate_up(e)
                    load_down(e - 1)
                load_down(NE - 1)
                for n, t in enumerate(main):
                    if n == 0:
                        sp.wait_ge(*W("dn_free", NE + 1))
                        sp.wait_ge(*W("scattered", 32 + 16 * NE))
                        for st in range(2):
                            sp.dma_start(gpb2[:, st, :], gp_d[1, st, :].partition_broadcast(P)).then_inc(S("gpb2_in"), 16)
                    if n >= 2:
                        sp.wait_ge(*W(f"out_stored{n % 2}", 16 * (n // 2)))
                    sp.dma_start(yt[:, n % 2, :], y_d[t * P:(t + 1) * P, :]).then_inc(S(f"yt_in{n % 2}"), 16)
                    sp.dma_start(xr[:, n % 2, :], x1_d[t * P:(t + 1) * P, :]).then_inc(S(f"xr_in{n % 2}"), 16)
                    if n:
                        store_out(sp, L, main, n - 1)
                store_out(sp, L, main, len(main) - 1)
            for i in range(2):
                sp.wait_ge(*counter(DEPTH - 1)(f"out_stored{i}", 16 * len(main) // 2))

        @block.tensor
        def _(pe):
            def tr(dst, src, n):
                return pe.transpose(dst, src, masks[0:n, IDN, 0:n])

            pe.wait_ge(sem("consts"), 1)
            for L, main, jobs, slots in LAYERS:
                S, W = sem, counter(L)
                where = {sl: n for n, sl in enumerate(slots)}
                slot_n = CL + (CC if main[0] == 0 else 0)

                def weights(n):
                    pe.wait_ge(*W(f"w_in{n % WS}", 16 * (n // WS + 1)))
                    return wslot[:, n % WS, :]

                pe.wait_ge(*W("par_in", 16 * 16))
                for i, n in enumerate((P, P, P, 72)):
                    m = tr(PS[:, 0, i * P:i * P + n], prow[0:n, i, :], n)
                m.then_inc(S("par_T"), 1)
                pe.wait_ge(*W("par_taken", 1))
                pe.wait_ge(sem("cstat_ready"), 1)
                for n, (kind, i) in enumerate(jobs):
                    u = n % 4
                    if n >= 4:
                        pe.wait_ge(*W("act_job", n - 3))
                    if kind == "ada":
                        for q in range(4):
                            wv = weights(where["ada", i, q])
                            for kk in range(2):
                                for h in range(2):
                                    m = pe.matmul(PS[0:33, 2 * u + h, :], cstat[:, 2 * q + kk, :],
                                                  wv[:, kk * D + h * 512:kk * D + (h + 1) * 512],
                                                  start=q + kk == 0, stop=q + kk == 4)
                            if q < 3:
                                m.then_inc(S("ada_used"), 1)
                    elif kind == "adaT":
                        pe.wait_ge(*W("act_job", jobs.index(("ada", i)) + 1))
                        for k in range(KD):
                            m = tr(PS[:, 2 * u, k * 33:(k + 1) * 33], arow[:, i % 2, k * P:(k + 1) * P], 33)
                    elif kind == "norm":
                        pe.wait_ge(*W("xn_ready", i + 1))
                        for k in range(KD):
                            m = tr(PS[:, 2 * u + k // 4, (k % 4) * P:(k % 4 + 1) * P], xt[:, i, k * P:(k + 1) * P], P)
                    elif kind in ("g", "a", "xbc"):
                        if i == 0 and kind == "g":
                            pe.wait_ge(*W("act_job", jobs.index(("norm", NT - 1)) + 1))
                        wv = weights(where[kind, i // 2, 0]).rearrange("p (k n) -> p k n", k=KD)
                        for s in (0, 1) if kind == "xbc" else segs(main):
                            for k in range(KD):
                                m = pe.matmul(seg_banks(u, s), wv[:, k, (i % 2) * P:(i % 2 + 1) * P],
                                              uT[:, k, SEG[s][0]:SEG[s][0] + SEG[s][1]], start=k == 0, stop=k == KD - 1)
                    elif kind == "dt":
                        wv = weights(where["dt", 0, 0])[:, 0:KD * 32].rearrange("p (k n) -> p k n", k=KD)
                        for s in (0, 1):
                            for k in range(KD):
                                m = pe.matmul(PS[0:32, 2 * u + s, 0:SEG[s][1]], wv[:, k, :],
                                              uT[:, k, SEG[s][0]:SEG[s][0] + SEG[s][1]], start=k == 0, stop=k == KD - 1)
                    elif kind == "z":
                        for q in range(4):
                            wv = weights(where["z", 0, q]).rearrange("p (k n) -> p k n", k=KD)
                            for k in range(KD):
                                m = pe.matmul(PS[:, 2 * u + q // 2, (q % 2) * 256:(q % 2 + 1) * 256],
                                              uT[:, k, i * P:(i + 1) * P], wv[:, k, :], start=k == 0, stop=k == KD - 1)
                    elif kind == "dtT":
                        pe.wait_ge(*W("act_job", jobs.index(("dt", 0)) + 1))
                        for t in range(NT):
                            m = tr(PS[:, 2 * u, t * 32:(t + 1) * 32], dtT[:, t * P:(t + 1) * P], 32)
                    elif kind == "cum":
                        pe.wait_ge(*W("da_ready", 1))
                        dav = dts[:, DA, :].rearrange("p (t d h) -> p t d h", d=2, h=H)
                        for b, pair in enumerate(((LE, GE), (GT, LT))):
                            for d, mk in enumerate(pair):
                                pe.matmul(PS[:, 2 * u, b * 256 + d * 96:b * 256 + d * 96 + 96].rearrange(
                                    "p (t h) -> p t h", h=H), masks[:, mk, :], dav[:, :, d, :], start=True, stop=True)
                        m = pe.matmul(PS[:, 2 * u + 1, 0:DTN], ones[:], dts[:, DA, :], start=True, stop=True)
                    elif kind == "xT":
                        pe.wait_ge(*W("conv_done", i + 1))
                        for t in range(NT):
                            src = acc5[:, i % 3, c5(t):c5(t) + P] if i < 8 else bct[:, i - 8, c5(t):c5(t) + P]
                            m = tr(PS[:, 2 * u + t // 4, (t % 4) * P:(t % 4 + 1) * P], src, P)
                    elif kind == "mean":
                        pe.wait_ge(*W("conf_done", KD))
                        for s in segs(main):
                            f = c31(0 if s == 0 else NCT)
                            for k in range(KD):
                                m = pe.matmul(seg_banks(u, s), masks[:, AVG, :], vT[:, k, f:f + SEG[s][1]],
                                              start=k == 0, stop=k == KD - 1)
                    m.then_inc(S("pe_job"), 1)
                pe.wait_ge(*W("act_job", len(jobs)))
                for k in range(KD):
                    pe.wait_ge(*W("sq_ready", k + 1))
                    for s in segs(main):
                        f = c31(0 if s == 0 else NCT)
                        m = pe.matmul(seg_banks(0, s), masks[:, AVG, :], sqb[:, k % 2, f:f + SEG[s][1]],
                                      start=k == 0, stop=k == KD - 1)
                    m.then_inc(S("sq_used"), 1)
                pe.wait_ge(*W("var_taken", 1))
                pe.wait_ge(*W("conv_done", 2 * KD))
                todo = [(ch, g) for ch in main for g in range(G)]

                def outputs(q):
                    ch, g = todo[q]
                    pe.wait_ge(*W("m_ready", q + 1))
                    if q >= 2:
                        pe.wait_ge(*W("yd_taken", q - 1))
                    for r in range(R):
                        pr = g * 256 + (r // 2) * P
                        m = pe.matmul(PS[:, 3 + 2 * (q % 2), r * P:(r + 1) * P], GB[:, q % 2, r * P:(r + 1) * P],
                                      xtok[:, ch, pr:pr + P], start=True, stop=True)
                    m.then_inc(S("yd_ready"), 1)

                for q, (ch, g) in enumerate(todo):
                    pe.wait_ge(*W("dam_ready", q + 1))
                    if q >= 2:
                        pe.wait_ge(*W("e_ready", q - 1))
                    pe.matmul(PS[:, q % 2, :], masks[:, GT, :], dAm[:, q % 2, 0, :], start=True, stop=False)
                    pe.matmul(PS[:, q % 2, :], masks[:, LT, :], dAm[:, q % 2, 1, :], start=False, stop=True).then_inc(
                        S("arg_ready"), 1)
                    if q >= 2:
                        pe.wait_ge(*W("sul_ready", 2 * q - 2))
                    pe.matmul(PS[:, 2 + 2 * (q % 2), 0:P], bct[:, g, c5(ch):c5(ch) + P], bct[:, G + g, c5(ch):c5(ch) + P],
                              start=True, stop=True).then_inc(S("s_ready"), 1)
                    if q:
                        outputs(q - 1)
                outputs(len(todo) - 1)
                q = len(todo)
                pe.wait_ge(*W("yd_taken", q))
                nread = nupd = 0
                for d, n, ch in STEPS:
                    if (d, n, ch) in reads(main):
                        pe.wait_ge(*W("h_ready", nupd))
                        if nread:
                            pe.wait_ge(*W("o_taken", nread))
                        for g in range(G):
                            m = pe.matmul(PS[:, 4 + g // 2, (g % 2) * 256:(g % 2 + 1) * 256],
                                          bct[:, G + g, c5(ch):c5(ch) + P], hst[:, d, g * 256:(g + 1) * 256],
                                          start=True, stop=True)
                        m.then_inc(S("o_ready"), 1)
                        nread += 1
                    if (d, n, ch) in UPDATES:
                        pe.wait_ge(*W("xw_ready", nupd + 1))
                        if nupd:
                            pe.wait_ge(*W("h_ready", nupd))
                        for g in range(G):
                            m = pe.matmul(PS[:, 6 + g // 2, (g % 2) * 256:(g % 2 + 1) * 256],
                                          btok[:, ch, g * NS:(g + 1) * NS], xw[:, g * 256:(g + 1) * 256],
                                          start=True, stop=True)
                        m.then_inc(S("st_ready"), 1)
                        nupd += 1
                pe.wait_ge(*W("o_taken", nread))
                pe.wait_ge(*W("h_ready", nupd))
                pe.wait_ge(*W("yd_taken", q))
                for n, t in enumerate(main):
                    pe.wait_ge(*W("yn_ready", n + 1))
                    if n >= 4:
                        pe.wait_ge(*W("yT_ready", n - 3))
                    for k in range(KD):
                        m = tr(PS[:, 2 * (n % 4) + k // 4, (k % 4) * P:(k % 4 + 1) * P], Y[:, t, k * P:(k + 1) * P], P)
                    m.then_inc(S("ynT_done"), 1)
                pe.wait_ge(*W("yT_ready", len(main)))
                pe.wait_ge(*W("v_ready", KD))
                n = len(slots)
                for pi, pair in enumerate(pairs(main)):
                    if pi >= 2:
                        pe.wait_ge(*W("m_taken", 2 * (pi - 1)))
                    for q in range(KD):
                        wv = weights(n)
                        for b in range(2):
                            k = 2 * q + b
                            for ti, t in enumerate(pair):
                                lhs = yT[:, k, t * P:(t + 1) * P] if k < KD else vT[:, k - KD, c31(t):c31(t) + P]
                                for h in range(2):
                                    m = pe.matmul(PS[:, 4 * (pi % 2) + 2 * ti + h, :], lhs,
                                                  wv[:, b * D + h * 512:b * D + (h + 1) * 512],
                                                  start=k == 0, stop=k == 2 * KD - 1)
                        m.then_inc(S("wo_used"), 1)
                        n += 1
                for n, t in enumerate(main):
                    pe.wait_ge(*W("xn2_ready", n + 1))
                    if n == 0:
                        pe.wait_ge(*W("m_taken", len(main)))
                        pe.wait_ge(*W("rw_in", 16))
                    for k in range(KD):
                        m = tr(PS[:, k // 4, (k % 4) * P:(k % 4 + 1) * P], xn2[:, n, k * P:(k + 1) * P], P)
                    m.then_inc(S("u2T_done"), 1)
                    pe.wait_ge(*W("u2_ready", n + 1))
                    for k in range(KD):
                        m = pe.matmul(PS[:, 2 + n, 0:NE], u2T[:, k, :], rw[:, k, :],
                                      start=k == 0, stop=k == KD - 1)
                    m.then_inc(S("logit_ready"), 1)
                pe.wait_ge(*W("aff_ready", len(main)))
                for n, t in enumerate(main):
                    dst = PS[0:NE, 4, t * P:(t + 1) * P] if t < NCT else PS[0:NE, 5, (t - NCT) * P:(t - NCT + 1) * P]
                    m = tr(dst, aff[:, n, :], P)
                m.then_inc(S("affT_done"), 1)
                pe.wait_ge(*W("gi_ready", 1))
                for b in range(2):
                    m = tr(PS[0:slot_n, 6, b * NE:(b + 1) * NE], gi[:, b, 0:slot_n], NE)
                m.then_inc(S("giT_done"), 1)

                base_in = 16 * NE * L

                def sel_transposes():
                    for k in range(KD):
                        m = tr(PS[:, k // 4, (k % 4) * P:(k % 4) * P + slot_n], sel[0:slot_n, k * P:(k + 1) * P], slot_n)
                    m.then_inc(S("selT_done"), 1)

                def gate_up(par, e):
                    pe.wait_ge(*W("selT_act", e + 1))
                    pe.wait_ge(*W("selT_dve", e + 1))
                    for k in range(KD):
                        for mi in range(2):
                            pe.wait_ge(sem(f"gu_in{2 * k + mi}"), base_in + e * 16 + 16)
                            for b, (f, w) in enumerate(FB):
                                m = pe.matmul(PS[0:slot_n, 3 * mi + b, 0:w], selT[:, par, k, 0:slot_n],
                                              wr[:, 2 * k + mi, f:f + w], start=k == 0, stop=k == KD - 1)
                            m.then_inc(S("gu_used"), 1)

                def down(par, e, lo, hi):
                    flat = wr[:, 16:24, :].rearrange("p q n -> p (q n)")
                    for j in range(lo, hi):
                        first = (j * D - 1) // FE + 1 if j else 0
                        for q in range(first, ((j + 1) * D - 1) // FE + 1):
                            pe.wait_ge(sem(f"dn_in{q}"), base_in + e * 16 + 16)
                        for h in range(2):
                            m = pe.matmul(PS[0:slot_n, 6 + h, :], hT[:, par, j, 0:slot_n],
                                          flat[:, j * D + h * 512:j * D + (h + 1) * 512], start=j == 0, stop=j == JF - 1)
                    if hi == JF:
                        m.then_inc(S("dn_used"), 1)

                def h_transposes():
                    hv = hh[0:slot_n, :].rearrange("s (p j) -> s p j", j=JF)
                    for j in range(JF):
                        m = tr(PS[:, 2 + j // 4, (j % 4) * P:(j % 4) * P + slot_n], hv[:, :, j], slot_n)
                    m.then_inc(S("hT_done"), 1)

                def expert(par, e, first=False, last=False):
                    if not first:
                        pe.wait_ge(*W("hT_act", e))
                        pe.wait_ge(*W("hT_dve", e))
                    gate_up(par, e)
                    if not first:
                        pe.wait_ge(*W("dn_free", e))
                        down(1 - par, e - 1, 0, 4)
                    pe.wait_ge(*W("h_rows", 3 * e + 3))
                    if not last:
                        pe.wait_ge(*W("sel_in", 16 * e + 32))
                    if not first:
                        down(1 - par, e - 1, 4, 5)
                    if not last:
                        sel_transposes()
                    h_transposes()
                    if not first:
                        down(1 - par, e - 1, 5, JF)

                pe.wait_ge(*W("affT_taken", 1))
                pe.wait_ge(*W("sel_in", 16))
                sel_transposes()
                expert(0, 0, first=True)
                with pe.Fori(1, NE - 3, 2) as e:
                    expert(1, e)
                    expert(0, e + 1)
                for e in range(NE - 3, NE):
                    expert(e % 2, e, last=e == NE - 1)
                pe.wait_ge(*W("hT_act", NE))
                pe.wait_ge(*W("hT_dve", NE))
                pe.wait_ge(*W("dn_free", NE))
                down(1, NE - 1, 0, JF)

        @block.scalar
        def _(act):
            for L, main, jobs, slots in LAYERS:
                S, W = sem, counter(L)
                slot_n = CL + (CC if main[0] == 0 else 0)
                v0, vw = seg_cols(main, g31)

                def rms(src, junk_, col, stage, n):
                    act.activation(junk_, src, ACT.Square, accum_out=ss[:, col:col + 1]).then_inc(S(f"{stage}_sq"), 1)
                    act.wait_ge(*W(f"{stage}_sq", n + 1))
                    act.activation(ss[:, col + 1:col + 2], ss[:, col:col + 1], ACT.Sqrt, bias=eps[:, 0:1],
                                   scale=1.0 / D).then_inc(S(f"{stage}_rms"), 1)

                def silu5(j):
                    act.wait_ge(*W("taps_done", j + 1))
                    dst = acc5[:, j % 3, :] if j < 8 else bct[:, j - 8, :]
                    act.activation(dst, acc5[:, j % 3, :], ACT.Silu,
                                   bias=par[:, COL["conv_b"] + j:COL["conv_b"] + j + 1]).then_inc(S("conv_done"), 1)

                act.wait_ge(*W("par_T", 1))
                act.copy(par[:, 0:P * 3 + 72], PS[:, 0, 0:P * 3 + 72]).then_inc(S("par_taken"), 1)
                act.wait_ge(*W("par_taken", 1))
                if L == 0:
                    act.wait_ge(sem("cstat_zero"), 1)
                    act.activation(cstat[:, :, 0:33:32].rearrange("p k s -> p s k"),
                                   par[:, COL["c"]:COL["c"] + 16].rearrange("p (s k) -> p s k", s=2),
                                   ACT.Silu).then_inc(sem("cstat_ready"), 1)
                    act.wait_ge(sem("eps_set"), 1)
                act.wait_ge(*W("x_in", 16 * NT))
                for t in range(NT):
                    if t:
                        act.wait_ge(*W("x_sq", t))
                    act.activation(junk[:], xt[:, t, :], ACT.Square, accum_out=ss[:, t:t + 1]).then_inc(S("x_sq"), 1)
                act.wait_ge(*W("x_sq", NT))
                act.activation(ss[:, 8:8 + NT], ss[:, 0:NT], ACT.Sqrt, bias=eps[:, 0:1], scale=1.0 / D).then_inc(
                    S("x_rms"), 1)
                act.wait_ge(*W("x_rstd", 1))
                for t in range(NT):
                    act.mul(xt[:, t, :], xt[:, t, :], rstd[:, t:t + 1]).then_inc(S("xn_ready"), 1)
                for n, (kind, i) in enumerate(jobs):
                    u = n % 4
                    if kind == "norm" and i == 0:
                        act.wait_ge(*W("mod_ready", 1))
                    if kind == "g" and i:
                        act.wait_ge(*W("v_made", i))
                    if kind == "ada" and i >= 2:
                        if i - 2 in GATES:
                            act.wait_ge(*W("gp_ready", 2))
                        else:
                            act.wait_ge(*W("pe_job", jobs.index(("adaT", i - 2)) + 1))
                    if kind == "xbc" and i >= 2:
                        act.wait_ge(*W("taps_done", i - 1))
                    if kind == "xbc" and i == 0:
                        act.wait_ge(*W("pads_ready", 1))
                    if kind == "z" and i == main[0]:
                        act.wait_ge(*W("gp_out", 4 * 16))
                    if kind == "mean":
                        for b in range(2):
                            act.wait_ge(*W(f"sz_out{b}", 16 * len(main) // 2))
                    act.wait_ge(*W("pe_job", n + 1))
                    if kind == "ada":
                        ins = act.copy(arow[:, i % 2, :], unit2(u, 33))
                    elif kind == "adaT":
                        ins = act.copy(modc[:, i, :, :], PS[:, 2 * u, 0:KD * 33].rearrange(
                            "p (k s) -> p s k", s=33)[:, 0:33:32, :])
                    elif kind == "norm":
                        st = 0 if i >= NCT else 1
                        for k in range(KD):
                            ins = act.activation(uT[:, k, i * P:(i + 1) * P],
                                                 PS[:, 2 * u + k // 4, (k % 4) * P:(k % 4 + 1) * P],
                                                 ACT.Identity, bias=modc[:, 0, st, k:k + 1], scale=scl[:, 0, st, k:k + 1])
                    elif kind in ("g", "a"):
                        for s in segs(main):
                            dst = (sg if kind == "g" else asb)[:, SEG[s][0]:SEG[s][0] + SEG[s][1]]
                            ins = act.activation(dst, seg_banks(u, s), ACT.Sigmoid if kind == "g" else ACT.Copy)
                    elif kind == "dt":
                        for s in (0, 1):
                            ins = act.copy(dtT[:, SEG[s][0]:SEG[s][0] + SEG[s][1]], PS[0:32, 2 * u + s, 0:SEG[s][1]])
                    elif kind == "z":
                        zi = main.index(i)
                        if zi >= 2:
                            act.wait_ge(*W(f"sz_out{zi % 2}", 16 * (zi // 2)))
                        ins = act.activation(szt[:, zi % 2, :], unit2(u), ACT.Silu)
                    elif kind == "dtT":
                        ins = act.copy(dts[:, D1, :], PS[:, 2 * u, 0:DTN])
                    elif kind == "cum":
                        for b, dst in ((0, EC), (1, ER)):
                            act.activation(dts[:, dst, :], PS[:, 2 * u, b * 256:b * 256 + DTN], ACT.Exp)
                        ins = act.activation(dts[:, ET, :], PS[:, 2 * u + 1, 0:DTN], ACT.Exp)
                    elif kind == "xbc":
                        for s in (0, 1):
                            f = g5 + c5(0 if s == 0 else NCT)
                            ins = act.copy(pre5[:, i % 2, f:f + SEG[s][1]], seg_banks(u, s))
                    elif kind == "xT":
                        dst = xtok[:, :, i * P:(i + 1) * P] if i < 8 else btok[:, :, (i - 8) * P:(i - 7) * P]
                        act.copy(dst[:, 0:4, :], PS[:, 2 * u, :].rearrange("p (t n) -> p t n", n=P))
                        ins = act.copy(dst[:, 4:6, :], PS[:, 2 * u + 1, 0:256].rearrange("p (t n) -> p t n", n=P))
                    elif kind == "mean":
                        for s in segs(main):
                            f = c31(0 if s == 0 else NCT)
                            ins = act.copy(mean[:, f:f + SEG[s][1]], seg_banks(u, s))
                    ins.then_inc(S("act_job"), 1)
                    if kind == "z":
                        act.wait_ge(*W("act_job", n + 1))
                        act.dma_start(sz_d[i * P:(i + 1) * P, :], szt[:, zi % 2, :]).then_inc(S(f"sz_out{zi % 2}"), 16)
                    if kind == "dtT":
                        act.wait_ge(*W("sp_abs", 1))
                        act.activation(dts[:, D3, :], dts[:, D2, :], ACT.Exp, scale=-1.0).then_inc(S("sp_exp"), 1)
                        act.wait_ge(*W("sp_one", 1))
                        act.activation(dts[:, EC, :], dts[:, D2, :], ACT.Ln).then_inc(S("sp_ln"), 1)
                        act.activation(hdrow[:, 3, :], hdrow[:, 1, :], ACT.Exp).then_inc(S("a_exp"), 1)
                    if kind == "xbc" and i >= 1:
                        silu5(i - 1)
                        if i == 15:
                            silu5(15)
                for k in range(KD):
                    act.wait_ge(*W("vc_ready", k + 1))
                    if k >= 2:
                        act.wait_ge(*W("sq_used", k - 1))
                    act.activation(sqb[:, k % 2, v0:v0 + vw], vT[:, k, v0:v0 + vw], ACT.Square).then_inc(S("sq_ready"), 1)
                act.wait_ge(*W("sq_used", KD))
                for s in segs(main):
                    f = c31(0 if s == 0 else NCT)
                    ins = act.activation(rs[:, f:f + SEG[s][1]], seg_banks(0, s), ACT.Sqrt, bias=eps[:, 0:1])
                ins.then_inc(S("var_taken"), 1)
                for k in range(KD):
                    act.wait_ge(*W("vn_ready", k + 1))
                    act.activation(vT[:, k, v0:v0 + vw], vT[:, k, v0:v0 + vw], ACT.Silu,
                                   bias=par[:, COL["ln_b"] + k:COL["ln_b"] + k + 1],
                                   scale=par[:, COL["ln_g"] + k:COL["ln_g"] + k + 1]).then_inc(S("v_ready"), 1)
                for q in range(len(main) * G):
                    act.wait_ge(*W("arg_ready", q + 1))
                    if q >= 2:
                        act.wait_ge(*W("m_ready", q - 1))
                    act.activation(E[:, q % 2, :], PS[:, q % 2, :], ACT.Exp).then_inc(S("e_ready"), 1)

                def take_yT(n):
                    act.wait_ge(*W("ynT_done", n + 1))
                    for k in range(KD):
                        ins = act.mul(yT[:, k, main[n] * P:(main[n] + 1) * P],
                                      PS[:, 2 * (n % 4) + k // 4, (k % 4) * P:(k % 4 + 1) * P],
                                      par[:, COL["norm_g"] + k:COL["norm_g"] + k + 1])
                    ins.then_inc(S("yT_ready"), 1)

                for n, t in enumerate(main):
                    act.wait_ge(*W("yz_ready", n + 1))
                    if n:
                        act.wait_ge(*W("y_rstd", n))
                    rms(Y[:, t, :], otmp[:], 0, "y", n)
                    act.wait_ge(*W("y_rstd", n + 1))
                    act.mul(Y[:, t, :], Y[:, t, :], rstd[:, n:n + 1]).then_inc(S("yn_ready"), 1)
                    if n:
                        take_yT(n - 1)
                take_yT(len(main) - 1)

                def take_u2(n):
                    act.wait_ge(*W("u2T_done", n + 1))
                    if n:
                        act.wait_ge(*W("logit_ready", n))
                    st = 0 if main[n] >= NCT else 1
                    for k in range(KD):
                        ins = act.activation(u2T[:, k, :], PS[:, k // 4, (k % 4) * P:(k % 4 + 1) * P], ACT.Identity,
                                             bias=modc[:, 3, st, k:k + 1], scale=scl[:, 1, st, k:k + 1])
                    ins.then_inc(S("u2_ready"), 1)

                for n, t in enumerate(main):
                    act.wait_ge(*W("wo_used", (n // 2 + 1) * KD))
                    b = 4 * ((n // 2) % 2) + 2 * (n % 2)
                    if n:
                        act.wait_ge(*W("x1_rstd", n))
                    rms(PS[:, b:b + 2, :].rearrange("p b n -> p (b n)"), xn2[:, n, :], 0, "m", n)
                    act.wait_ge(*W("x1_ready", n + 1))
                    rms(xres[:, n % 2, :], xn2[:, n, :], 2, "x1", n)
                    act.wait_ge(*W("x1_rstd", n + 1))
                    act.mul(xn2[:, n, :], xres[:, n % 2, :], rstd[:, 1:2]).then_inc(S("xn2_ready"), 1)
                for n in range(len(main)):
                    take_u2(n)
                for n, t in enumerate(main):
                    act.wait_ge(*W("lmax_ready", n + 1))
                    act.activation(aff[:, n, :], PS[:, 2 + n, 0:NE], ACT.Exp, bias=sm[:, 0, n:n + 1],
                                   accum_out=sm[:, 1, n:n + 1]).then_inc(S("lexp_ready"), 1)

                def take_sel(par, n):
                    act.wait_ge(*W("selT_done", n))
                    for st, (lo, hi) in enumerate(((0, CL), (CL, slot_n))):
                        for k in range(KD // 2) if hi > lo else ():
                            ins = act.activation(selT[:, par, k, lo:hi], PS[:, k // 4, (k % 4) * P + lo:(k % 4) * P + hi],
                                                 ACT.Identity, bias=modc[:, 3, st, k:k + 1], scale=scl[:, 1, st, k:k + 1])
                    ins.then_inc(S("selT_act"), 1)

                def down_out(par, e):
                    act.wait_ge(*W("dn_used", e + 1))
                    act.wait_ge(*W("gate_cur", e + 1))
                    act.wait_ge(*W("scattered", 16 * e + 16))
                    act.mul(ob[0:slot_n, par, :], PS[0:slot_n, 6:8, :].rearrange("p b n -> p (b n)"),
                            gcur[0:slot_n, par:par + 1]).then_inc(S("dn_free"), 1)

                def expert(par, e, first=False, last=False):
                    for b, (f, w) in enumerate(FB):
                        if b == 0:
                            act.wait_ge(*W("gu_used", e * 16 + 16))
                        if b or not first:
                            act.wait_ge(*W("h_rows", 3 * e + b))
                        act.activation(hs[0:slot_n, 0:w], PS[0:slot_n, b, 0:w], ACT.Silu).then_inc(S("hs_ready"), 1)
                    if not last:
                        take_sel(1 - par, e + 2)
                    act.wait_ge(*W("hT_done", e + 1))
                    act.copy(hT[:, par, 0:4, 0:slot_n], PS[:, 2, :].rearrange("p (j s) -> p j s", s=P)[:, :, 0:slot_n]).then_inc(
                        S("hT_act"), 1)
                    if not first:
                        down_out(1 - par, e - 1)

                act.wait_ge(*W("affT_taken", 1))
                take_sel(0, 1)
                expert(0, 0, first=True)
                with act.Fori(1, NE - 3, 2) as e:
                    expert(1, e)
                    expert(0, e + 1)
                for e in range(NE - 3, NE):
                    expert(e % 2, e, last=e == NE - 1)
                down_out(1, NE - 1)
                for n, t in enumerate(main):
                    act.wait_ge(*W(f"yt_in{n % 2}", 16 * (n // 2 + 1)))
                    if n:
                        act.wait_ge(*W("xf_ready", n))
                    rms(yt[:, n % 2, :], junk3[:], 4, "f", n)

        @block.vector
        def _(dve):
            chained = [0]

            def chain(ins):
                chained[0] += 1
                ins.then_inc(sem("dve_chain"), 1)
                dve.wait_ge(sem("dve_chain"), chained[0])

            def seen(ins, at_name, n):
                ins.then_inc(sem(at_name), 1)
                dve.wait_ge(*counter(L)(at_name, n))

            dve.memset(eps[:, 0:1], EPS).then_inc(sem("eps_set"), 1)
            dve.memset(cstat[:], 0.0).then_inc(sem("cstat_zero"), 1)
            for L, main, jobs, slots in LAYERS:
                S, W = sem, counter(L)
                slot_n = CL + (CC if main[0] == 0 else 0)
                v0, vw = seg_cols(main, g31)
                TT, TS, STT = dve.tensor_tensor, dve.tensor_scalar, dve.scalar_tensor_tensor

                def inv(dst, src):
                    return dve.reciprocal(dst, src)

                dve.wait_ge(*W("x_rms", 1))
                inv(rstd[:, 0:NT], ss[:, 8:8 + NT]).then_inc(S("x_rstd"), 1)
                first_col = par[:, COL["dw_w"]:COL["dw_w"] + K31 * KD]
                for j in range(KD):
                    dve.wait_ge(*W("v_made", j + 1))
                    tap = lambda k: first_col[:, k * KD + j:k * KD + j + 1]
                    a = cacc[:, j % 2, v0:v0 + vw]
                    chain(TS(a, vT[:, j, v0 + 1:v0 + 1 + vw], tap(1), par[:, COL["dw_b"] + j:COL["dw_b"] + j + 1],
                             ALU.mult, ALU.add))
                    for k in range(2, K31):
                        chain(STT(a, vT[:, j, v0 + k:v0 + k + vw], tap(k), a, ALU.mult, ALU.add))
                    STT(vT[:, j, v0:v0 + vw], vT[:, j, v0:v0 + vw], tap(0), a, ALU.mult, ALU.add).then_inc(S("conf_done"), 1)
                dtr = lambda i: dts[:, i, :].rearrange("p (t h) -> p t h", t=NT)
                over_t = lambda i: hdrow[:, i, :].unsqueeze(1).to_broadcast([P, NT, 2 * H])
                dve.wait_ge(*W("act_job", jobs.index(("dtT", 0)) + 1))
                chain(TT(dtr(D1), dtr(D1), over_t(0), ALU.add))
                STT(dts[:, D2, :], dts[:, D1, :], -1.0, dts[:, D1, :], ALU.mult, ALU.max).then_inc(S("sp_abs"), 1)
                chain(TS(dts[:, D1, :], dts[:, D1, :], 0.0, None, ALU.max))
                dve.wait_ge(*W("sp_exp", 1))
                TS(dts[:, D2, :], dts[:, D3, :], 1.0, None, ALU.add).then_inc(S("sp_one"), 1)
                dve.wait_ge(*W("sp_one", 1))
                chain(TS(dts[:, WDT, :], dts[:, D2, :], 1.0, 1e-30, ALU.subtract, ALU.max))
                chain(inv(dts[:, WDT, :], dts[:, WDT, :]))
                chain(STT(dts[:, DTV, :], dts[:, D2, :], 1.0, dts[:, D3, :], ALU.is_le, ALU.mult))
                chain(TT(dts[:, DTV, :], dts[:, DTV, :], dts[:, D1, :], ALU.add))
                chain(TT(dts[:, WDT, :], dts[:, WDT, :], dts[:, D3, :], ALU.mult))
                dve.wait_ge(*W("sp_ln", 1))
                chain(TT(dts[:, WDT, :], dts[:, WDT, :], dts[:, EC, :], ALU.mult))
                chain(TT(dts[:, DTV, :], dts[:, DTV, :], dts[:, WDT, :], ALU.add))
                dve.wait_ge(*W("a_exp", 1))
                chain(TT(dtr(DA), dtr(DTV), over_t(3), ALU.mult))
                TS(dts[:, DA, :], dts[:, DA, :], -1.0, None, ALU.mult).then_inc(S("da_ready"), 1)
                for j in range(2 * KD):
                    dve.wait_ge(*W("act_job", jobs.index(("xbc", j)) + 1))
                    if j >= 3:
                        if j - 3 < 8:
                            dve.wait_ge(*W("pe_job", jobs.index(("xT", j - 3)) + 1))
                        else:
                            dve.wait_ge(*W("conv_done", j - 2))
                    tap = lambda k: par[:, COL["conv_w"] + k * 16 + j:COL["conv_w"] + k * 16 + j + 1]
                    a = acc5[:, j % 3, :]
                    chain(TS(a, pre5[:, j % 2, 0:W5], tap(0), None, ALU.mult))
                    for k in range(1, K5):
                        ins = STT(a, pre5[:, j % 2, k:k + W5], tap(k), a, ALU.mult, ALU.add)
                        if k < K5 - 1:
                            chain(ins)
                    ins.then_inc(S("taps_done"), 1)
                dve.wait_ge(*W("act_job", jobs.index(("cum", 0)) + 1))
                for d in range(2):
                    ins = TT(dtr(WDT)[:, :, d * H:(d + 1) * H], dtr(DTV)[:, :, d * H:(d + 1) * H],
                             dts[:, ER, d * 96:(d + 1) * 96].rearrange("p (t h) -> p t h", h=H), ALU.mult)
                ins.then_inc(S("wdt_ready"), 1)
                dve.wait_ge(*W("act_job", len(jobs)))
                for k in range(KD):
                    for s in segs(main):
                        f = c31(0 if s == 0 else NCT)
                        ins = TT(vT[:, k, f:f + SEG[s][1]], vT[:, k, f:f + SEG[s][1]], mean[:, f:f + SEG[s][1]], ALU.subtract)
                    ins.then_inc(S("vc_ready"), 1)
                dve.wait_ge(*W("var_taken", 1))
                for s in segs(main):
                    f = c31(0 if s == 0 else NCT)
                    chain(inv(rs[:, f:f + SEG[s][1]], rs[:, f:f + SEG[s][1]]))
                for k in range(KD):
                    for s in segs(main):
                        f = c31(0 if s == 0 else NCT)
                        ins = TT(vT[:, k, f:f + SEG[s][1]], vT[:, k, f:f + SEG[s][1]], rs[:, f:f + SEG[s][1]], ALU.mult)
                    ins.then_inc(S("vn_ready"), 1)
                dve.wait_ge(*W("y_init", len(main)))
                todo = [(ch, g) for ch in main for g in range(G)]

                def add_outputs(q):
                    ch, g = todo[q]
                    dve.wait_ge(*W("yd_ready", q + 1))
                    yv = Y[:, ch, g * 256:(g + 1) * 256].rearrange("p (a b n) -> p a b n", a=2, b=2)
                    pv = PS[:, 3 + 2 * (q % 2), :].rearrange("p (a c n) -> p a c n", a=2, n=HD)[:, :, 0:4:3, :]
                    return TT(yv, yv, pv, ALU.add).then_inc(S("yd_taken"), 1)

                for q, (ch, g) in enumerate(todo):
                    dt_of = lambda d, h: dts[:, DTV, ch * 32 + d * H + h:ch * 32 + d * H + h + 1]
                    dve.wait_ge(*W("s_ready", q + 1))
                    for b, mk in enumerate((LE, GE)):
                        TT(SUL[:, b, :], PS[:, 2 + 2 * (q % 2), 0:P], masks[:, mk, :], ALU.mult).then_inc(S("sul_ready"), 1)
                    dve.wait_ge(*W("sul_ready", 2 * q + 2))
                    for r in range(R):
                        ins = TS(GA[:, r * P:(r + 1) * P], SUL[:, 1, :], dt_of(1, g * R + r), None, ALU.mult)
                    chain(ins)
                    if q >= 2:
                        dve.wait_ge(*W("yd_ready", q - 1))
                    for r in range(R):
                        ins = STT(GB[:, q % 2, r * P:(r + 1) * P], SUL[:, 0, :], dt_of(0, g * R + r),
                                  GA[:, r * P:(r + 1) * P], ALU.mult, ALU.add)
                    chain(ins)
                    dve.wait_ge(*W("e_ready", q + 1))
                    TT(GB[:, q % 2, :], GB[:, q % 2, :], E[:, q % 2, :], ALU.mult).then_inc(S("m_ready"), 1)
                    if q:
                        add_outputs(q - 1)
                add_outputs(len(todo) - 1)
                dve.wait_ge(*W("yd_taken", len(todo)))
                nread = nupd = 0
                for d, n, ch in STEPS:
                    per_head = lambda buf, f: dts[:, buf, f:f + H].unsqueeze(2).to_broadcast([P, H, HD])
                    hv = hst[:, d, :].rearrange("p (h n) -> p h n", h=H)
                    ov = otmp[:].rearrange("p (h n) -> p h n", h=H)
                    if (d, n, ch) in reads(main):
                        dve.wait_ge(*W("o_ready", nread + 1))
                        seen(TT(ov, PS[:, 4:6, :].rearrange("p b (h n) -> p (b h) n", n=HD), per_head(EC, d * 96 + ch * H),
                                ALU.mult), "o_taken", nread + 1)
                        nread += 1
                        chain(TT(Y[:, ch, :], Y[:, ch, :], otmp[:], ALU.add))
                    if (d, n, ch) in UPDATES:
                        if n:
                            chain(TT(hv, hv, per_head(ET, ch * 32 + d * H), ALU.mult))
                        dve.wait_ge(*W("st_ready", nupd + 1))
                        new = PS[:, 6:8, :].rearrange("p b n -> p (b n)")
                        if n:
                            ins = TT(hst[:, d, :], hst[:, d, :], new, ALU.add)
                        else:
                            ins = dve.tensor_copy(hst[:, d, :], new)
                        nupd += 1
                        seen(ins, "h_ready", nupd)
                for n, t in enumerate(main):
                    dve.wait_ge(*W(f"szl_in{n % 2}", 16 * (n // 2 + 1)))
                    TT(Y[:, t, :], Y[:, t, :], szl[:, n % 2, :], ALU.mult).then_inc(S("yz_ready"), 1)
                    dve.wait_ge(*W("y_rms", n + 1))
                    inv(rstd[:, n:n + 1], ss[:, 1:2]).then_inc(S("y_rstd"), 1)
                for n, t in enumerate(main):
                    st = 0 if t >= NCT else 1
                    b = 4 * ((n // 2) % 2) + 2 * (n % 2)
                    dve.wait_ge(*W("m_rms", n + 1))
                    chain(inv(rstd[:, 0:1], ss[:, 1:2]))
                    if n == 0:
                        dve.wait_ge(*W("gpb_in", 32))
                    xr_ = xres[:, n % 2, :]
                    seen(STT(xn2[:, n, :], PS[:, b:b + 2, :].rearrange("p b n -> p (b n)"), rstd[:, 0:1], gpb[:, st, :],
                             ALU.mult, ALU.mult), "m_taken", n + 1)
                    dve.wait_ge(*W(f"xres_in{n % 2}", 16 * (n // 2 + 1)))
                    TT(xr_, xr_, xn2[:, n, :], ALU.add).then_inc(S("x1_ready"), 1)
                    dve.wait_ge(*W("x1_rms", n + 1))
                    inv(rstd[:, 1:2], ss[:, 3:4]).then_inc(S("x1_rstd"), 1)
                for n, t in enumerate(main):
                    dve.wait_ge(*W("logit_ready", n + 1))
                    chain(dve.reduce_max(sm[:, 2, n:n + 1], PS[:, 2 + n, 0:NE], AX_X))
                    TS(sm[:, 0, n:n + 1], sm[:, 2, n:n + 1], -1.0, None, ALU.mult).then_inc(S("lmax_ready"), 1)
                    dve.wait_ge(*W("lexp_ready", n + 1))
                    chain(inv(sm[:, 3, n:n + 1], sm[:, 1, n:n + 1]))
                    TS(aff[:, n, :], aff[:, n, :], sm[:, 3, n:n + 1], None, ALU.mult).then_inc(S("aff_ready"), 1)
                npt = 48 if main[0] == 0 else NE
                chain(dve.memset(affT[:], -1.0))
                dve.wait_ge(*W("affT_done", 1))
                if main[0] == 0:
                    dve.tensor_copy(affT[32:32 + NE, 0:CTX], PS[0:NE, 4, 0:CTX])
                seen(dve.tensor_copy(affT[0:NE, :], PS[0:NE, 5, :]), "affT_taken", 1)
                for r in range(CL // 8):
                    c8 = slice(8 * r, 8 * r + 8)
                    chain(dve.max(topv[0:npt, c8], affT[0:npt, :]))
                    dve.max_index(topi_u[0:npt, c8], topv[0:npt, c8], affT[0:npt, :])
                    chain(dve.match_replace(affT[0:npt, :], topv[0:npt, c8], affT[0:npt, :], -1.0))
                if main[0] == 0:
                    dve.tensor_copy(gi[:, 0, CL:SL], topv[32:32 + NE, 0:CC])
                    dve.tensor_copy(gi[:, 1, CL:SL], topi_u[32:32 + NE, 0:CC])
                dve.tensor_copy(gi[:, 0, 0:CL], topv[0:NE, :])
                chain(dve.tensor_copy(gi[:, 1, 0:CL], topi_u[0:NE, :]))
                TS(gi[:, 1, 0:CL], gi[:, 1, 0:CL], float(CTX), None, ALU.add).then_inc(S("gi_ready"), 1)
                dve.wait_ge(*W("giT_done", 1))
                chain(dve.tensor_copy(gateT[0:slot_n, :], PS[0:slot_n, 6, 0:NE]))
                seen(dve.tensor_copy(idxT_u[0:slot_n, :], PS[0:slot_n, 6, NE:2 * NE]), "dn_free", 1)

                def next_rows(e):
                    dve.tensor_copy(idg_u[0:slot_n, :], idxT_u[0:slot_n, bass.ds(e, 1)]).then_inc(S("idg_ready"), 1)

                def take_sel(par, n):
                    dve.wait_ge(*W("selT_done", n))
                    for st, (lo, hi) in enumerate(((0, CL), (CL, slot_n))):
                        for k in range(KD // 2, KD) if hi > lo else ():
                            ins = TS(selT[:, par, k, lo:hi], PS[:, k // 4, (k % 4) * P + lo:(k % 4) * P + hi],
                                     scl[:, 1, st, k:k + 1], modc[:, 3, st, k:k + 1], ALU.mult, ALU.add)
                    ins.then_inc(S("selT_dve"), 1)

                def scatter_rows(par, e):
                    dve.wait_ge(*W("scattered", 16 * e + 16))
                    dve.tensor_copy(ids_u[0:slot_n, par:par + 1], idxT_u[0:slot_n, bass.ds(e, 1)])
                    dve.tensor_copy(gcur[0:slot_n, par:par + 1], gateT[0:slot_n, bass.ds(e, 1)]).then_inc(S("gate_cur"), 1)

                def expert(par, e, first=False, nxt=True, last=False):
                    for b, (f, w) in enumerate(FB):
                        dve.wait_ge(*W("hs_ready", 3 * e + b + 1))
                        if b == 0 and not first:
                            dve.wait_ge(*W("hT_done", e))
                        TT(hh[0:slot_n, f:f + w], hs[0:slot_n, 0:w], PS[0:slot_n, 3 + b, 0:w], ALU.mult).then_inc(
                            S("h_rows"), 1)
                    if not first:
                        scatter_rows(1 - par, e - 1)
                    if not last:
                        take_sel(1 - par, e + 2)
                        if nxt:
                            next_rows(e + 2)
                    dve.wait_ge(*W("hT_done", e + 1))
                    dve.tensor_copy(hT[:, par, 4:8, 0:slot_n], PS[:, 3, :].rearrange("p (j s) -> p j s", s=P)[:, :, 0:slot_n])
                    dve.tensor_copy(hT[:, par, 8:11, 0:slot_n],
                                    PS[:, 4, 0:3 * P].rearrange("p (j s) -> p j s", s=P)[:, :, 0:slot_n]).then_inc(
                        S("hT_dve"), 1)

                next_rows(0)
                take_sel(0, 1)
                next_rows(1)
                expert(0, 0, first=True)
                with dve.Fori(1, NE - 3, 2) as e:
                    expert(1, e)
                    expert(0, e + 1)
                for e in range(NE - 3, NE):
                    expert(e % 2, e, nxt=e + 2 < NE, last=e == NE - 1)
                scatter_rows(1, NE - 1)
                for n, t in enumerate(main):
                    st = 0 if t >= NCT else 1
                    dve.wait_ge(*W("f_rms", n + 1))
                    chain(inv(rstd[:, 2:3], ss[:, 5:6]))
                    if n == 0:
                        dve.wait_ge(*W("gpb2_in", 32))
                    yv = yt[:, n % 2, :]
                    chain(STT(yv, yv, rstd[:, 2:3], gpb2[:, st, :], ALU.mult, ALU.mult))
                    dve.wait_ge(*W(f"xr_in{n % 2}", 16 * (n // 2 + 1)))
                    TT(xr[:, n % 2, :], xr[:, n % 2, :], yv, ALU.add).then_inc(S("xf_ready"), 1)

        @block.gpsimd
        def _(pool):
            chained = [0]

            def chain(ins):
                chained[0] += 1
                ins.then_inc(sem("pool_chain"), 1)
                pool.wait_ge(sem("pool_chain"), chained[0])

            pool.memset(ones[:], 1.0)
            pool.memset(masks[:, AVG, :], 1.0 / D)
            chain(pool.memset(masks[:, 0:AVG, :], 1.0))
            for mk, op, b, cm, st in ((IDN, ALU.is_equal, 0, 1, -1), (LE, ALU.is_ge, 0, -1, 1), (GE, ALU.is_ge, 0, 1, -1),
                                      (GT, ALU.is_ge, -1, 1, -1), (LT, ALU.is_ge, -1, -1, 1)):
                ins = pool.affine_select(out=masks[:, mk, :], in_=masks[:, mk, :], compare_op=op, fill=0.0, base=b,
                                         pattern=[[st, P]], channel_multiplier=cm)
            ins.then_inc(sem("consts"), 1)
            for L, main, jobs, slots in LAYERS:
                S, W = sem, counter(L)
                slot_n = CL + (CC if main[0] == 0 else 0)
                TT = pool.tensor_tensor
                bcol = par[:, COL["ada_b"]:COL["ada_b"] + 48].rearrange("p (s k) -> p s k", k=KD)
                pool.wait_ge(*W("par_taken", 1))
                for s in range(6):
                    if s in GATES:
                        gi_ = GATES.index(s)
                        pool.wait_ge(*W("act_job", jobs.index(("ada", s)) + 1))
                        if gi_ == 0:
                            pool.wait_ge(*W("brow_in", 8 * 16))
                        for r in (0, 32):
                            row = arow[r:r + 1, s % 2, :]
                            chain(TT(row, row, brow[r:r + 1, 2 * gi_, :], ALU.add))
                            TT(brow[r:r + 1, 2 * gi_ + 1, :], row, brow[r:r + 1, 2 * gi_ + 1, :], ALU.mult).then_inc(
                                S("gp_ready"), 1)
                            pool.wait_ge(*W("gp_ready", 2 * gi_ + r // 32 + 1))
                            pool.dma_start(gp_d[gi_, r // 32:r // 32 + 1, :], brow[r:r + 1, 2 * gi_ + 1, :]).then_inc(
                                S("gp_out"), 16)
                        continue
                    pool.wait_ge(*W("act_job", jobs.index(("adaT", s)) + 1))
                    chain(TT(modc[:, s, :, :], modc[:, s, :, :], bcol[:, s, :].unsqueeze(1).to_broadcast([P, 2, KD]), ALU.add))
                    if s in (1, 4):
                        chain(pool.tensor_scalar(scl[:, s // 4, :, :], modc[:, s, :, :], 1.0, None, ALU.add))
                        gain = par[:, COL["pre_g" if s == 1 else "moe_g"]:][:, 0:KD]
                        ins = TT(scl[:, s // 4, :, :], scl[:, s // 4, :, :], gain.unsqueeze(1).to_broadcast([P, 2, KD]), ALU.mult)
                        ins.then_inc(S("mod_ready"), 1)
                pool.wait_ge(*W("pe_job", jobs.index(("norm", NT - 1)) + 1))
                for j in range(KD):
                    for f in (0, g31 + CTX, 2 * g31 + T):
                        pool.memset(vT[:, j, f:f + g31], 0.0)
                for b in range(2):
                    for f in (0, g5 + CTX, 2 * g5 + T):
                        ins = pool.memset(pre5[:, b, f:f + g5], 0.0)
                ins.then_inc(S("pads_ready"), 1)
                for j in range(KD):
                    pool.wait_ge(*W("act_job", jobs.index(("a", j)) + 1))
                    for s in segs(main):
                        f = g31 + c31(0 if s == 0 else NCT)
                        w = slice(SEG[s][0], SEG[s][0] + SEG[s][1])
                        ins = TT(vT[:, j, f:f + SEG[s][1]], asb[:, w], sg[:, w], ALU.mult)
                    ins.then_inc(S("v_made"), 1)
                pool.wait_ge(*W("pe_job", jobs.index(("xT", 11)) + 1))
                pool.wait_ge(*W("act_job", jobs.index(("xT", 11)) + 1))
                pool.wait_ge(*W("pe_job", jobs.index(("xbc", 15)) + 1))
                heads = lambda ap: ap.rearrange("p (h n) -> p h n", h=H)
                for ch in main:
                    TT(heads(Y[:, ch, :]), heads(xtok[:, ch, :]), hdrow[:, 2, 0:H].unsqueeze(2).to_broadcast([P, H, HD]),
                       ALU.mult).then_inc(S("y_init"), 1)
                pool.wait_ge(*W("conv_done", 2 * KD))
                pool.wait_ge(*W("act_job", len(jobs)))
                q = 0
                for ch in main:
                    for g in range(G):
                        if q >= 2:
                            pool.wait_ge(*W("arg_ready", q - 1))
                        for d, mk in ((0, LE), (1, GE)):
                            f = ch * 32 + d * H + g * R
                            ins = TT(dAm[:, q % 2, d, :].rearrange("p (r n) -> p r n", r=R),
                                     masks[:, mk, :].unsqueeze(1).to_broadcast([P, R, P]),
                                     dts[:, DA, f:f + R].unsqueeze(2).to_broadcast([P, R, P]), ALU.mult)
                        ins.then_inc(S("dam_ready"), 1)
                        q += 1
                pool.wait_ge(*W("wdt_ready", 1))
                nupd = 0
                for d, n, ch in STEPS:
                    if (d, n, ch) in UPDATES:
                        if nupd:
                            pool.wait_ge(*W("st_ready", nupd))
                        f = ch * 32 + d * H
                        TT(heads(xw[:]), heads(xtok[:, ch, :]), dts[:, WDT, f:f + H].unsqueeze(2).to_broadcast([P, H, HD]),
                           ALU.mult).then_inc(S("xw_ready"), 1)
                        nupd += 1
                pool.wait_ge(*W("yd_ready", q))
                pool.wait_ge(*W("m_ready", q))
                for i in range(2):
                    pool.wait_ge(*W(f"sz_out{i}", 16 * len(main) // 2))
                for n, t in enumerate(main):
                    if n >= 2:
                        pool.wait_ge(*W("yz_ready", n - 1))
                    pool.dma_start(szl[:, n % 2, :], sz_d[t * P:(t + 1) * P, :]).then_inc(S(f"szl_in{n % 2}"), 16)
                pool.wait_ge(*W("yn_ready", len(main)))
                for st in range(2):
                    pool.dma_start(gpb[:, st, :], gp_d[0, st, :].partition_broadcast(P)).then_inc(S("gpb_in"), 16)
                pool.dma_start(rw[:], router_w[L].rearrange("(k p) e -> p k e", p=P)).then_inc(S("rw_in"), 16)
                for n, t in enumerate(main):
                    if n >= 2:
                        pool.wait_ge(*W(f"x1_out{n % 2}", 16 * (n // 2)))
                        pool.wait_ge(*W("xn2_ready", n - 1))
                    pool.dma_start(xres[:, n % 2, :], src_rows(L, t)).then_inc(S(f"xres_in{n % 2}"), 16)
                    if n:
                        store_x1(pool, L, main, n - 1)
                store_x1(pool, L, main, len(main) - 1)
                for i in range(2):
                    pool.wait_ge(*W(f"x1_out{i}", 16 * len(main) // 2))
                    pool.wait_ge(*W(f"xn_out{i}", 16 * len(main) // 2))

                pool.wait_ge(*W("u2T_done", len(main)))
                chain(pool.memset(zro[:], 0.0))
                for i in range(2):
                    pool.dma_start(y_d[i * T // 2:(i + 1) * T // 2, :].rearrange("(t p) n -> p t n", p=P),
                                   zro[:].unsqueeze(1).to_broadcast([P, NT // 2, D])).then_inc(S("scattered"), 16)
                    pool.wait_ge(*W("scattered", 16 * (i + 1)))

                def settle(n):
                    if L or not isinstance(n, int) or n:
                        pool.wait_ge(*W("settled", n))
                    TT(eps[:, 1:2], masks[:, IDN, 0:1], masks[:, IDN, 0:1], ALU.add).then_inc(S("settled"), 1)

                def gather(e, n):
                    pool.wait_ge(*W("idg_ready", e + 1))
                    settle(n)
                    pool.indirect_dma_start(out=sel[0:slot_n, :], out_offset=None, in_=xn_d,
                                            in_offset=bass.IndirectOffsetOnAxis(idg_u[0:slot_n, 0:1], 0)).then_inc(
                        S("sel_in"), 16)

                def scatter(par, e, n):
                    pool.wait_ge(*W("dn_free", e + 2))
                    pool.wait_ge(*W("scattered", 16 * e + 32))
                    settle(n)
                    pool.indirect_dma_start(out=y_d, out_offset=bass.IndirectOffsetOnAxis(ids_u[0:slot_n, par:par + 1], 0),
                                            in_=ob[0:slot_n, par, :], in_offset=None, compute_op=ALU.add).then_inc(
                        S("scattered"), 16)

                for e in range(3):
                    gather(e, e)
                with pool.Fori(1, NE - 3, 2) as e:
                    gather(e + 2, 2 * e + 1)
                    scatter(0, e - 1, 2 * e + 2)
                    gather(e + 3, 2 * e + 3)
                    scatter(1, e, 2 * e + 4)
                gather(NE - 1, 2 * NE - 5)
                for e in range(NE - 4, NE):
                    scatter(e % 2, e, NE + e)


_INS = ["x", "c", "ctx", "c_ctx", "ada_w", "ada_b", "mix_pre_g", "w_in", "conv_w", "conv_b", "dt_bias", "a_log",
        "d_skip", "ssd_norm_g", "cm_dw_w", "cm_dw_b", "cm_ln_g", "cm_ln_b", "w_out", "mix_post_g", "moe_pre_g",
        "router_w", "exp_w_gate", "exp_w_up", "exp_w_down", "moe_post_g"]


def kernel(**inputs):
    import concourse.bacc as bacc
    from concourse.bass_utils import run_bass_kernel_spmd

    nc = bacc.Bacc("TRN2", target_bir_lowering=False, num_devices=1)
    arrays, aps = {}, {}
    for name in _INS:
        a = np.ascontiguousarray(inputs[name])
        arrays[f"in_{name}"] = a
        aps[name] = nc.dram_tensor(f"in_{name}", a.shape, mybir.dt.from_np(a.dtype), kind="ExternalInput").ap()
    out = nc.dram_tensor("out_x", (1, SEQ, D), F32, kind="ExternalOutput").ap()
    build(nc, out=out, **aps)
    r = run_bass_kernel_spmd(nc, [arrays], core_ids=[0])
    return r.results[0]["out_x"]
```

```python
from contextlib import ExitStack

import numpy as np
import concourse.bass as bass
from concourse import mybir
from concourse.alu_op_type import AluOpType as ALU

ACT = mybir.ActivationFunctionType
AX_X = mybir.AxisListType.X
F32 = mybir.dt.float32
F32R = mybir.dt.float32r
U32 = mybir.dt.uint32

P = 128
D = 1024
KD = D // P
CTX, SEQ = 256, 512
T = CTX + SEQ
NT = T // P
NCT = CTX // P
DEPTH = 2
H, HD, G, R, NS = 16, 64, 4, 4, 128
XBC = 2048
SSD_IN = XBC + 2 * H
Z_END = SSD_IN + D
IN_COLS = Z_END + 2 * D
K5, K31 = 5, 31
NE, FE = 16, 1408
FB = [(0, 512), (512, 512), (1024, 384)]
JF = FE // P
GU = 2 * KD
UNITS = GU + JF
RING = 9
AHEAD = 5
CL, CC = 2 * SEQ // NE, 2 * CTX // NE
EPS = 1e-6
WS = 5
SEG = [(0, CTX), (CTX, SEQ)]

COL = {"conv_w": 0, "conv_b": 80, "dw_b": 96, "ln_g": 104, "ln_b": 112, "pre_g": 120,
       "dw_w": 128, "moe_g": 376, "ada_b": 384, "norm_g": 432, "c": 440, "c_ctx": 448}


GATES = (2, 5)


def first_jobs(main):
    jobs = []
    for s in range(6):
        jobs.append(("ada", s))
        if s >= 1 and s - 1 not in GATES:
            jobs.append(("adaT", s - 1))
    jobs += [("norm", t) for t in range(NT)]
    for j in range(KD):
        jobs += [("g", j), ("a", j)]
    jobs += [("dt", 0)] + [("z", t) for t in main] + [("dtT", 0)]
    jobs += [("cum", 0)]
    for j in range(XBC // P):
        jobs.append(("xbc", j))
        if 2 <= j < 14:
            jobs.append(("xT", j - 2))
    jobs += [("mean", 0)]
    return jobs


def weight_slots(jobs):
    out = []
    for kind, i in jobs:
        if kind == "ada":
            out += [("ada", i, q) for q in range(4)]
        elif kind == "g" and i % 2 == 0:
            out += [("g", i // 2, 0), ("a", i // 2, 0)]
        elif kind == "dt":
            out += [("dt", 0, 0)] + [("z", 0, q) for q in range(4)]
        elif kind == "xbc" and i % 2 == 0:
            out.append(("xbc", i // 2, 0))
    return out


def build(nc, x, c, ctx, c_ctx, ada_w, ada_b, mix_pre_g, w_in, conv_w, conv_b, dt_bias, a_log,
          d_skip, ssd_norm_g, cm_dw_w, cm_dw_b, cm_ln_g, cm_ln_b, w_out, mix_post_g, moe_pre_g,
          router_w, exp_w_gate, exp_w_up, exp_w_down, moe_post_g, out):
    base = (nc.sbuf_base + 63) // 64 * 64
    end = nc.sbuf_usable_end

    def at(name, shape, off, dt=F32):
        n = int(np.prod(shape[1:])) * 4
        assert base + off + n <= end, (name, off + n, end - base)
        return nc.alloc_sbuf_tensor_at(name, list(shape), dt, offset=base + off)

    o = 0

    def perm(name, shape, dt=F32):
        nonlocal o
        t = at(name, shape, o, dt)
        o += (int(np.prod(shape[1:])) * 4 + 31) // 32 * 32
        return t

    masks = perm("masks", [P, 6, P])
    IDN, LE, GE, GT, LT, AVG = range(6)
    ones = perm("ones", [P, P])
    par = perm("par", [P, 512])
    cstat = perm("cstat", [P, KD, 33])
    modc = perm("modc", [P, 6, 2, KD])
    scl = perm("scl", [P, 2, 2, KD])
    ss = perm("ss", [P, 16])
    rstd = perm("rstd", [P, 16])
    eps = perm("eps", [P, 2])
    hdrow = perm("hdrow", [P, 5, 2 * H])
    W0 = o = (o + 63) // 64 * 64
    wslot = at("wslot", [P, WS, 2048], W0)
    o = W0 + WS * 8192
    U0 = o
    uT = at("uT", [P, KD, T], U0)
    Y = at("Y", [P, NT, D], U0)
    o += KD * T * 4
    X0 = o
    xtok = at("xtok", [P, NT, D], X0)
    o += NT * D * 4
    btok = at("btok", [P, NT, G * NS], o)
    o += NT * G * NS * 4
    B0 = o
    g5 = K5 // 2
    W5 = T + g5
    bct = at("bct", [P, 2 * G, W5], B0)
    yT = at("yT", [P, KD, T], B0)
    brow = at("brow", [33, 4, D], B0)
    o += 2 * G * W5 * 4
    g31 = K31 // 2
    W31 = T + g31
    PAD31 = T + 3 * g31
    vT = at("vT", [P, KD, PAD31], o)
    o += KD * PAD31 * 4
    TMP = (o + 63) // 64 * 64
    room = (end - base - TMP) // 32 * 32

    def tmp(first, specs):
        off, got = first, []
        for name, shape in specs:
            got.append(at(name, shape, TMP + off))
            off += (int(np.prod(shape[1:])) * 4 + 31) // 32 * 32
        assert off <= room, (off, room)
        return got, off

    prow = at("prow", [P, 4, P], U0)
    (xt, junk, arow), _ = tmp(2048, [("xt", [P, NT, D]), ("junk", [P, D]), ("arow", [33, 2, D])])
    (sg, asb, cacc, pre5, acc5, szt, dtT), _ = tmp(0, [
        ("sg", [P, T]), ("asb", [P, T]), ("cacc", [P, 2, W31]), ("pre5", [P, 2, W5 + 2 * g5]),
        ("acc5", [P, 3, W5]), ("szt", [P, 2, D]), ("dtT", [2 * H, T])])
    DTN = NT * 2 * H
    (dts, ), dt_end = tmp(room - 9 * DTN * 4, [("dts", [P, 9, DTN])])
    D1, D2, D3, DTV, DA, EC, ER, ET, WDT = range(9)
    (mean, sqb, rs), ln_end = tmp(31 * 1024, [("mean", [P, W31]), ("sqb", [P, 2, W31]), ("rs", [P, W31])])
    assert TMP + ln_end <= TMP + room - 9 * DTN * 4
    (dAm, E, xw, hst, SUL, GB, GA, otmp), ssd_end = tmp(0, [
        ("dAm", [P, 2, 2, 512]), ("E", [P, 2, 512]), ("xw", [P, D]), ("hst", [P, 2, D]), ("SUL", [P, 2, 2, P]),
        ("GB", [P, 2, 512]), ("GA", [P, 2, 512]), ("otmp", [P, D])])
    (szl,), _ = tmp(ssd_end, [("szl", [P, 2, D])])
    (gpb, xres, xn2, u2T, rw, sm, aff), _ = tmp(0, [
        ("gpb", [P, 2, D]), ("xres", [P, 2, D]), ("xn2", [P, NT, D]), ("u2T", [P, KD, P]),
        ("rw", [P, KD, NE]), ("sm", [P, 4, NT]), ("aff", [P, NT, NE])])
    SL = CL + CC
    o = W0

    def moe(name, shape, dt=F32):
        nonlocal o
        t = at(name, shape, o, dt)
        o += (int(np.prod(shape[1:])) * 4 + 31) // 32 * 32
        return t

    wr = moe("wr", [P, RING, FE])
    whi = moe("whi", [P, RING, FE], F32R)
    wlo = moe("wlo", [P, RING, FE], F32R)
    selF = moe("selF", [P, KD, SL])
    shi = moe("shi", [P, KD, SL], F32R)
    slo = moe("slo", [P, KD, SL], F32R)
    hhi = moe("hhi", [P, 2, JF, SL], F32R)
    hlo = moe("hlo", [P, 2, JF, SL], F32R)
    affT, topv, topi, gi = (moe(n, sh) for n, sh in (
        ("affT", [48, SEQ]), ("topv", [48, CL]), ("topi", [48, CL]), ("gi", [NE, 2, SL])))
    idxT, gateT, idg, ids, gcur = (moe(n, sh) for n, sh in (
        ("idxT", [SL, NE]), ("gateT", [SL, NE]), ("idg", [SL, 1]), ("ids", [SL, 2]), ("gcur", [SL, 2])))
    sel, hs, hh = (moe(n, sh) for n, sh in (("sel", [SL, D]), ("hs", [SL, 512]), ("hh", [SL, FE])))
    zro = at("zro", [P, D], o)
    ob = moe("ob", [SL, 2, D])
    topi_u, idg_u, ids_u, idxT_u = (b[:].bitcast(U32) for b in (topi, idg, ids, idxT))
    yt = at("yt", [P, NT, D], U0 + 4096)
    xr = at("xr", [P, NT, D], U0 + 4096 + NT * D * 4)
    gpb2 = at("gpb2", [P, 2, D], U0 + 4096 + 2 * NT * D * 4)
    assert U0 + 4096 + (2 * NT + 2) * D * 4 <= B0
    PS = nc.alloc_psum_tensor("PS", [P, 8, 512], F32)

    def dram(name, shape):
        return nc.dram_tensor(name, shape, F32, kind="Internal").ap()

    x1_d, xn_d, y_d, sz_d = (dram(n, (T, D)) for n in ("x1_d", "xn_d", "y_d", "sz_d"))
    xl_d = dram("xl_d", (T, D))
    gp_d = dram("gp_d", (DEPTH, 2, 2, D))

    sems = {}

    def sem(name):
        if name not in sems:
            sems[name] = nc.alloc_semaphore(name)
        return sems[name]

    LAYERS = []
    for L in range(DEPTH):
        main = list(range(NT)) if L < DEPTH - 1 else list(range(NCT, NT))
        jobs = first_jobs(main)
        LAYERS.append((L, main, jobs, weight_slots(jobs)))

    def gu(e, i):
        return (e, i) if isinstance(e, int) and e == 0 else (e, GU - UNITS + i)

    def dn(e, i):
        return (e, GU + i) if isinstance(e, int) and e == NE - 1 else (e, 2 * GU + i)

    def number(u):
        return u[0] * UNITS + u[1]

    def slot_turn(u):
        return u[1] % RING, u[0] * (UNITS // RING) + u[1] // RING

    def seg_banks(unit, s):
        return PS[:, 2 * unit + s, 0:SEG[s][1]]

    def unit2(unit, rows=P):
        return PS[0:rows, 2 * unit:2 * unit + 2, :].rearrange("p b n -> p (b n)")

    def c5(t):
        return P * t + (g5 if t >= NCT else 0)

    def c31(t):
        return P * t + (g31 if t >= NCT else 0)

    def logits(n):
        return PS[:, 4 * ((n // 2) % 2) + 2 + n % 2, 0:NE]

    def segs(main):
        return (0, 1) if main[0] == 0 else (1,)

    def pairs(main):
        return [main[i:i + 2] for i in range(0, len(main), 2)]

    def src_rows(L, t):
        if L:
            return xl_d[t * P:(t + 1) * P, :]
        return ctx[0, t * P:(t + 1) * P, :] if t < NCT else x[0, (t - NCT) * P:(t - NCT + 1) * P, :]

    def slot_free(L, jobs, slots, n):
        kind, i, q = slots[n]
        if kind == "ada" and q < 3:
            return counter(L)("ada_used", 3 * i + q + 1)
        last = {"ada": i, "g": 2 * i + 1, "a": 2 * i + 1, "xbc": 2 * i + 1, "dt": 0,
                "z": max((j[1] for j in jobs if j[0] == "z"))}[kind]
        return counter(L)("pe_job", jobs.index((kind, last)) + 1)

    def scan(d):
        ctx_first = list(range(NCT)) if d == 0 else list(range(NCT))[::-1]
        lat = list(range(NCT, NT)) if d == 0 else list(range(NCT, NT))[::-1]
        return ctx_first + lat

    STEPS = [(d, n, scan(d)[n]) for n in range(NT) for d in range(2)]

    def reads(main):
        return [s for s in STEPS if s[1] and s[2] in main]

    UPDATES = [s for s in STEPS if s[1] < NT - 1]

    units = NT * G
    TOTAL = {}

    def count(total, names):
        TOTAL.update({name: total for name in names.split()})

    count(1, "par_T par_taken f_rms x_rms x_rstd pads_ready sp_abs sp_exp sp_one sp_ln a_exp da_ready wdt_ready var_taken "
             "affT_done affT_taken gi_ready giT_done")
    count(2, "mod_ready")
    count(NT, "x_sq xn_ready y_init yz_ready y_sq y_rms y_rstd yn_ready ynT_done yT_ready yT_dve m_sq m_rms m_taken x1_ready "
              "x1_sq x1_rms x1_rstd xn2_ready u2T_done u2_ready logit_ready lmax_ready lexp_ready aff_ready "
              "f_sq xf_ready")
    count(KD, "v_made conf_done vc_ready sq_ready sq_used vn_ready v_ready")
    count(XBC // P, "taps_done conv_done")
    count(units, "ga_ready dam_ready arg_ready e_ready s_ready m_ready yd_ready yd_taken")
    count(2 * units, "sul_ready")
    count(len(reads(range(NT))), "o_ready o_taken")
    count(len(UPDATES), "xw_ready st_ready h_ready")
    count(len(LAYERS[0][2]), "pe_job act_job")
    count(18, "ada_used")
    count(4, "gp_ready")
    count(NT // 2 * KD, "wo_used")
    count(16 * 16, "par_in")
    count(16 * NT, "out_stored")
    count(8 * 16, "brow_in")
    count(4 * 16, "gp_out")
    count(2 * 16, "gpb_in gpb2_in")
    count(16, "rw_in xr_in yt_in")
    count(16 * NT // 2, "sz_out0 sz_out1 szl_in0 szl_in1 x1_out0 x1_out1 xn_out0 xn_out1 "
                        "xres_in0 xres_in1")
    count(NE, "selT_done selT_act selT_dve hT_done hT_act hT_dve gate_cur selF_act selF_dve shi_dve idg_ready")
    count(NE + 1, "dn_free")
    count(2 * NE, "settled")
    count(3 * NE, "hs_ready h_rows")
    count(UNITS * NE, "hi_made lo_made unit_used")
    for i in range(RING):
        count(16 * UNITS * NE // RING, f"unit_in{i}")
    count(16 * NE, "sel_in")
    count(16 * NE + 32, "scattered")
    pieces = len(LAYERS[0][3]) + NT // 2 * KD
    for i in range(WS):
        count(16 * len(range(i, pieces, WS)), f"w_in{i}")

    def counter(L):
        return lambda name, v: (sem(name), L * TOTAL[name] + v)

    def steps_at(main, q):
        n = len(main) * G
        return [s for k, s in enumerate(STEPS) if (k + 1) * n // len(STEPS) - 1 == q]

    def seg_cols(main, gap):
        return (0, T + gap) if main[0] == 0 else (CTX + gap, SEQ)

    def store_out(pool, L, main, n):
        t = main[n]
        dst = xl_d[t * P:(t + 1) * P, :] if L < DEPTH - 1 else out[0, (t - NCT) * P:(t - NCT + 1) * P, :]
        pool.wait_ge(*counter(L)("xf_ready", n + 1))
        pool.dma_start(dst, xr[:, t, :]).then_inc(sem("out_stored"), 16)

    def store_x1(pool, L, main, n):
        t = main[n]
        pool.wait_ge(*counter(L)("x1_ready", n + 1))
        pool.dma_start(x1_d[t * P:(t + 1) * P, :], xres[:, n % 2, :]).then_inc(sem(f"x1_out{n % 2}"), 16)
        pool.wait_ge(*counter(L)("xn2_ready", n + 1))
        pool.dma_start(xn_d[t * P:(t + 1) * P, :], xn2[:, n, :]).then_inc(sem(f"xn_out{n % 2}"), 16)

    with nc.Block() as block:
        @block.sync
        def _(sp):
            for L, main, jobs, slots in LAYERS:
                S, W = sem, counter(L)
                if L:
                    sp.wait_ge(*W("lo_made", 0))

                def rows(ap, n0, what):
                    ti, r = divmod(COL[what] + n0, P)
                    sp.dma_start(prow[r:r + ap.shape[0], ti, :], ap).then_inc(S("par_in"), 16)

                rows(conv_w[L].rearrange("k (t p) -> (k t) p", p=P), 0, "conv_w")
                for src, what in ((conv_b, "conv_b"), (cm_dw_b, "dw_b"), (cm_ln_g, "ln_g"), (cm_ln_b, "ln_b"),
                                  (mix_pre_g, "pre_g"), (moe_pre_g, "moe_g"), (ssd_norm_g, "norm_g"), (ada_b, "ada_b")):
                    rows(src[L].rearrange("(t p) -> t p", p=P), 0, what)
                dw = cm_dw_w[L].rearrange("k (t p) -> (k t) p", p=P)
                rows(dw[0:P], 0, "dw_w")
                rows(dw[P:K31 * KD], P, "dw_w")
                rows(c[0].rearrange("(t p) -> t p", p=P), 0, "c")
                rows(c_ctx.rearrange("(t p) -> t p", p=P), 0, "c_ctx")
                for i, src in enumerate((dt_bias[L].rearrange("a h -> (a h)"), a_log[L].rearrange("a h -> (a h)"), d_skip[L])):
                    sp.dma_start(hdrow[:, i, 0:src.shape[0]], src.partition_broadcast(P)).then_inc(S("par_in"), 16)
                if L:
                    sp.wait_ge(*W("unit_used", 0))
                for gi_, s in enumerate(GATES):
                    for r in (0, 32):
                        sp.dma_start(brow[r:r + 1, 2 * gi_, :], ada_b[L:L + 1, s * D:(s + 1) * D]).then_inc(S("brow_in"), 16)
                        sp.dma_start(brow[r:r + 1, 2 * gi_ + 1, :], (mix_post_g, moe_post_g)[gi_][L:L + 1, :]).then_inc(
                            S("brow_in"), 16)
                win = w_in[L].rearrange("(k p) n -> p k n", p=P)
                aw = ada_w[L].rearrange("(k p) n -> p k n", p=P)
                for n, (kind, i, q) in enumerate(slots):
                    if n == WS and L == 0:
                        for t in range(NT):
                            sp.dma_start(xt[:, t, :], src_rows(L, t)).then_inc(sem("x_in"), 16)
                    if n >= WS:
                        sp.wait_ge(*slot_free(L, jobs, slots, n - WS))
                    dst = wslot[:, n % WS, :]
                    if kind == "ada":
                        dst = dst.rearrange("p (k n) -> p k n", k=2)
                        src = aw[:, 2 * q:2 * q + 2, i * D:(i + 1) * D]
                    elif kind == "dt":
                        dst = dst[:, 0:KD * 32].rearrange("p (k n) -> p k n", k=KD)
                        src = win[:, :, XBC:SSD_IN]
                    else:
                        dst = dst.rearrange("p (k n) -> p k n", k=KD)
                        first = {"g": Z_END + D + i * 256, "a": Z_END + i * 256, "z": SSD_IN + q * 256,
                                 "xbc": i * 256}[kind]
                        src = win[:, :, first:first + 256]
                    sp.dma_start(dst, src).then_inc(S(f"w_in{n % WS}"), 16)
                wo = w_out[L].rearrange("(q b p) n -> q p b n", b=2, p=P)
                for m in range(len(pairs(main)) * KD):
                    n = len(slots) + m
                    if m >= WS:
                        sp.wait_ge(*W("wo_used", m - WS + 1))
                    else:
                        sp.wait_ge(*slot_free(L, jobs, slots, n - WS))
                    sp.dma_start(wslot[:, n % WS, :].rearrange("p (b n) -> p b n", b=2), wo[m % KD]).then_inc(
                        S(f"w_in{n % WS}"), 16)
                sp.wait_ge(*W("wo_used", len(pairs(main)) * KD))

                def load(u, src):
                    slot, turn = slot_turn(u)
                    if not isinstance(turn, int) or turn:
                        sp.wait_ge(*W("lo_made", number(u) - RING + 1))
                    sp.dma_start(wr[:, slot, 0:src.shape[-1]], src).then_inc(S(f"unit_in{slot}"), 16)

                def load_gate_up(e):
                    for k in range(KD):
                        for mi, w in ((0, exp_w_gate), (1, exp_w_up)):
                            load(gu(e, 2 * k + mi), w[L, bass.ds(e, 1), k * P:(k + 1) * P, :].rearrange("o p n -> (o p) n"))

                def load_down(e):
                    src = exp_w_down[L, bass.ds(e, 1), :, :].rearrange("o (p j) n -> (o p) j n", j=JF)
                    for j in range(JF):
                        load(dn(e, j), src[:, j, :])

                load_gate_up(0)
                with sp.Fori(1, NE) as e:
                    load_gate_up(e)
                    load_down(e - 1)
                load_down(NE - 1)

        @block.tensor
        def _(pe):
            def tr(dst, src, n):
                return pe.transpose(dst, src, masks[0:n, IDN, 0:n])

            pe.wait_ge(sem("consts"), 1)
            for L, main, jobs, slots in LAYERS:
                S, W = sem, counter(L)
                where = {sl: n for n, sl in enumerate(slots)}
                slot_n = CL + (CC if main[0] == 0 else 0)

                def weights(n):
                    pe.wait_ge(*W(f"w_in{n % WS}", 16 * (n // WS + 1)))
                    return wslot[:, n % WS, :]

                pe.wait_ge(*W("par_in", 16 * 16))
                for i, n in enumerate((P, P, P, 72)):
                    m = tr(PS[:, 0, i * P:i * P + n], prow[0:n, i, :], n)
                m.then_inc(S("par_T"), 1)
                pe.wait_ge(*W("par_taken", 1))
                pe.wait_ge(sem("cstat_ready"), 1)
                for n, (kind, i) in enumerate(jobs):
                    u = n % 4
                    if n >= 4:
                        pe.wait_ge(*W("act_job", n - 3))
                    if L and n == 3:
                        pe.wait_ge(*counter(L - 1)("dn_free", NE + 1))
                    if kind == "ada":
                        for q in range(4):
                            wv = weights(where["ada", i, q])
                            for kk in range(2):
                                for h in range(2):
                                    m = pe.matmul(PS[0:33, 2 * u + h, :], cstat[:, 2 * q + kk, :],
                                                  wv[:, kk * D + h * 512:kk * D + (h + 1) * 512],
                                                  start=q + kk == 0, stop=q + kk == 4)
                            if q < 3:
                                m.then_inc(S("ada_used"), 1)
                    elif kind == "adaT":
                        pe.wait_ge(*W("act_job", jobs.index(("ada", i)) + 1))
                        for k in range(KD):
                            m = tr(PS[:, 2 * u, k * 33:(k + 1) * 33], arow[:, i % 2, k * P:(k + 1) * P], 33)
                    elif kind == "norm":
                        pe.wait_ge(*W("xn_ready", i + 1))
                        for k in range(KD):
                            m = tr(PS[:, 2 * u + k // 4, (k % 4) * P:(k % 4 + 1) * P], xt[:, i, k * P:(k + 1) * P], P)
                    elif kind in ("g", "a", "xbc"):
                        if i == 0 and kind == "g":
                            pe.wait_ge(*W("act_job", jobs.index(("norm", NT - 1)) + 1))
                        wv = weights(where[kind, i // 2, 0]).rearrange("p (k n) -> p k n", k=KD)
                        for s in (0, 1) if kind == "xbc" else segs(main):
                            for k in range(KD):
                                m = pe.matmul(seg_banks(u, s), wv[:, k, (i % 2) * P:(i % 2 + 1) * P],
                                              uT[:, k, SEG[s][0]:SEG[s][0] + SEG[s][1]], start=k == 0, stop=k == KD - 1)
                    elif kind == "dt":
                        wv = weights(where["dt", 0, 0])[:, 0:KD * 32].rearrange("p (k n) -> p k n", k=KD)
                        for s in (0, 1):
                            for k in range(KD):
                                m = pe.matmul(PS[0:32, 2 * u + s, 0:SEG[s][1]], wv[:, k, :],
                                              uT[:, k, SEG[s][0]:SEG[s][0] + SEG[s][1]], start=k == 0, stop=k == KD - 1)
                    elif kind == "z":
                        for q in range(4):
                            wv = weights(where["z", 0, q]).rearrange("p (k n) -> p k n", k=KD)
                            for k in range(KD):
                                m = pe.matmul(PS[:, 2 * u + q // 2, (q % 2) * 256:(q % 2 + 1) * 256],
                                              uT[:, k, i * P:(i + 1) * P], wv[:, k, :], start=k == 0, stop=k == KD - 1)
                    elif kind == "dtT":
                        pe.wait_ge(*W("act_job", jobs.index(("dt", 0)) + 1))
                        for t in range(NT):
                            m = tr(PS[:, 2 * u, t * 32:(t + 1) * 32], dtT[:, t * P:(t + 1) * P], 32)
                    elif kind == "cum":
                        pe.wait_ge(*W("da_ready", 1))
                        dav = dts[:, DA, :].rearrange("p (t d h) -> p t d h", d=2, h=H)
                        for b, pair in enumerate(((LE, GE), (GT, LT))):
                            for d, mk in enumerate(pair):
                                pe.matmul(PS[:, 2 * u, b * 256 + d * 96:b * 256 + d * 96 + 96].rearrange(
                                    "p (t h) -> p t h", h=H), masks[:, mk, :], dav[:, :, d, :], start=True, stop=True)
                        m = pe.matmul(PS[:, 2 * u + 1, 0:DTN], ones[:], dts[:, DA, :], start=True, stop=True)
                    elif kind == "xT":
                        pe.wait_ge(*W("conv_done", i + 1))
                        for t in range(NT):
                            src = acc5[:, i % 3, c5(t):c5(t) + P] if i < 8 else bct[:, i - 8, c5(t):c5(t) + P]
                            m = tr(PS[:, 2 * u + t // 4, (t % 4) * P:(t % 4 + 1) * P], src, P)
                    elif kind == "mean":
                        pe.wait_ge(*W("conf_done", KD))
                        for s in segs(main):
                            f = c31(0 if s == 0 else NCT)
                            for k in range(KD):
                                m = pe.matmul(seg_banks(u, s), masks[:, AVG, :], vT[:, k, f:f + SEG[s][1]],
                                              start=k == 0, stop=k == KD - 1)
                    m.then_inc(S("pe_job"), 1)
                pe.wait_ge(*W("act_job", len(jobs)))
                for k in range(KD):
                    pe.wait_ge(*W("sq_ready", k + 1))
                    for s in segs(main):
                        f = c31(0 if s == 0 else NCT)
                        m = pe.matmul(seg_banks(0, s), masks[:, AVG, :], sqb[:, k % 2, f:f + SEG[s][1]],
                                      start=k == 0, stop=k == KD - 1)
                    m.then_inc(S("sq_used"), 1)
                pe.wait_ge(*W("var_taken", 1))
                pe.wait_ge(*W("conv_done", 2 * KD))
                todo = [(ch, g) for ch in main for g in range(G)]

                def outputs(q):
                    ch, g = todo[q]
                    pe.wait_ge(*W("m_ready", q + 1))
                    if q:
                        pe.wait_ge(*W("yd_taken", q))
                    for r in range(R):
                        pr = g * 256 + (r // 2) * P
                        m = pe.matmul(PS[:, 3, r * P:(r + 1) * P], GB[:, q % 2, r * P:(r + 1) * P],
                                      xtok[:, ch, pr:pr + P], start=True, stop=True)
                    m.then_inc(S("yd_ready"), 1)

                done = {"read": 0, "upd": 0}

                def state_step(d, n, ch):
                    if (d, n, ch) in reads(main):
                        pe.wait_ge(*W("h_ready", done["upd"]))
                        if done["read"]:
                            pe.wait_ge(*W("o_taken", done["read"]))
                        for g in range(G):
                            m = pe.matmul(PS[:, 4 + g // 2, (g % 2) * 256:(g % 2 + 1) * 256],
                                          bct[:, G + g, c5(ch):c5(ch) + P], hst[:, d, g * 256:(g + 1) * 256],
                                          start=True, stop=True)
                        m.then_inc(S("o_ready"), 1)
                        done["read"] += 1
                    if (d, n, ch) in UPDATES:
                        pe.wait_ge(*W("xw_ready", done["upd"] + 1))
                        if done["upd"]:
                            pe.wait_ge(*W("h_ready", done["upd"]))
                        for g in range(G):
                            m = pe.matmul(PS[:, 6 + g // 2, (g % 2) * 256:(g % 2 + 1) * 256],
                                          btok[:, ch, g * NS:(g + 1) * NS], xw[:, g * 256:(g + 1) * 256],
                                          start=True, stop=True)
                        m.then_inc(S("st_ready"), 1)
                        done["upd"] += 1

                def scores(q):
                    ch, g = todo[q]
                    pe.wait_ge(*W("dam_ready", q + 1))
                    if q:
                        pe.wait_ge(*W("e_ready", q))
                    pe.matmul(PS[:, 0, :], masks[:, GT, :], dAm[:, q % 2, 0, :], start=True, stop=False)
                    pe.matmul(PS[:, 0, :], masks[:, LT, :], dAm[:, q % 2, 1, :], start=False, stop=True).then_inc(
                        S("arg_ready"), 1)
                    if q >= 2:
                        pe.wait_ge(*W("sul_ready", 2 * q - 2))
                    pe.matmul(PS[:, 1 + q % 2, 0:P], bct[:, g, c5(ch):c5(ch) + P], bct[:, G + g, c5(ch):c5(ch) + P],
                              start=True, stop=True).then_inc(S("s_ready"), 1)

                scores(0)
                for q in range(len(todo)):
                    if q + 1 < len(todo):
                        scores(q + 1)
                    if q:
                        outputs(q - 1)
                    for s in steps_at(main, q):
                        state_step(*s)
                outputs(len(todo) - 1)
                q = len(todo)
                pe.wait_ge(*W("yd_taken", q))
                pe.wait_ge(*W("o_taken", done["read"]))
                pe.wait_ge(*W("h_ready", done["upd"]))
                for n, t in enumerate(main):
                    pe.wait_ge(*W("yn_ready", n + 1))
                    if n >= 4:
                        pe.wait_ge(*W("yT_ready", n - 3))
                        pe.wait_ge(*W("yT_dve", n - 3))
                    for k in range(KD):
                        m = tr(PS[:, 2 * (n % 4) + k // 4, (k % 4) * P:(k % 4 + 1) * P], Y[:, t, k * P:(k + 1) * P], P)
                    m.then_inc(S("ynT_done"), 1)
                pe.wait_ge(*W("yT_ready", len(main)))
                pe.wait_ge(*W("yT_dve", len(main)))
                pe.wait_ge(*W("v_ready", KD))
                def router_rows(n):
                    b = 4 * ((n // 2) % 2)
                    pe.wait_ge(*W("m_taken", n // 2 * 2 + 2))
                    pe.wait_ge(*W("xn2_ready", n + 1))
                    if n % 2:
                        pe.wait_ge(*W("u2_ready", n))
                    for k in range(KD):
                        m = tr(PS[:, b + k // 4, (k % 4) * P:(k % 4 + 1) * P], xn2[:, n, k * P:(k + 1) * P], P)
                    m.then_inc(S("u2T_done"), 1)

                def router_logits(n):
                    pe.wait_ge(*W("u2_ready", n + 1))
                    if n == 0:
                        pe.wait_ge(*W("rw_in", 16))
                    for k in range(KD):
                        m = pe.matmul(logits(n), u2T[:, k, :], rw[:, k, :], start=k == 0, stop=k == KD - 1)
                    m.then_inc(S("logit_ready"), 1)

                n = len(slots)
                for pi, pair in enumerate(pairs(main)):
                    if pi >= 2:
                        pe.wait_ge(*W("lexp_ready", 2 * (pi - 1)))
                    for q in range(KD):
                        wv = weights(n)
                        for b in range(2):
                            k = 2 * q + b
                            for ti, t in enumerate(pair):
                                lhs = yT[:, k, t * P:(t + 1) * P] if k < KD else vT[:, k - KD, c31(t):c31(t) + P]
                                for h in range(2):
                                    m = pe.matmul(PS[:, 4 * (pi % 2) + 2 * ti + h, :], lhs,
                                                  wv[:, b * D + h * 512:b * D + (h + 1) * 512],
                                                  start=k == 0, stop=k == 2 * KD - 1)
                        m.then_inc(S("wo_used"), 1)
                        n += 1
                        if pi and q == 4:
                            router_rows(2 * pi - 2)
                        if pi and q == 5:
                            router_logits(2 * pi - 2)
                            router_rows(2 * pi - 1)
                        if pi and q == 6:
                            router_logits(2 * pi - 1)
                for t in range(len(main) - 2, len(main)):
                    router_rows(t)
                    router_logits(t)
                pe.wait_ge(*W("aff_ready", len(main)))
                for n, t in enumerate(main):
                    dst = PS[0:NE, 4, t * P:(t + 1) * P] if t < NCT else PS[0:NE, 5, (t - NCT) * P:(t - NCT + 1) * P]
                    m = tr(dst, aff[:, n, :], P)
                m.then_inc(S("affT_done"), 1)
                pe.wait_ge(*W("gi_ready", 1))
                for b in range(2):
                    m = tr(PS[0:slot_n, 6, b * NE:(b + 1) * NE], gi[:, b, 0:slot_n], NE)
                m.then_inc(S("giT_done"), 1)

                def sel_transposes():
                    for k in range(KD):
                        m = tr(PS[:, k // 4, (k % 4) * P:(k % 4) * P + slot_n], sel[0:slot_n, k * P:(k + 1) * P], slot_n)
                    m.then_inc(S("selT_done"), 1)

                def product(u, dst, hi, lo, widths, start, stop):
                    slot, _ = slot_turn(u)
                    pe.wait_ge(*W("lo_made", number(u) + 1))
                    for b, (f, w) in enumerate(widths):
                        for n, (x_, w_) in enumerate(((hi, whi), (lo, whi), (hi, wlo))):
                            m = pe.matmul(dst(b, w), x_, w_[:, slot, f:f + w], start=start and n == 0, stop=stop and n == 2)
                    m.then_inc(S("unit_used"), 1)

                def gate_up(e):
                    pe.wait_ge(*W("selT_dve", e + 1))
                    for k in range(KD):
                        for mi in range(2):
                            product(gu(e, 2 * k + mi), lambda b, w: PS[0:slot_n, 3 * mi + b, 0:w], shi[:, k, 0:slot_n],
                                    slo[:, k, 0:slot_n], FB, k == 0, k == KD - 1)

                def down(par, e, lo, hi):
                    for j in range(lo, hi):
                        product(dn(e, j), lambda b, w: PS[0:slot_n, 6 + b, 0:w], hhi[:, par, j, 0:slot_n],
                                hlo[:, par, j, 0:slot_n], [(0, 512), (512, 512)], j == 0, j == JF - 1)

                def h_transposes():
                    hv = hh[0:slot_n, :].rearrange("s (p j) -> s p j", j=JF)
                    for j in range(JF):
                        m = tr(PS[:, 2 + j // 4, (j % 4) * P:(j % 4) * P + slot_n], hv[:, :, j], slot_n)
                    m.then_inc(S("hT_done"), 1)

                def expert(par, e, first=False, last=False):
                    if not first:
                        pe.wait_ge(*W("hT_dve", e))
                    gate_up(e)
                    if not first:
                        pe.wait_ge(*W("dn_free", e))
                        down(1 - par, e - 1, 0, 6)
                    pe.wait_ge(*W("h_rows", 3 * e + 3))
                    if not last:
                        pe.wait_ge(*W("sel_in", 16 * e + 32))
                    if not first:
                        down(1 - par, e - 1, 6, 7)
                    if not last:
                        sel_transposes()
                    h_transposes()
                    if not first:
                        down(1 - par, e - 1, 7, JF)

                pe.wait_ge(*W("affT_taken", 1))
                pe.wait_ge(*W("sel_in", 16))
                sel_transposes()
                expert(0, 0, first=True)
                with pe.Fori(1, NE - 3, 2) as e:
                    expert(1, e)
                    expert(0, e + 1)
                for e in range(NE - 3, NE):
                    expert(e % 2, e, last=e == NE - 1)
                pe.wait_ge(*W("hT_dve", NE))
                pe.wait_ge(*W("dn_free", NE))
                down(1, NE - 1, 0, JF)

        @block.scalar
        def _(act):
            def take_params(L):
                W = counter(L)
                act.wait_ge(*W("par_T", 1))
                act.copy(par[:, 0:P * 3 + 72], PS[:, 0, 0:P * 3 + 72]).then_inc(sem("par_taken"), 1)
                act.wait_ge(*W("par_taken", 1))
                if L == 0:
                    act.wait_ge(sem("cstat_zero"), 1)
                    act.activation(cstat[:, :, 0:33:32].rearrange("p k s -> p s k"),
                                   par[:, COL["c"]:COL["c"] + 16].rearrange("p (s k) -> p s k", s=2),
                                   ACT.Silu).then_inc(sem("cstat_ready"), 1)
                    act.wait_ge(sem("eps_set"), 1)

            take_params(0)
            for L, main, jobs, slots in LAYERS:
                S, W = sem, counter(L)
                slot_n = CL + (CC if main[0] == 0 else 0)
                v0, vw = seg_cols(main, g31)

                def rms(src, junk_, col, stage, n):
                    act.activation(junk_, src, ACT.Square, accum_out=ss[:, col:col + 1]).then_inc(S(f"{stage}_sq"), 1)
                    act.wait_ge(*W(f"{stage}_sq", n + 1))
                    act.activation(ss[:, col + 1:col + 2], ss[:, col:col + 1], ACT.Sqrt, bias=eps[:, 0:1],
                                   scale=1.0 / D).then_inc(S(f"{stage}_rms"), 1)

                def silu5(j):
                    act.wait_ge(*W("taps_done", j + 1))
                    dst = acc5[:, j % 3, :] if j < 8 else bct[:, j - 8, :]
                    act.activation(dst, acc5[:, j % 3, :], ACT.Silu,
                                   bias=par[:, COL["conv_b"] + j:COL["conv_b"] + j + 1]).then_inc(S("conv_done"), 1)

                rows_in = xt if L == 0 else xr
                if L == 0:
                    act.wait_ge(sem("x_in"), 16 * NT)
                for t in range(NT):
                    if L:
                        act.wait_ge(*counter(L - 1)("xf_ready", t + 1))
                    if t:
                        act.wait_ge(*W("x_sq", t))
                    act.activation(junk[:], rows_in[:, t, :], ACT.Square, accum_out=ss[:, t:t + 1]).then_inc(S("x_sq"), 1)
                act.wait_ge(*W("x_sq", NT))
                act.activation(ss[:, 8:8 + NT], ss[:, 0:NT], ACT.Sqrt, bias=eps[:, 0:1], scale=1.0 / D).then_inc(
                    S("x_rms"), 1)
                act.wait_ge(*W("x_rstd", 1))
                for t in range(NT):
                    act.mul(xt[:, t, :], rows_in[:, t, :], rstd[:, t:t + 1]).then_inc(S("xn_ready"), 1)
                for n, (kind, i) in enumerate(jobs):
                    u = n % 4
                    if kind == "norm" and i == 0:
                        act.wait_ge(*W("mod_ready", 1))
                    if kind == "g" and i:
                        act.wait_ge(*W("v_made", i))
                    if kind == "ada" and i >= 2:
                        if i - 2 in GATES:
                            act.wait_ge(*W("gp_ready", 2))
                        else:
                            act.wait_ge(*W("pe_job", jobs.index(("adaT", i - 2)) + 1))
                    if kind == "xbc" and i >= 2:
                        act.wait_ge(*W("taps_done", i - 1))
                    if kind == "xbc" and i == 0:
                        act.wait_ge(*W("pads_ready", 1))
                    if kind == "z" and i == main[0]:
                        act.wait_ge(*W("gp_out", 4 * 16))
                    if kind == "mean":
                        for b in range(2):
                            act.wait_ge(*W(f"sz_out{b}", 16 * len(main) // 2))
                    act.wait_ge(*W("pe_job", n + 1))
                    if kind == "ada":
                        ins = act.copy(arow[:, i % 2, :], unit2(u, 33))
                    elif kind == "adaT":
                        ins = act.copy(modc[:, i, :, :], PS[:, 2 * u, 0:KD * 33].rearrange(
                            "p (k s) -> p s k", s=33)[:, 0:33:32, :])
                    elif kind == "norm":
                        st = 0 if i >= NCT else 1
                        for k in range(KD):
                            ins = act.activation(uT[:, k, i * P:(i + 1) * P],
                                                 PS[:, 2 * u + k // 4, (k % 4) * P:(k % 4 + 1) * P],
                                                 ACT.Identity, bias=modc[:, 0, st, k:k + 1], scale=scl[:, 0, st, k:k + 1])
                    elif kind in ("g", "a"):
                        for s in segs(main):
                            dst = (sg if kind == "g" else asb)[:, SEG[s][0]:SEG[s][0] + SEG[s][1]]
                            ins = act.activation(dst, seg_banks(u, s), ACT.Sigmoid if kind == "g" else ACT.Copy)
                    elif kind == "dt":
                        for s in (0, 1):
                            ins = act.copy(dtT[:, SEG[s][0]:SEG[s][0] + SEG[s][1]], PS[0:32, 2 * u + s, 0:SEG[s][1]])
                    elif kind == "z":
                        zi = main.index(i)
                        if zi >= 2:
                            act.wait_ge(*W(f"sz_out{zi % 2}", 16 * (zi // 2)))
                        ins = act.activation(szt[:, zi % 2, :], unit2(u), ACT.Silu)
                    elif kind == "dtT":
                        ins = act.copy(dts[:, D1, :], PS[:, 2 * u, 0:DTN])
                    elif kind == "cum":
                        for b, dst in ((0, EC), (1, ER)):
                            act.activation(dts[:, dst, :], PS[:, 2 * u, b * 256:b * 256 + DTN], ACT.Exp)
                        ins = act.activation(dts[:, ET, :], PS[:, 2 * u + 1, 0:DTN], ACT.Exp)
                    elif kind == "xbc":
                        for s in (0, 1):
                            f = g5 + c5(0 if s == 0 else NCT)
                            ins = act.copy(pre5[:, i % 2, f:f + SEG[s][1]], seg_banks(u, s))
                    elif kind == "xT":
                        dst = xtok[:, :, i * P:(i + 1) * P] if i < 8 else btok[:, :, (i - 8) * P:(i - 7) * P]
                        act.copy(dst[:, 0:4, :], PS[:, 2 * u, :].rearrange("p (t n) -> p t n", n=P))
                        ins = act.copy(dst[:, 4:6, :], PS[:, 2 * u + 1, 0:256].rearrange("p (t n) -> p t n", n=P))
                    elif kind == "mean":
                        for s in segs(main):
                            f = c31(0 if s == 0 else NCT)
                            ins = act.copy(mean[:, f:f + SEG[s][1]], seg_banks(u, s))
                    ins.then_inc(S("act_job"), 1)
                    if kind == "z":
                        act.wait_ge(*W("act_job", n + 1))
                        act.dma_start(sz_d[i * P:(i + 1) * P, :], szt[:, zi % 2, :]).then_inc(S(f"sz_out{zi % 2}"), 16)
                    if kind == "dtT":
                        act.wait_ge(*W("sp_abs", 1))
                        act.activation(dts[:, D3, :], dts[:, D2, :], ACT.Exp, scale=-1.0).then_inc(S("sp_exp"), 1)
                        act.wait_ge(*W("sp_one", 1))
                        act.activation(dts[:, EC, :], dts[:, D2, :], ACT.Ln).then_inc(S("sp_ln"), 1)
                        act.activation(hdrow[:, 3, :], hdrow[:, 1, :], ACT.Exp).then_inc(S("a_exp"), 1)
                    if kind == "xbc" and i >= 1:
                        silu5(i - 1)
                        if i == 15:
                            silu5(15)
                for k in range(KD):
                    act.wait_ge(*W("vc_ready", k + 1))
                    if k >= 2:
                        act.wait_ge(*W("sq_used", k - 1))
                    act.activation(sqb[:, k % 2, v0:v0 + vw], vT[:, k, v0:v0 + vw], ACT.Square).then_inc(S("sq_ready"), 1)
                act.wait_ge(*W("sq_used", KD))
                for s in segs(main):
                    f = c31(0 if s == 0 else NCT)
                    ins = act.activation(rs[:, f:f + SEG[s][1]], seg_banks(0, s), ACT.Sqrt, bias=eps[:, 0:1])
                ins.then_inc(S("var_taken"), 1)
                for k in range(KD):
                    act.wait_ge(*W("vn_ready", k + 1))
                    act.activation(vT[:, k, v0:v0 + vw], vT[:, k, v0:v0 + vw], ACT.Silu,
                                   bias=par[:, COL["ln_b"] + k:COL["ln_b"] + k + 1],
                                   scale=par[:, COL["ln_g"] + k:COL["ln_g"] + k + 1]).then_inc(S("v_ready"), 1)
                for q, (ch, g) in enumerate((ch, g) for ch in main for g in range(G)):
                    act.wait_ge(*W("arg_ready", q + 1))
                    if q >= 2:
                        act.wait_ge(*W("m_ready", q - 1))
                    act.activation(E[:, q % 2, :], PS[:, 0, :], ACT.Exp).then_inc(S("e_ready"), 1)
                    act.wait_ge(*W("sul_ready", 2 * q + 2))
                    for r in range(R):
                        f = ch * 32 + H + g * R + r
                        ins = act.mul(GA[:, q % 2, r * P:(r + 1) * P], SUL[:, q % 2, 1, :], dts[:, DTV, f:f + 1])
                    ins.then_inc(S("ga_ready"), 1)

                def take_yT(n):
                    act.wait_ge(*W("ynT_done", n + 1))
                    for k in range(KD // 2):
                        ins = act.mul(yT[:, k, main[n] * P:(main[n] + 1) * P],
                                      PS[:, 2 * (n % 4) + k // 4, (k % 4) * P:(k % 4 + 1) * P],
                                      par[:, COL["norm_g"] + k:COL["norm_g"] + k + 1])
                    ins.then_inc(S("yT_ready"), 1)

                for n, t in enumerate(main):
                    act.wait_ge(*W("yz_ready", n + 1))
                    if n:
                        act.wait_ge(*W("y_rstd", n))
                    rms(Y[:, t, :], otmp[:], 0, "y", n)
                    act.wait_ge(*W("y_rstd", n + 1))
                    act.mul(Y[:, t, :], Y[:, t, :], rstd[:, n:n + 1]).then_inc(S("yn_ready"), 1)
                    if n:
                        take_yT(n - 1)
                take_yT(len(main) - 1)

                def take_u2(n):
                    act.wait_ge(*W("u2T_done", n + 1))
                    if n:
                        act.wait_ge(*W("logit_ready", n))
                    st = 0 if main[n] >= NCT else 1
                    for k in range(KD):
                        ins = act.activation(u2T[:, k, :], PS[:, 4 * ((n // 2) % 2) + k // 4, (k % 4) * P:(k % 4 + 1) * P], ACT.Identity,
                                             bias=modc[:, 3, st, k:k + 1], scale=scl[:, 1, st, k:k + 1])
                    ins.then_inc(S("u2_ready"), 1)

                for n, t in enumerate(main):
                    act.wait_ge(*W("wo_used", (n // 2 + 1) * KD))
                    b = 4 * ((n // 2) % 2) + 2 * (n % 2)
                    if n:
                        act.wait_ge(*W("x1_rstd", n))
                    rms(PS[:, b:b + 2, :].rearrange("p b n -> p (b n)"), xn2[:, n, :], 0, "m", n)
                    act.wait_ge(*W("x1_ready", n + 1))
                    rms(xres[:, n % 2, :], xn2[:, n, :], 2, "x1", n)
                    act.wait_ge(*W("x1_rstd", n + 1))
                    act.mul(xn2[:, n, :], xres[:, n % 2, :], rstd[:, 1:2]).then_inc(S("xn2_ready"), 1)
                    for r in (n - 1, n) if n % 2 else ():
                        take_u2(r)
                    for r in (n - 1, n) if n % 2 else ():
                        act.wait_ge(*W("lmax_ready", r + 1))
                        act.activation(aff[:, r, :], logits(r), ACT.Exp, bias=sm[:, 0, r:r + 1],
                                       accum_out=sm[:, 1, r:r + 1]).then_inc(S("lexp_ready"), 1)
                def high(u, width):
                    slot, turn = slot_turn(u)
                    act.wait_ge(*W(f"unit_in{slot}", 16 * turn + 16))
                    if not isinstance(turn, int) or turn:
                        act.wait_ge(*W("unit_used", number(u) - RING + 1))
                    act.copy(whi[:, slot, 0:width], wr[:, slot, 0:width]).then_inc(S("hi_made"), 1)

                def take_sel(e):
                    act.wait_ge(*W("selT_done", e + 1))
                    for st, (lo, hi) in enumerate(((0, CL), (CL, slot_n))):
                        for k in range(KD // 2) if hi > lo else ():
                            ins = act.activation(selF[:, k, lo:hi], PS[:, k // 4, (k % 4) * P + lo:(k % 4) * P + hi],
                                                 ACT.Identity, bias=modc[:, 3, st, k:k + 1], scale=scl[:, 1, st, k:k + 1])
                    ins.then_inc(S("selF_act"), 1)
                    act.wait_ge(*W("selF_act", e + 1))
                    act.copy(shi[:, 0:KD // 2, 0:slot_n], selF[:, 0:KD // 2, 0:slot_n]).then_inc(S("selT_act"), 1)

                def down_out(par, e):
                    act.wait_ge(*W("unit_used", number(dn(e, JF - 1)) + 1))
                    act.wait_ge(*W("gate_cur", e + 1))
                    act.wait_ge(*W("scattered", 16 * e + 16))
                    act.mul(ob[0:slot_n, par, :], PS[0:slot_n, 6:8, :].rearrange("p b n -> p (b n)"),
                            gcur[0:slot_n, par:par + 1]).then_inc(S("dn_free"), 1)

                def expert(par, e, first=False, last=False):
                    for i in range(AHEAD, GU):
                        high(gu(e, i), FE)
                    for j in range(7) if not first else ():
                        high(dn(e - 1, j), D)
                    for b, (f, w) in enumerate(FB):
                        if b == 0:
                            act.wait_ge(*W("unit_used", number(gu(e, GU - 1)) + 1))
                        if b or not first:
                            act.wait_ge(*W("h_rows", 3 * e + b))
                        act.activation(hs[0:slot_n, 0:w], PS[0:slot_n, b, 0:w], ACT.Silu).then_inc(S("hs_ready"), 1)
                        if not first:
                            high(dn(e - 1, 7 + b), D)
                    if not first:
                        high(dn(e - 1, JF - 1), D)
                    for i in range(AHEAD) if not last else ():
                        high(gu(e + 1, i), FE)
                    if not last:
                        take_sel(e + 1)
                    act.wait_ge(*W("hT_done", e + 1))
                    for j, n in ((0, 4), (4, 4), (8, 3)):
                        ins = act.copy(hhi[:, par, j:j + n, 0:slot_n],
                                       PS[:, 2 + j // 4, 0:n * P].rearrange("p (j s) -> p j s", s=P)[:, :, 0:slot_n])
                    ins.then_inc(S("hT_act"), 1)
                    if not first:
                        down_out(1 - par, e - 1)

                act.wait_ge(*W("affT_taken", 1))
                for i in range(AHEAD):
                    high(gu(0, i), FE)
                take_sel(0)
                expert(0, 0, first=True)
                with act.Fori(1, NE - 3, 2) as e:
                    expert(1, e)
                    expert(0, e + 1)
                for e in range(NE - 3, NE):
                    expert(e % 2, e, last=e == NE - 1)
                for j in range(JF):
                    high(dn(NE - 1, j), D)
                down_out(1, NE - 1)
                if L < DEPTH - 1:
                    take_params(L + 1)
                act.wait_ge(*W("yt_in", 16))
                for n, t in enumerate(main):
                    if n:
                        act.wait_ge(*W("f_sq", n))
                    act.activation(junk[:], yt[:, t, :], ACT.Square, accum_out=ss[:, t:t + 1]).then_inc(S("f_sq"), 1)
                act.wait_ge(*W("f_sq", len(main)))
                act.activation(ss[:, 8:8 + NT], ss[:, 0:NT], ACT.Sqrt, bias=eps[:, 0:1], scale=1.0 / D).then_inc(
                    S("f_rms"), 1)

        @block.vector
        def _(dve):
            chained = [0]

            def chain(ins):
                chained[0] += 1
                ins.then_inc(sem("dve_chain"), 1)
                dve.wait_ge(sem("dve_chain"), chained[0])

            def seen(ins, at_name, n):
                ins.then_inc(sem(at_name), 1)
                dve.wait_ge(*counter(L)(at_name, n))

            dve.memset(eps[:, 0:1], EPS).then_inc(sem("eps_set"), 1)
            dve.memset(cstat[:], 0.0).then_inc(sem("cstat_zero"), 1)
            for L, main, jobs, slots in LAYERS:
                S, W = sem, counter(L)
                slot_n = CL + (CC if main[0] == 0 else 0)
                v0, vw = seg_cols(main, g31)
                TT, TS, STT = dve.tensor_tensor, dve.tensor_scalar, dve.scalar_tensor_tensor

                def inv(dst, src):
                    return dve.reciprocal(dst, src)

                dve.wait_ge(*W("x_rms", 1))
                inv(rstd[:, 0:NT], ss[:, 8:8 + NT]).then_inc(S("x_rstd"), 1)
                dtr = lambda i: dts[:, i, :].rearrange("p (t h) -> p t h", t=NT)
                over_t = lambda i: hdrow[:, i, :].unsqueeze(1).to_broadcast([P, NT, 2 * H])

                def dt_quantities():
                    dve.wait_ge(*W("act_job", jobs.index(("dtT", 0)) + 1))
                    chain(TT(dtr(D1), dtr(D1), over_t(0), ALU.add))
                    STT(dts[:, D2, :], dts[:, D1, :], -1.0, dts[:, D1, :], ALU.mult, ALU.max).then_inc(S("sp_abs"), 1)
                    chain(TS(dts[:, D1, :], dts[:, D1, :], 0.0, None, ALU.max))
                    dve.wait_ge(*W("sp_exp", 1))
                    TS(dts[:, D2, :], dts[:, D3, :], 1.0, None, ALU.add).then_inc(S("sp_one"), 1)
                    dve.wait_ge(*W("sp_one", 1))
                    chain(TS(dts[:, WDT, :], dts[:, D2, :], 1.0, 1e-30, ALU.subtract, ALU.max))
                    chain(inv(dts[:, WDT, :], dts[:, WDT, :]))
                    chain(STT(dts[:, DTV, :], dts[:, D2, :], 1.0, dts[:, D3, :], ALU.is_le, ALU.mult))
                    chain(TT(dts[:, DTV, :], dts[:, DTV, :], dts[:, D1, :], ALU.add))
                    chain(TT(dts[:, WDT, :], dts[:, WDT, :], dts[:, D3, :], ALU.mult))
                    dve.wait_ge(*W("sp_ln", 1))
                    chain(TT(dts[:, WDT, :], dts[:, WDT, :], dts[:, EC, :], ALU.mult))
                    chain(TT(dts[:, DTV, :], dts[:, DTV, :], dts[:, WDT, :], ALU.add))
                    dve.wait_ge(*W("a_exp", 1))
                    chain(TT(dtr(DA), dtr(DTV), over_t(3), ALU.mult))
                    TS(dts[:, DA, :], dts[:, DA, :], -1.0, None, ALU.mult).then_inc(S("da_ready"), 1)

                first_col = par[:, COL["dw_w"]:COL["dw_w"] + K31 * KD]
                for j in range(KD):
                    if j == (KD - 1 if main[0] == 0 else KD - 2):
                        dt_quantities()
                    dve.wait_ge(*W("v_made", j + 1))
                    tap = lambda k: first_col[:, k * KD + j:k * KD + j + 1]
                    a = cacc[:, j % 2, v0:v0 + vw]
                    chain(TS(a, vT[:, j, v0 + 1:v0 + 1 + vw], tap(1), par[:, COL["dw_b"] + j:COL["dw_b"] + j + 1],
                             ALU.mult, ALU.add))
                    for k in range(2, K31):
                        chain(STT(a, vT[:, j, v0 + k:v0 + k + vw], tap(k), a, ALU.mult, ALU.add))
                    STT(vT[:, j, v0:v0 + vw], vT[:, j, v0:v0 + vw], tap(0), a, ALU.mult, ALU.add).then_inc(S("conf_done"), 1)
                for j in range(2 * KD):
                    dve.wait_ge(*W("act_job", jobs.index(("xbc", j)) + 1))
                    if j >= 3:
                        if j - 3 < 8:
                            dve.wait_ge(*W("pe_job", jobs.index(("xT", j - 3)) + 1))
                        else:
                            dve.wait_ge(*W("conv_done", j - 2))
                    tap = lambda k: par[:, COL["conv_w"] + k * 16 + j:COL["conv_w"] + k * 16 + j + 1]
                    a = acc5[:, j % 3, :]
                    chain(TS(a, pre5[:, j % 2, 0:W5], tap(0), None, ALU.mult))
                    for k in range(1, K5):
                        ins = STT(a, pre5[:, j % 2, k:k + W5], tap(k), a, ALU.mult, ALU.add)
                        if k < K5 - 1:
                            chain(ins)
                    ins.then_inc(S("taps_done"), 1)
                dve.wait_ge(*W("act_job", jobs.index(("cum", 0)) + 1))
                for d in range(2):
                    ins = TT(dtr(WDT)[:, :, d * H:(d + 1) * H], dtr(DTV)[:, :, d * H:(d + 1) * H],
                             dts[:, ER, d * 96:(d + 1) * 96].rearrange("p (t h) -> p t h", h=H), ALU.mult)
                ins.then_inc(S("wdt_ready"), 1)
                dve.wait_ge(*W("act_job", len(jobs)))
                for k in range(KD):
                    for s in segs(main):
                        f = c31(0 if s == 0 else NCT)
                        ins = TT(vT[:, k, f:f + SEG[s][1]], vT[:, k, f:f + SEG[s][1]], mean[:, f:f + SEG[s][1]], ALU.subtract)
                    ins.then_inc(S("vc_ready"), 1)
                dve.wait_ge(*W("var_taken", 1))
                for s in segs(main):
                    f = c31(0 if s == 0 else NCT)
                    chain(inv(rs[:, f:f + SEG[s][1]], rs[:, f:f + SEG[s][1]]))
                for k in range(KD):
                    for s in segs(main):
                        f = c31(0 if s == 0 else NCT)
                        ins = TT(vT[:, k, f:f + SEG[s][1]], vT[:, k, f:f + SEG[s][1]], rs[:, f:f + SEG[s][1]], ALU.mult)
                    ins.then_inc(S("vn_ready"), 1)
                dve.wait_ge(*W("y_init", len(main)))
                todo = [(ch, g) for ch in main for g in range(G)]

                def add_outputs(q):
                    ch, g = todo[q]
                    dve.wait_ge(*W("yd_ready", q + 1))
                    yv = Y[:, ch, g * 256:(g + 1) * 256].rearrange("p (a b n) -> p a b n", a=2, b=2)
                    pv = PS[:, 3, :].rearrange("p (a c n) -> p a c n", a=2, n=HD)[:, :, 0:4:3, :]
                    return TT(yv, yv, pv, ALU.add).then_inc(S("yd_taken"), 1)

                done = {"read": 0, "upd": 0}

                def state_step(d, n, ch):
                    per_head = lambda buf, f: dts[:, buf, f:f + H].unsqueeze(2).to_broadcast([P, H, HD])
                    ov = otmp[:].rearrange("p (h n) -> p h n", h=H)
                    if (d, n, ch) in reads(main):
                        dve.wait_ge(*W("o_ready", done["read"] + 1))
                        seen(TT(ov, PS[:, 4:6, :].rearrange("p b (h n) -> p (b h) n", n=HD), per_head(EC, d * 96 + ch * H),
                                ALU.mult), "o_taken", done["read"] + 1)
                        done["read"] += 1
                        chain(TT(Y[:, ch, :], Y[:, ch, :], otmp[:], ALU.add))
                    if (d, n, ch) in UPDATES:
                        if n:
                            hv = hst[:, d, :].rearrange("p (h n) -> p h n", h=H)
                            chain(TT(hv, hv, per_head(ET, ch * 32 + d * H), ALU.mult))
                        dve.wait_ge(*W("st_ready", done["upd"] + 1))
                        new = PS[:, 6:8, :].rearrange("p b n -> p (b n)")
                        if n:
                            ins = TT(hst[:, d, :], hst[:, d, :], new, ALU.add)
                        else:
                            ins = dve.tensor_copy(hst[:, d, :], new)
                        done["upd"] += 1
                        seen(ins, "h_ready", done["upd"])

                def mask_scores(q):
                    dve.wait_ge(*W("s_ready", q + 1))
                    if q >= 2:
                        dve.wait_ge(*W("ga_ready", q - 1))
                    for b, mk in enumerate((LE, GE)):
                        TT(SUL[:, q % 2, b, :], PS[:, 1 + q % 2, 0:P], masks[:, mk, :], ALU.mult).then_inc(
                            S("sul_ready"), 1)

                mask_scores(0)
                for q, (ch, g) in enumerate(todo):
                    if q + 1 < len(todo):
                        mask_scores(q + 1)
                    dve.wait_ge(*W("ga_ready", q + 1))
                    if q >= 2:
                        dve.wait_ge(*W("yd_ready", q - 1))
                    for r in range(R):
                        f = ch * 32 + g * R + r
                        ins = STT(GB[:, q % 2, r * P:(r + 1) * P], SUL[:, q % 2, 0, :], dts[:, DTV, f:f + 1],
                                  GA[:, q % 2, r * P:(r + 1) * P], ALU.mult, ALU.add)
                    chain(ins)
                    dve.wait_ge(*W("e_ready", q + 1))
                    TT(GB[:, q % 2, :], GB[:, q % 2, :], E[:, q % 2, :], ALU.mult).then_inc(S("m_ready"), 1)
                    if q:
                        add_outputs(q - 1)
                    for s in steps_at(main, q):
                        if q:
                            dve.wait_ge(*W("yd_taken", q))
                        state_step(*s)
                add_outputs(len(todo) - 1)
                dve.wait_ge(*W("yd_taken", len(todo)))
                def take_yT(n):
                    dve.wait_ge(*W("ynT_done", n + 1))
                    for k in range(KD // 2, KD):
                        ins = TS(yT[:, k, main[n] * P:(main[n] + 1) * P],
                                 PS[:, 2 * (n % 4) + k // 4, (k % 4) * P:(k % 4 + 1) * P],
                                 par[:, COL["norm_g"] + k:COL["norm_g"] + k + 1], None, ALU.mult)
                    ins.then_inc(S("yT_dve"), 1)

                for n, t in enumerate(main):
                    dve.wait_ge(*W(f"szl_in{n % 2}", 16 * (n // 2 + 1)))
                    TT(Y[:, t, :], Y[:, t, :], szl[:, n % 2, :], ALU.mult).then_inc(S("yz_ready"), 1)
                    dve.wait_ge(*W("y_rms", n + 1))
                    inv(rstd[:, n:n + 1], ss[:, 1:2]).then_inc(S("y_rstd"), 1)
                    if n:
                        take_yT(n - 1)
                take_yT(len(main) - 1)
                for n, t in enumerate(main):
                    st = 0 if t >= NCT else 1
                    b = 4 * ((n // 2) % 2) + 2 * (n % 2)
                    dve.wait_ge(*W("m_rms", n + 1))
                    chain(inv(rstd[:, 0:1], ss[:, 1:2]))
                    if n == 0:
                        dve.wait_ge(*W("gpb_in", 32))
                    xr_ = xres[:, n % 2, :]
                    seen(STT(xn2[:, n, :], PS[:, b:b + 2, :].rearrange("p b n -> p (b n)"), rstd[:, 0:1], gpb[:, st, :],
                             ALU.mult, ALU.mult), "m_taken", n + 1)
                    dve.wait_ge(*W(f"xres_in{n % 2}", 16 * (n // 2 + 1)))
                    TT(xr_, xr_, xn2[:, n, :], ALU.add).then_inc(S("x1_ready"), 1)
                    dve.wait_ge(*W("x1_rms", n + 1))
                    inv(rstd[:, 1:2], ss[:, 3:4]).then_inc(S("x1_rstd"), 1)
                    for r in (n - 1, n) if n % 2 else ():
                        dve.wait_ge(*W("logit_ready", r + 1))
                        chain(dve.reduce_max(sm[:, 2, r:r + 1], logits(r), AX_X))
                        TS(sm[:, 0, r:r + 1], sm[:, 2, r:r + 1], -1.0, None, ALU.mult).then_inc(S("lmax_ready"), 1)
                    for r in (n - 1, n) if n % 2 else ():
                        dve.wait_ge(*W("lexp_ready", r + 1))
                        chain(inv(sm[:, 3, r:r + 1], sm[:, 1, r:r + 1]))
                        TS(aff[:, r, :], aff[:, r, :], sm[:, 3, r:r + 1], None, ALU.mult).then_inc(S("aff_ready"), 1)
                npt = 48 if main[0] == 0 else NE
                for i in range(2):
                    dve.wait_ge(*W(f"xn_out{i}", 16 * len(main) // 2))
                dve.wait_ge(*W("affT_done", 1))
                chain(dve.memset(affT[:], -1.0))
                if main[0] == 0:
                    dve.tensor_copy(affT[32:32 + NE, 0:CTX], PS[0:NE, 4, 0:CTX])
                seen(dve.tensor_copy(affT[0:NE, :], PS[0:NE, 5, :]), "affT_taken", 1)
                for r in range(CL // 8):
                    c8 = slice(8 * r, 8 * r + 8)
                    chain(dve.max(topv[0:npt, c8], affT[0:npt, :]))
                    dve.max_index(topi_u[0:npt, c8], topv[0:npt, c8], affT[0:npt, :])
                    chain(dve.match_replace(affT[0:npt, :], topv[0:npt, c8], affT[0:npt, :], -1.0))
                if main[0] == 0:
                    dve.tensor_copy(gi[:, 0, CL:SL], topv[32:32 + NE, 0:CC])
                    dve.tensor_copy(gi[:, 1, CL:SL], topi_u[32:32 + NE, 0:CC])
                dve.tensor_copy(gi[:, 0, 0:CL], topv[0:NE, :])
                chain(dve.tensor_copy(gi[:, 1, 0:CL], topi_u[0:NE, :]))
                TS(gi[:, 1, 0:CL], gi[:, 1, 0:CL], float(CTX), None, ALU.add).then_inc(S("gi_ready"), 1)
                dve.wait_ge(*W("giT_done", 1))
                chain(dve.tensor_copy(gateT[0:slot_n, :], PS[0:slot_n, 6, 0:NE]))
                seen(dve.tensor_copy(idxT_u[0:slot_n, :], PS[0:slot_n, 6, NE:2 * NE]), "dn_free", 1)

                def next_rows(e):
                    dve.tensor_copy(idg_u[0:slot_n, :], idxT_u[0:slot_n, bass.ds(e, 1)]).then_inc(S("idg_ready"), 1)

                def low(u, width):
                    slot, _ = slot_turn(u)
                    dve.wait_ge(*W("hi_made", number(u) + 1))
                    TT(wlo[:, slot, 0:width], wr[:, slot, 0:width], whi[:, slot, 0:width].bitcast(F32), ALU.subtract).then_inc(
                        S("lo_made"), 1)

                def take_sel(e):
                    half = slice(KD // 2, KD)
                    dve.wait_ge(*W("selT_done", e + 1))
                    for st, (lo, hi) in enumerate(((0, CL), (CL, slot_n))):
                        for k in range(KD // 2, KD) if hi > lo else ():
                            ins = TS(selF[:, k, lo:hi], PS[:, k // 4, (k % 4) * P + lo:(k % 4) * P + hi],
                                     scl[:, 1, st, k:k + 1], modc[:, 3, st, k:k + 1], ALU.mult, ALU.add)
                    ins.then_inc(S("selF_dve"), 1)
                    dve.wait_ge(*W("selF_dve", e + 1))
                    dve.tensor_copy(shi[:, half, 0:slot_n], selF[:, half, 0:slot_n]).then_inc(S("shi_dve"), 1)
                    dve.wait_ge(*W("shi_dve", e + 1))
                    dve.wait_ge(*W("selT_act", e + 1))
                    TT(slo[:, :, 0:slot_n], selF[:, :, 0:slot_n], shi[:, :, 0:slot_n].bitcast(F32), ALU.subtract).then_inc(
                        S("selT_dve"), 1)

                def scatter_rows(par, e):
                    dve.wait_ge(*W("scattered", 16 * e + 16))
                    dve.tensor_copy(ids_u[0:slot_n, par:par + 1], idxT_u[0:slot_n, bass.ds(e, 1)])
                    dve.tensor_copy(gcur[0:slot_n, par:par + 1], gateT[0:slot_n, bass.ds(e, 1)]).then_inc(S("gate_cur"), 1)

                def expert(par, e, first=False, nxt=True, last=False):
                    for i in range(AHEAD, GU):
                        low(gu(e, i), FE)
                    for j in range(7) if not first else ():
                        low(dn(e - 1, j), D)
                    for b, (f, w) in enumerate(FB):
                        dve.wait_ge(*W("hs_ready", 3 * e + b + 1))
                        if b == 0 and not first:
                            dve.wait_ge(*W("hT_done", e))
                        TT(hh[0:slot_n, f:f + w], hs[0:slot_n, 0:w], PS[0:slot_n, 3 + b, 0:w], ALU.mult).then_inc(
                            S("h_rows"), 1)
                        if not first:
                            low(dn(e - 1, 7 + b), D)
                    if not first:
                        low(dn(e - 1, JF - 1), D)
                    for i in range(AHEAD) if not last else ():
                        low(gu(e + 1, i), FE)
                    if not first:
                        scatter_rows(1 - par, e - 1)
                    if not last:
                        take_sel(e + 1)
                        if nxt:
                            next_rows(e + 2)
                    dve.wait_ge(*W("hT_act", e + 1))
                    for j, n in ((0, 4), (4, 4), (8, 3)):
                        ins = TT(hlo[:, par, j:j + n, 0:slot_n],
                                 PS[:, 2 + j // 4, 0:n * P].rearrange("p (j s) -> p j s", s=P)[:, :, 0:slot_n],
                                 hhi[:, par, j:j + n, 0:slot_n].bitcast(F32), ALU.subtract)
                    ins.then_inc(S("hT_dve"), 1)

                next_rows(0)
                for i in range(AHEAD):
                    low(gu(0, i), FE)
                take_sel(0)
                next_rows(1)
                expert(0, 0, first=True)
                with dve.Fori(1, NE - 3, 2) as e:
                    expert(1, e)
                    expert(0, e + 1)
                for e in range(NE - 3, NE):
                    expert(e % 2, e, nxt=e + 2 < NE, last=e == NE - 1)
                for j in range(JF):
                    low(dn(NE - 1, j), D)
                scatter_rows(1, NE - 1)
                dve.wait_ge(*W("f_rms", 1))
                chain(inv(rstd[:, 0:NT], ss[:, 8:8 + NT]))
                dve.wait_ge(*W("gpb2_in", 32))
                dve.wait_ge(*W("xr_in", 16))
                for n, t in enumerate(main):
                    st = 0 if t >= NCT else 1
                    chain(STT(yt[:, t, :], yt[:, t, :], rstd[:, t:t + 1], gpb2[:, st, :], ALU.mult, ALU.mult))
                    TT(xr[:, t, :], xr[:, t, :], yt[:, t, :], ALU.add).then_inc(S("xf_ready"), 1)

        @block.gpsimd
        def _(pool):
            chained = [0]

            def chain(ins):
                chained[0] += 1
                ins.then_inc(sem("pool_chain"), 1)
                pool.wait_ge(sem("pool_chain"), chained[0])

            pool.memset(ones[:], 1.0)
            pool.memset(masks[:, AVG, :], 1.0 / D)
            chain(pool.memset(masks[:, 0:AVG, :], 1.0))
            for mk, op, b, cm, st in ((IDN, ALU.is_equal, 0, 1, -1), (LE, ALU.is_ge, 0, -1, 1), (GE, ALU.is_ge, 0, 1, -1),
                                      (GT, ALU.is_ge, -1, 1, -1), (LT, ALU.is_ge, -1, -1, 1)):
                ins = pool.affine_select(out=masks[:, mk, :], in_=masks[:, mk, :], compare_op=op, fill=0.0, base=b,
                                         pattern=[[st, P]], channel_multiplier=cm)
            ins.then_inc(sem("consts"), 1)
            for L, main, jobs, slots in LAYERS:
                S, W = sem, counter(L)
                slot_n = CL + (CC if main[0] == 0 else 0)
                TT = pool.tensor_tensor
                bcol = par[:, COL["ada_b"]:COL["ada_b"] + 48].rearrange("p (s k) -> p s k", k=KD)
                pool.wait_ge(*W("par_taken", 1))
                for s in range(6):
                    if s in GATES:
                        gi_ = GATES.index(s)
                        pool.wait_ge(*W("act_job", jobs.index(("ada", s)) + 1))
                        if gi_ == 0:
                            pool.wait_ge(*W("brow_in", 8 * 16))
                        for r in (0, 32):
                            row = arow[r:r + 1, s % 2, :]
                            chain(TT(row, row, brow[r:r + 1, 2 * gi_, :], ALU.add))
                            TT(brow[r:r + 1, 2 * gi_ + 1, :], row, brow[r:r + 1, 2 * gi_ + 1, :], ALU.mult).then_inc(
                                S("gp_ready"), 1)
                            pool.wait_ge(*W("gp_ready", 2 * gi_ + r // 32 + 1))
                            pool.dma_start(gp_d[L, gi_, r // 32:r // 32 + 1, :], brow[r:r + 1, 2 * gi_ + 1, :]).then_inc(
                                S("gp_out"), 16)
                        continue
                    pool.wait_ge(*W("act_job", jobs.index(("adaT", s)) + 1))
                    chain(TT(modc[:, s, :, :], modc[:, s, :, :], bcol[:, s, :].unsqueeze(1).to_broadcast([P, 2, KD]), ALU.add))
                    if s in (1, 4):
                        chain(pool.tensor_scalar(scl[:, s // 4, :, :], modc[:, s, :, :], 1.0, None, ALU.add))
                        gain = par[:, COL["pre_g" if s == 1 else "moe_g"]:][:, 0:KD]
                        ins = TT(scl[:, s // 4, :, :], scl[:, s // 4, :, :], gain.unsqueeze(1).to_broadcast([P, 2, KD]), ALU.mult)
                        ins.then_inc(S("mod_ready"), 1)
                pool.wait_ge(*W("pe_job", jobs.index(("norm", NT - 1)) + 1))
                for j in range(KD):
                    for f in (0, g31 + CTX, 2 * g31 + T):
                        pool.memset(vT[:, j, f:f + g31], 0.0)
                for b in range(2):
                    for f in (0, g5 + CTX, 2 * g5 + T):
                        ins = pool.memset(pre5[:, b, f:f + g5], 0.0)
                ins.then_inc(S("pads_ready"), 1)
                for j in range(KD):
                    pool.wait_ge(*W("act_job", jobs.index(("a", j)) + 1))
                    for s in segs(main):
                        f = g31 + c31(0 if s == 0 else NCT)
                        w = slice(SEG[s][0], SEG[s][0] + SEG[s][1])
                        ins = TT(vT[:, j, f:f + SEG[s][1]], asb[:, w], sg[:, w], ALU.mult)
                    ins.then_inc(S("v_made"), 1)
                pool.wait_ge(*W("pe_job", jobs.index(("xT", 11)) + 1))
                pool.wait_ge(*W("act_job", jobs.index(("xT", 11)) + 1))
                pool.wait_ge(*W("pe_job", jobs.index(("xbc", 15)) + 1))
                heads = lambda ap: ap.rearrange("p (h n) -> p h n", h=H)
                for ch in main:
                    TT(heads(Y[:, ch, :]), heads(xtok[:, ch, :]), hdrow[:, 2, 0:H].unsqueeze(2).to_broadcast([P, H, HD]),
                       ALU.mult).then_inc(S("y_init"), 1)
                pool.wait_ge(*W("conv_done", 2 * KD))
                pool.wait_ge(*W("act_job", len(jobs)))
                def load_gates(ns):
                    for n in ns:
                        if n == 0:
                            pool.wait_ge(*W("vn_ready", KD))
                            for i in range(2):
                                pool.wait_ge(*W(f"sz_out{i}", 16 * len(main) // 2))
                        if n >= 2:
                            pool.wait_ge(*W("yz_ready", n - 1))
                        t = main[n]
                        pool.dma_start(szl[:, n % 2, :], sz_d[t * P:(t + 1) * P, :]).then_inc(S(f"szl_in{n % 2}"), 16)

                pool.wait_ge(*W("wdt_ready", 1))
                nupd = 0
                todo = [(ch, g) for ch in main for g in range(G)]

                def masked_da(q):
                    ch, g = todo[q]
                    if q >= 2:
                        pool.wait_ge(*W("arg_ready", q - 1))
                    for d, mk in ((0, LE), (1, GE)):
                        f = ch * 32 + d * H + g * R
                        ins = TT(dAm[:, q % 2, d, :].rearrange("p (r n) -> p r n", r=R),
                                 masks[:, mk, :].unsqueeze(1).to_broadcast([P, R, P]),
                                 dts[:, DA, f:f + R].unsqueeze(2).to_broadcast([P, R, P]), ALU.mult)
                    ins.then_inc(S("dam_ready"), 1)

                masked_da(0)
                for q in range(len(todo)):
                    if q + 1 < len(todo):
                        masked_da(q + 1)
                    for d, n, at_ in steps_at(main, q):
                        if (d, n, at_) in UPDATES:
                            if nupd:
                                pool.wait_ge(*W("st_ready", nupd))
                            f = at_ * 32 + d * H
                            TT(heads(xw[:]), heads(xtok[:, at_, :]), dts[:, WDT, f:f + H].unsqueeze(2).to_broadcast(
                                [P, H, HD]), ALU.mult).then_inc(S("xw_ready"), 1)
                            nupd += 1
                    if q == 2 * G - 1:
                        load_gates(range(2))
                for n in range(2, len(main)):
                    load_gates([n])
                pool.wait_ge(*W("yn_ready", len(main)))
                for st in range(2):
                    pool.dma_start(gpb[:, st, :], gp_d[L, 0, st, :].partition_broadcast(P)).then_inc(S("gpb_in"), 16)
                pool.dma_start(rw[:], router_w[L].rearrange("(k p) e -> p k e", p=P)).then_inc(S("rw_in"), 16)
                if L:
                    pool.wait_ge(*counter(L - 1)("out_stored", 16 * NT))
                for n, t in enumerate(main):
                    if n >= 2:
                        pool.wait_ge(*W(f"x1_out{n % 2}", 16 * (n // 2)))
                        pool.wait_ge(*W("xn2_ready", n - 1))
                    pool.dma_start(xres[:, n % 2, :], src_rows(L, t)).then_inc(S(f"xres_in{n % 2}"), 16)
                    if n:
                        store_x1(pool, L, main, n - 1)
                store_x1(pool, L, main, len(main) - 1)
                for i in range(2):
                    pool.wait_ge(*W(f"x1_out{i}", 16 * len(main) // 2))
                    pool.wait_ge(*W(f"xn_out{i}", 16 * len(main) // 2))

                pool.wait_ge(*W("logit_ready", len(main)))
                chain(pool.memset(zro[:], 0.0))
                for i in range(2):
                    pool.dma_start(y_d[i * T // 2:(i + 1) * T // 2, :].rearrange("(t p) n -> p t n", p=P),
                                   zro[:].unsqueeze(1).to_broadcast([P, NT // 2, D])).then_inc(S("scattered"), 16)
                    pool.wait_ge(*W("scattered", 16 * (i + 1)))

                def settle(n):
                    if L or not isinstance(n, int) or n:
                        pool.wait_ge(*W("settled", n))
                    TT(eps[:, 1:2], masks[:, IDN, 0:1], masks[:, IDN, 0:1], ALU.add).then_inc(S("settled"), 1)

                def gather(e, n):
                    pool.wait_ge(*W("idg_ready", e + 1))
                    settle(n)
                    pool.indirect_dma_start(out=sel[0:slot_n, :], out_offset=None, in_=xn_d,
                                            in_offset=bass.IndirectOffsetOnAxis(idg_u[0:slot_n, 0:1], 0)).then_inc(
                        S("sel_in"), 16)

                def scatter(par, e, n):
                    pool.wait_ge(*W("dn_free", e + 2))
                    pool.wait_ge(*W("scattered", 16 * e + 32))
                    settle(n)
                    pool.indirect_dma_start(out=y_d, out_offset=bass.IndirectOffsetOnAxis(ids_u[0:slot_n, par:par + 1], 0),
                                            in_=ob[0:slot_n, par, :], in_offset=None, compute_op=ALU.add).then_inc(
                        S("scattered"), 16)

                for e in range(3):
                    gather(e, e)
                with pool.Fori(1, NE - 3, 2) as e:
                    gather(e + 2, 2 * e + 1)
                    scatter(0, e - 1, 2 * e + 2)
                    gather(e + 3, 2 * e + 3)
                    scatter(1, e, 2 * e + 4)
                gather(NE - 1, 2 * NE - 5)
                for e in range(NE - 4, NE):
                    scatter(e % 2, e, NE + e)
                rows = lambda d: d.rearrange("(t p) n -> p t n", p=P)[:, main[0]:NT, :]
                pool.wait_ge(*W("unit_used", UNITS * NE))
                for st in range(2):
                    pool.dma_start(gpb2[:, st, :], gp_d[L, 1, st, :].partition_broadcast(P)).then_inc(S("gpb2_in"), 16)
                pool.dma_start(xr[:, main[0]:NT, :], rows(x1_d)).then_inc(S("xr_in"), 16)
                pool.wait_ge(*W("scattered", 32 + 16 * NE))
                pool.dma_start(yt[:, main[0]:NT, :], rows(y_d)).then_inc(S("yt_in"), 16)
                for n in range(len(main)):
                    store_out(pool, L, main, n)
            pool.wait_ge(*counter(DEPTH - 1)("out_stored", 16 * len(main)))


_INS = ["x", "c", "ctx", "c_ctx", "ada_w", "ada_b", "mix_pre_g", "w_in", "conv_w", "conv_b", "dt_bias", "a_log",
        "d_skip", "ssd_norm_g", "cm_dw_w", "cm_dw_b", "cm_ln_g", "cm_ln_b", "w_out", "mix_post_g", "moe_pre_g",
        "router_w", "exp_w_gate", "exp_w_up", "exp_w_down", "moe_post_g"]


def kernel(**inputs):
    import concourse.bacc as bacc
    from concourse.bass_utils import run_bass_kernel_spmd

    nc = bacc.Bacc("TRN2", target_bir_lowering=False, num_devices=1)
    arrays, aps = {}, {}
    for name in _INS:
        a = np.ascontiguousarray(inputs[name])
        arrays[f"in_{name}"] = a
        aps[name] = nc.dram_tensor(f"in_{name}", a.shape, mybir.dt.from_np(a.dtype), kind="ExternalInput").ap()
    out = nc.dram_tensor("out_x", (1, SEQ, D), F32, kind="ExternalOutput").ap()
    build(nc, out=out, **aps)
    r = run_bass_kernel_spmd(nc, [arrays], core_ids=[0])
    return r.results[0]["out_x"]
```

```python
import numpy as np
import concourse.bass as bass
from concourse import mybir
from concourse.alu_op_type import AluOpType as ALU

ACT = mybir.ActivationFunctionType
AX_X = mybir.AxisListType.X
F32 = mybir.dt.float32
F32R = mybir.dt.float32r
U32 = mybir.dt.uint32

P = 128
D = 1024
KD = D // P
CTX, SEQ = 256, 512
T = CTX + SEQ
NT = T // P
NCT = CTX // P
DEPTH = 2
H, HD, G, R, NS = 16, 64, 4, 4, 128
XBC = 2048
SSD_IN = XBC + 2 * H
Z_END = SSD_IN + D
IN_COLS = Z_END + 2 * D
K5, K31 = 5, 31
NE, FE = 16, 1408
FB = [(0, 512), (512, 512), (1024, 384)]
JF = FE // P
GU = 2 * KD
UNITS = GU + JF
RING = 9
AHEAD = 5
CL, CC = 2 * SEQ // NE, 2 * CTX // NE
EPS = 1e-6
WS = 5
SEG = [(0, CTX), (CTX, SEQ)]

COL = {"conv_w": 0, "conv_b": 80, "dw_b": 96, "ln_g": 104, "ln_b": 112, "pre_g": 120,
       "dw_w": 128, "moe_g": 376, "ada_b": 384, "norm_g": 432, "c": 440, "c_ctx": 448}


GATES = (2, 5)


EARLY = 4


def first_jobs(main, first):
    jobs = [("par", 0)] if first else []
    for s in range(6):
        jobs.append(("ada", s))
        if s == 1 and not first:
            jobs.append(("par", 0))
        if s >= 1 and s - 1 not in GATES:
            jobs.append(("adaT", s - 1))
    jobs += [("norm", t) for t in range(NT)]
    for j in range(KD):
        jobs += [("g", j), ("a", j)]
    jobs += [("dt", 0)] + [("z", t) for t in main] + [("dtT", 0)]
    for j in range(XBC // P):
        jobs.append(("xbc", j))
        if j == 1:
            jobs.append(("cum", 0))
        if 2 <= j < 14:
            jobs.append(("xT", j - 2))
    jobs += [("mean", 0)]
    return jobs


def weight_slots(jobs):
    out = []
    for kind, i in jobs:
        if kind == "ada":
            out += [("ada", i, q) for q in range(4)]
        elif kind == "g" and i % 2 == 0:
            out += [("g", i // 2, 0), ("a", i // 2, 0)]
        elif kind == "dt":
            out += [("dt", 0, 0)] + [("z", 0, q) for q in range(4)]
        elif kind == "xbc" and i % 2 == 0:
            out.append(("xbc", i // 2, 0))
    return out


def build(nc, x, c, ctx, c_ctx, ada_w, ada_b, mix_pre_g, w_in, conv_w, conv_b, dt_bias, a_log,
          d_skip, ssd_norm_g, cm_dw_w, cm_dw_b, cm_ln_g, cm_ln_b, w_out, mix_post_g, moe_pre_g,
          router_w, exp_w_gate, exp_w_up, exp_w_down, moe_post_g, out):
    base = (nc.sbuf_base + 63) // 64 * 64
    end = nc.sbuf_usable_end

    def at(name, shape, off, dt=F32):
        n = int(np.prod(shape[1:])) * 4
        assert base + off + n <= end, (name, off + n, end - base)
        return nc.alloc_sbuf_tensor_at(name, list(shape), dt, offset=base + off)

    o = 0

    def perm(name, shape, dt=F32):
        nonlocal o
        t = at(name, shape, o, dt)
        o += (int(np.prod(shape[1:])) * 4 + 31) // 32 * 32
        return t

    masks = perm("masks", [P, 6, P])
    IDN, LE, GE, GT, LT, AVG = range(6)
    ones = perm("ones", [P, P])
    par = perm("par", [P, 512])
    cstat = perm("cstat", [P, KD, 33])
    modc = perm("modc", [P, 6, 2, KD])
    scl = perm("scl", [P, 2, 2, KD])
    ss = perm("ss", [P, 16])
    rstd = perm("rstd", [P, 16])
    eps = perm("eps", [P, 2])
    hdrow = perm("hdrow", [P, 5, 2 * H])
    W0 = o = (o + 63) // 64 * 64
    wslot = at("wslot", [P, WS, 2048], W0)
    o = W0 + WS * 8192
    U0 = o
    uT = at("uT", [P, KD, T], U0)
    Y = at("Y", [P, NT, D], U0)
    o += KD * T * 4
    X0 = o
    xtok = at("xtok", [P, NT, D], X0)
    o += NT * D * 4
    btok = at("btok", [P, NT, G * NS], o)
    o += NT * G * NS * 4
    B0 = o
    g5 = K5 // 2
    W5 = T + g5
    bct = at("bct", [P, 2 * G, W5], B0)
    yT = at("yT", [P, NT, KD, P], B0)
    ylo = at("ylo", [P, NT, KD, P], B0, F32R)
    yhi = at("yhi", [P, NT, KD, P], U0, F32R)
    vhi = at("vhi", [P, KD, T], X0, F32R)
    S0 = X0 + NT * D * 4
    woh = [at(f"woh{i}", [P, D], S0 + i * 4 * D, F32R) for i in range(3)]
    wol = at("wol", [P, WS, 2048], W0, F32R)
    brow = at("brow", [33, 4, D], B0)
    o += 2 * G * W5 * 4
    g31 = K31 // 2
    W31 = T + g31
    PAD31 = T + 3 * g31
    vT = at("vT", [P, KD, PAD31], o)
    vlo = at("vlo", [P, KD, PAD31], o, F32R)
    o += KD * PAD31 * 4
    TMP = (o + 63) // 64 * 64
    room = (end - base - TMP) // 32 * 32

    def tmp(first, specs):
        off, got = first, []
        for name, shape in specs:
            got.append(at(name, shape, TMP + off))
            off += (int(np.prod(shape[1:])) * 4 + 31) // 32 * 32
        assert off <= room, (off, room)
        return got, off

    prow = at("prow", [P, 4, P], U0)
    (xt, junk, arow), _ = tmp(2048, [("xt", [P, NT, D]), ("junk", [P, D]), ("arow", [33, 2, D])])
    (sg, asb, cacc, pre5, acc5, szt, dtT), _ = tmp(0, [
        ("sg", [P, T]), ("asb", [P, T]), ("cacc", [P, 2, W31]), ("pre5", [P, 2, W5 + 2 * g5]),
        ("acc5", [P, 3, W5]), ("szt", [P, 2, D]), ("dtT", [2 * H, T])])
    DTN = NT * 2 * H
    (dts, ), dt_end = tmp(room - 9 * DTN * 4, [("dts", [P, 9, DTN])])
    D1, D2, D3, DTV, DA, EC, ER, ET, WDT = range(9)
    (mean, sqb, rs), ln_end = tmp(31 * 1024, [("mean", [P, W31]), ("sqb", [P, 2, W31]), ("rs", [P, W31])])
    assert TMP + ln_end <= TMP + room - 9 * DTN * 4
    (dAm, E, xw, hst, SUL, GB, GA, otmp), ssd_end = tmp(0, [
        ("dAm", [P, 2, 2, 512]), ("E", [P, 2, 512]), ("xw", [P, D]), ("hst", [P, 2, D]), ("SUL", [P, 2, 2, P]),
        ("GB", [P, 2, 512]), ("GA", [P, 2, 512]), ("otmp", [P, D])])
    (szl,), _ = tmp(ssd_end, [("szl", [P, 2, D])])
    woh.append(at("woh3", [P, D], TMP + room - 4 * D, F32R))
    WOH = len(woh)
    assert ssd_end + 2 * 4 * D <= room - 4 * D
    (gpb, xres, xn2, u2T, rw, sm, aff), _ = tmp(0, [
        ("gpb", [P, 2, D]), ("xres", [P, 2, D]), ("xn2", [P, NT, D]), ("u2T", [P, KD, P]),
        ("rw", [P, KD, NE]), ("sm", [P, 4, NT]), ("aff", [P, NT, NE])])
    SL = CL + CC
    o = W0

    def moe(name, shape, dt=F32):
        nonlocal o
        t = at(name, shape, o, dt)
        o += (int(np.prod(shape[1:])) * 4 + 31) // 32 * 32
        return t

    wr = moe("wr", [P, RING, FE])
    whi = moe("whi", [P, RING, FE], F32R)
    wlo = moe("wlo", [P, RING, FE], F32R)
    selF = moe("selF", [P, KD, SL])
    shi = moe("shi", [P, KD, SL], F32R)
    slo = moe("slo", [P, KD, SL], F32R)
    hhi = moe("hhi", [P, 2, JF, SL], F32R)
    hlo = moe("hlo", [P, 2, JF, SL], F32R)
    affT, topv, topi, gi = (moe(n, sh) for n, sh in (
        ("affT", [48, SEQ]), ("topv", [48, CL]), ("topi", [48, CL]), ("gi", [NE, 2, SL])))
    idxT, gateT, idg, ids, gcur = (moe(n, sh) for n, sh in (
        ("idxT", [SL, NE]), ("gateT", [SL, NE]), ("idg", [SL, 1]), ("ids", [SL, 2]), ("gcur", [SL, 2])))
    sel, hs, hh = (moe(n, sh) for n, sh in (("sel", [SL, D]), ("hs", [SL, 512]), ("hh", [SL, FE])))
    zro = at("zro", [P, D], o)
    ob = moe("ob", [SL, 2, D])
    topi_u, idg_u, ids_u, idxT_u = (b[:].bitcast(U32) for b in (topi, idg, ids, idxT))
    yt = at("yt", [P, NT, D], U0 + 4096)
    xr = at("xr", [P, NT, D], U0 + 4096 + NT * D * 4)
    gpb2 = at("gpb2", [P, 2, D], U0 + 4096 + 2 * NT * D * 4)
    assert U0 + 4096 + (2 * NT + 2) * D * 4 <= B0
    PS = nc.alloc_psum_tensor("PS", [P, 8, 512], F32)

    def dram(name, shape):
        return nc.dram_tensor(name, shape, F32, kind="Internal").ap()

    x1_d, xn_d, y_d, sz_d = (dram(n, (T, D)) for n in ("x1_d", "xn_d", "y_d", "sz_d"))
    xl_d = dram("xl_d", (T, D))
    gp_d = dram("gp_d", (DEPTH, 2, 2, D))

    sems = {}

    def sem(name):
        if name not in sems:
            sems[name] = nc.alloc_semaphore(name)
        return sems[name]

    LAYERS = []
    for L in range(DEPTH):
        main = list(range(NT)) if L < DEPTH - 1 else list(range(NCT, NT))
        jobs = first_jobs(main, L == 0)
        LAYERS.append((L, main, jobs, weight_slots(jobs)))

    def gu(e, i):
        return (e, i) if isinstance(e, int) and e == 0 else (e, GU - UNITS + i)

    def dn(e, i):
        return (e, GU + i) if isinstance(e, int) and e == NE - 1 else (e, 2 * GU + i)

    def number(u):
        return u[0] * UNITS + u[1]

    def slot_turn(u):
        return u[1] % RING, u[0] * (UNITS // RING) + u[1] // RING

    def seg_banks(unit, s):
        return PS[:, 2 * unit + s, 0:SEG[s][1]]

    def unit2(unit, rows=P):
        return PS[0:rows, 2 * unit:2 * unit + 2, :].rearrange("p b n -> p (b n)")

    def c5(t):
        return P * t + (g5 if t >= NCT else 0)

    def c31(t):
        return P * t + (g31 if t >= NCT else 0)

    def logits(n):
        return PS[:, 4 * ((n // 2) % 2) + 2 + n % 2, 0:NE]

    def wo_order(m):
        return (m + KD // 2) % KD

    def segs(main):
        return (0, 1) if main[0] == 0 else (1,)

    def pairs(main):
        return [main[i:i + 2] for i in range(0, len(main), 2)]

    def src_rows(L, t):
        if L:
            return xl_d[t * P:(t + 1) * P, :]
        return ctx[0, t * P:(t + 1) * P, :] if t < NCT else x[0, (t - NCT) * P:(t - NCT + 1) * P, :]

    def slot_free(L, jobs, slots, n):
        kind, i, q = slots[n]
        if kind == "ada" and q < 3:
            return counter(L)("ada_used", 3 * i + q + 1)
        last = {"ada": i, "g": 2 * i + 1, "a": 2 * i + 1, "xbc": 2 * i + 1, "dt": 0,
                "z": max((j[1] for j in jobs if j[0] == "z"))}[kind]
        return counter(L)("pe_job", jobs.index((kind, last)) + 1)

    def scan(d):
        ctx_first = list(range(NCT)) if d == 0 else list(range(NCT))[::-1]
        lat = list(range(NCT, NT)) if d == 0 else list(range(NCT, NT))[::-1]
        return ctx_first + lat

    STEPS = [(d, n, scan(d)[n]) for n in range(NT) for d in range(2)]

    def reads(main):
        return [s for s in STEPS if s[1] and s[2] in main]

    UPDATES = [s for s in STEPS if s[1] < NT - 1]

    units = NT * G
    TOTAL = {}

    def count(total, names):
        TOTAL.update({name: total for name in names.split()})

    count(1, "f_rms x_rms x_rstd pads_ready sp_abs sp_exp sp_one sp_ln a_exp da_ready wdt_ready var_taken "
             "affT_done affT_taken gi_ready giT_done")
    count(2, "mod_ready")
    count(NT, "yT_fa yT_fd yhi_dve norm_dve")
    count(NT, "x_sq xn_ready y_init yz_ready y_sq y_rms y_rstd yn_ready ynT_done yT_ready yT_dve m_sq m_rms m_taken x1_ready "
              "x1_sq x1_rms x1_rstd xn2_ready u2T_done u2_ready logit_ready lmax_ready lexp_ready aff_ready "
              "f_sq xf_ready")
    count(KD, "v_made conf_done vc_ready sq_ready sq_used vn_ready v_ready")
    count(XBC // P, "taps_done conv_done")
    count(units, "ga_ready dam_ready arg_ready e_ready s_ready m_ready yd_ready yd_taken")
    count(2 * units, "sul_ready")
    count(len(reads(range(NT))), "o_ready o_taken")
    count(len(UPDATES), "xw_ready st_ready h_ready")
    count(len(LAYERS[0][2]), "pe_job act_job")
    count(18, "ada_used")
    count(4, "gp_ready")
    count(NT * KD, "wo_used")
    count(NT * KD - KD, "woh_made wol_made")
    count(KD, "vhi_made vlo_made")
    count(16 * 16, "par_in")
    count(16 * NT, "out_stored")
    count(8 * 16, "brow_in")
    count(4 * 16, "gp_out")
    count(2 * 16, "gpb_in gpb2_in")
    count(16, "rw_in xr_in yt_in")
    count(16 * NT // 2, "sz_out0 sz_out1 szl_in0 szl_in1 x1_out0 x1_out1 xn_out0 xn_out1 "
                        "xres_in0 xres_in1")
    count(NE, "selT_done selT_act selT_dve hT_done hT_act hT_dve gate_cur selF_act selF_dve shi_dve idg_ready")
    count(NE + 1, "dn_free")
    count(2 * NE, "settled")
    count(3 * NE, "hs_ready h_rows")
    count(UNITS * NE, "hi_made lo_made unit_used")
    for i in range(RING):
        count(16 * UNITS * NE // RING, f"unit_in{i}")
    count(16 * NE, "sel_in")
    count(16 * NE + 32, "scattered")
    pieces = len(LAYERS[0][3]) + NT // 2 * KD
    for i in range(WS):
        count(16 * len(range(i, pieces, WS)), f"w_in{i}")

    def counter(L):
        return lambda name, v: (sem(name), L * TOTAL[name] + v)

    def steps_at(main, q):
        n = len(main) * G
        return [s for k, s in enumerate(STEPS) if (k + 1) * n // len(STEPS) - 1 == q]

    def seg_cols(main, gap):
        return (0, T + gap) if main[0] == 0 else (CTX + gap, SEQ)

    def store_out(pool, L, main, n):
        t = main[n]
        dst = xl_d[t * P:(t + 1) * P, :] if L < DEPTH - 1 else out[0, (t - NCT) * P:(t - NCT + 1) * P, :]
        pool.wait_ge(*counter(L)("xf_ready", n + 1))
        pool.dma_start(dst, xr[:, t, :]).then_inc(sem("out_stored"), 16)

    def store_x1(pool, L, main, n):
        t = main[n]
        pool.wait_ge(*counter(L)("x1_ready", n + 1))
        pool.dma_start(x1_d[t * P:(t + 1) * P, :], xres[:, n % 2, :]).then_inc(sem(f"x1_out{n % 2}"), 16)
        pool.wait_ge(*counter(L)("xn2_ready", n + 1))
        pool.dma_start(xn_d[t * P:(t + 1) * P, :], xn2[:, n, :]).then_inc(sem(f"xn_out{n % 2}"), 16)

    with nc.Block() as block:
        @block.sync
        def _(sp):
            for L, main, jobs, slots in LAYERS:
                S, W = sem, counter(L)
                if L:
                    sp.wait_ge(*W("lo_made", 0))

                def load_params():
                    def rows(ap, n0, what):
                        ti, r = divmod(COL[what] + n0, P)
                        sp.dma_start(prow[r:r + ap.shape[0], ti, :], ap).then_inc(S("par_in"), 16)

                    rows(conv_w[L].rearrange("k (t p) -> (k t) p", p=P), 0, "conv_w")
                    for src, what in ((conv_b, "conv_b"), (cm_dw_b, "dw_b"), (cm_ln_g, "ln_g"), (cm_ln_b, "ln_b"),
                                      (mix_pre_g, "pre_g"), (moe_pre_g, "moe_g"), (ssd_norm_g, "norm_g"), (ada_b, "ada_b")):
                        rows(src[L].rearrange("(t p) -> t p", p=P), 0, what)
                    dw = cm_dw_w[L].rearrange("k (t p) -> (k t) p", p=P)
                    rows(dw[0:P], 0, "dw_w")
                    rows(dw[P:K31 * KD], P, "dw_w")
                    rows(c[0].rearrange("(t p) -> t p", p=P), 0, "c")
                    rows(c_ctx.rearrange("(t p) -> t p", p=P), 0, "c_ctx")
                    for i, src in enumerate((dt_bias[L].rearrange("a h -> (a h)"), a_log[L].rearrange("a h -> (a h)"), d_skip[L])):
                        sp.dma_start(hdrow[:, i, 0:src.shape[0]], src.partition_broadcast(P)).then_inc(S("par_in"), 16)
                    if L:
                        sp.wait_ge(*W("unit_used", 0))
                    for gi_, s in enumerate(GATES):
                        for r in (0, 32):
                            sp.dma_start(brow[r:r + 1, 2 * gi_, :], ada_b[L:L + 1, s * D:(s + 1) * D]).then_inc(S("brow_in"), 16)
                            sp.dma_start(brow[r:r + 1, 2 * gi_ + 1, :], (mix_post_g, moe_post_g)[gi_][L:L + 1, :]).then_inc(
                                S("brow_in"), 16)

                if L == 0:
                    load_params()
                win = w_in[L].rearrange("(k p) n -> p k n", p=P)
                aw = ada_w[L].rearrange("(k p) n -> p k n", p=P)
                for n, (kind, i, q) in enumerate(slots):
                    if n == WS and L:
                        load_params()
                    if n == WS and L == 0:
                        for t in range(NT):
                            sp.dma_start(xt[:, t, :], src_rows(L, t)).then_inc(sem("x_in"), 16)
                    if n >= WS:
                        sp.wait_ge(*slot_free(L, jobs, slots, n - WS))
                    dst = wslot[:, n % WS, :]
                    if kind == "ada":
                        dst = dst.rearrange("p (k n) -> p k n", k=2)
                        src = aw[:, 2 * q:2 * q + 2, i * D:(i + 1) * D]
                    elif kind == "dt":
                        dst = dst[:, 0:KD * 32].rearrange("p (k n) -> p k n", k=KD)
                        src = win[:, :, XBC:SSD_IN]
                    else:
                        dst = dst.rearrange("p (k n) -> p k n", k=KD)
                        first = {"g": Z_END + D + i * 256, "a": Z_END + i * 256, "z": SSD_IN + q * 256,
                                 "xbc": i * 256}[kind]
                        src = win[:, :, first:first + 256]
                    sp.dma_start(dst, src).then_inc(S(f"w_in{n % WS}"), 16)
                wo = w_out[L].rearrange("(q b p) n -> q p b n", b=2, p=P)
                for m in range(len(pairs(main)) * KD):
                    n = len(slots) + m
                    if m >= WS:
                        sp.wait_ge(*W("wo_used", 2 * (m - WS + 1)))
                    else:
                        sp.wait_ge(*slot_free(L, jobs, slots, n - WS))
                    sp.dma_start(wslot[:, n % WS, :].rearrange("p (b n) -> p b n", b=2), wo[wo_order(m)]).then_inc(
                        S(f"w_in{n % WS}"), 16)
                sp.wait_ge(*W("wo_used", len(main) * KD))

                def load(u, src):
                    slot, turn = slot_turn(u)
                    if not isinstance(turn, int) or turn:
                        sp.wait_ge(*W("lo_made", number(u) - RING + 1))
                    sp.dma_start(wr[:, slot, 0:src.shape[-1]], src).then_inc(S(f"unit_in{slot}"), 16)

                def load_gate_up(e):
                    for k in range(KD):
                        for mi, w in ((0, exp_w_gate), (1, exp_w_up)):
                            load(gu(e, 2 * k + mi), w[L, bass.ds(e, 1), k * P:(k + 1) * P, :].rearrange("o p n -> (o p) n"))

                def load_down(e):
                    src = exp_w_down[L, bass.ds(e, 1), :, :].rearrange("o (p j) n -> (o p) j n", j=JF)
                    for j in range(JF):
                        load(dn(e, j), src[:, j, :])

                load_gate_up(0)
                with sp.Fori(1, NE) as e:
                    load_gate_up(e)
                    load_down(e - 1)
                load_down(NE - 1)

        @block.tensor
        def _(pe):
            def tr(dst, src, n):
                return pe.transpose(dst, src, masks[0:n, IDN, 0:n])

            pe.wait_ge(sem("consts"), 1)
            for L, main, jobs, slots in LAYERS:
                S, W = sem, counter(L)
                where = {sl: n for n, sl in enumerate(slots)}
                slot_n = CL + (CC if main[0] == 0 else 0)

                def weights(n):
                    pe.wait_ge(*W(f"w_in{n % WS}", 16 * (n // WS + 1)))
                    return wslot[:, n % WS, :]

                for n, (kind, i) in enumerate(jobs):
                    u = n % 4
                    if n >= 4:
                        pe.wait_ge(*W("act_job", n - 3))
                    if L and n == 3:
                        pe.wait_ge(*counter(L - 1)("dn_free", NE + 1))
                    if kind == "par":
                        pe.wait_ge(*W("par_in", 16 * 16))
                        for t, w in enumerate((P, P, P, 72)):
                            m = tr(PS[:, 2 * u, t * P:t * P + w], prow[0:w, t, :], w)
                    elif kind == "ada":
                        if n <= 1:
                            pe.wait_ge(sem("cstat_ready"), 1)
                        for q in range(4):
                            wv = weights(where["ada", i, q])
                            for kk in range(2):
                                for h in range(2):
                                    m = pe.matmul(PS[0:33, 2 * u + h, :], cstat[:, 2 * q + kk, :],
                                                  wv[:, kk * D + h * 512:kk * D + (h + 1) * 512],
                                                  start=q + kk == 0, stop=q + kk == 4)
                            if q < 3:
                                m.then_inc(S("ada_used"), 1)
                    elif kind == "adaT":
                        pe.wait_ge(*W("act_job", jobs.index(("ada", i)) + 1))
                        for k in range(KD):
                            m = tr(PS[:, 2 * u, k * 33:(k + 1) * 33], arow[:, i % 2, k * P:(k + 1) * P], 33)
                    elif kind == "norm":
                        pe.wait_ge(*W("xn_ready", i + 1))
                        if i >= 4:
                            pe.wait_ge(*W("norm_dve", i - 3))
                        for k in range(KD):
                            m = tr(PS[:, 2 * u + k // 4, (k % 4) * P:(k % 4 + 1) * P], xt[:, i, k * P:(k + 1) * P], P)
                    elif kind in ("g", "a", "xbc"):
                        if i == 0 and kind == "g":
                            pe.wait_ge(*W("act_job", jobs.index(("norm", NT - 1)) + 1))
                            pe.wait_ge(*W("norm_dve", NT))
                        wv = weights(where[kind, i // 2, 0]).rearrange("p (k n) -> p k n", k=KD)
                        for s in (0, 1) if kind == "xbc" else segs(main):
                            for k in range(KD):
                                m = pe.matmul(seg_banks(u, s), wv[:, k, (i % 2) * P:(i % 2 + 1) * P],
                                              uT[:, k, SEG[s][0]:SEG[s][0] + SEG[s][1]], start=k == 0, stop=k == KD - 1)
                    elif kind == "dt":
                        wv = weights(where["dt", 0, 0])[:, 0:KD * 32].rearrange("p (k n) -> p k n", k=KD)
                        for s in (0, 1):
                            for k in range(KD):
                                m = pe.matmul(PS[0:32, 2 * u + s, 0:SEG[s][1]], wv[:, k, :],
                                              uT[:, k, SEG[s][0]:SEG[s][0] + SEG[s][1]], start=k == 0, stop=k == KD - 1)
                    elif kind == "z":
                        for q in range(4):
                            wv = weights(where["z", 0, q]).rearrange("p (k n) -> p k n", k=KD)
                            for k in range(KD):
                                m = pe.matmul(PS[:, 2 * u + q // 2, (q % 2) * 256:(q % 2 + 1) * 256],
                                              uT[:, k, i * P:(i + 1) * P], wv[:, k, :], start=k == 0, stop=k == KD - 1)
                    elif kind == "dtT":
                        pe.wait_ge(*W("act_job", jobs.index(("dt", 0)) + 1))
                        for t in range(NT):
                            m = tr(PS[:, 2 * u, t * 32:(t + 1) * 32], dtT[:, t * P:(t + 1) * P], 32)
                    elif kind == "cum":
                        pe.wait_ge(*W("da_ready", 1))
                        dav = dts[:, DA, :].rearrange("p (t d h) -> p t d h", d=2, h=H)
                        for b, pair in enumerate(((LE, GE), (GT, LT))):
                            for d, mk in enumerate(pair):
                                pe.matmul(PS[:, 2 * u, b * 256 + d * 96:b * 256 + d * 96 + 96].rearrange(
                                    "p (t h) -> p t h", h=H), masks[:, mk, :], dav[:, :, d, :], start=True, stop=True)
                        m = pe.matmul(PS[:, 2 * u + 1, 0:DTN], ones[:], dts[:, DA, :], start=True, stop=True)
                    elif kind == "xT":
                        pe.wait_ge(*W("conv_done", i + 1))
                        for t in range(NT):
                            src = acc5[:, i % 3, c5(t):c5(t) + P] if i < 8 else bct[:, i - 8, c5(t):c5(t) + P]
                            m = tr(PS[:, 2 * u + t // 4, (t % 4) * P:(t % 4 + 1) * P], src, P)
                    elif kind == "mean":
                        pe.wait_ge(*W("conf_done", KD))
                        for s in segs(main):
                            f = c31(0 if s == 0 else NCT)
                            for k in range(KD):
                                m = pe.matmul(seg_banks(u, s), masks[:, AVG, :], vT[:, k, f:f + SEG[s][1]],
                                              start=k == 0, stop=k == KD - 1)
                    m.then_inc(S("pe_job"), 1)
                pe.wait_ge(*W("act_job", len(jobs)))
                for k in range(KD):
                    pe.wait_ge(*W("sq_ready", k + 1))
                    for s in segs(main):
                        f = c31(0 if s == 0 else NCT)
                        m = pe.matmul(seg_banks(0, s), masks[:, AVG, :], sqb[:, k % 2, f:f + SEG[s][1]],
                                      start=k == 0, stop=k == KD - 1)
                    m.then_inc(S("sq_used"), 1)
                pe.wait_ge(*W("var_taken", 1))
                pe.wait_ge(*W("conv_done", 2 * KD))
                todo = [(ch, g) for ch in main for g in range(G)]

                def outputs(q):
                    ch, g = todo[q]
                    pe.wait_ge(*W("m_ready", q + 1))
                    if q:
                        pe.wait_ge(*W("yd_taken", q))
                    for r in range(R):
                        pr = g * 256 + (r // 2) * P
                        m = pe.matmul(PS[:, 3, r * P:(r + 1) * P], GB[:, q % 2, r * P:(r + 1) * P],
                                      xtok[:, ch, pr:pr + P], start=True, stop=True)
                    m.then_inc(S("yd_ready"), 1)

                done = {"read": 0, "upd": 0}

                def state_step(d, n, ch):
                    if (d, n, ch) in reads(main):
                        pe.wait_ge(*W("h_ready", done["upd"]))
                        if done["read"]:
                            pe.wait_ge(*W("o_taken", done["read"]))
                        for g in range(G):
                            m = pe.matmul(PS[:, 4 + g // 2, (g % 2) * 256:(g % 2 + 1) * 256],
                                          bct[:, G + g, c5(ch):c5(ch) + P], hst[:, d, g * 256:(g + 1) * 256],
                                          start=True, stop=True)
                        m.then_inc(S("o_ready"), 1)
                        done["read"] += 1
                    if (d, n, ch) in UPDATES:
                        pe.wait_ge(*W("xw_ready", done["upd"] + 1))
                        if done["upd"]:
                            pe.wait_ge(*W("h_ready", done["upd"]))
                        for g in range(G):
                            m = pe.matmul(PS[:, 6 + g // 2, (g % 2) * 256:(g % 2 + 1) * 256],
                                          btok[:, ch, g * NS:(g + 1) * NS], xw[:, g * 256:(g + 1) * 256],
                                          start=True, stop=True)
                        m.then_inc(S("st_ready"), 1)
                        done["upd"] += 1

                def scores(q):
                    ch, g = todo[q]
                    pe.wait_ge(*W("dam_ready", q + 1))
                    if q:
                        pe.wait_ge(*W("e_ready", q))
                    pe.matmul(PS[:, 0, :], masks[:, GT, :], dAm[:, q % 2, 0, :], start=True, stop=False)
                    pe.matmul(PS[:, 0, :], masks[:, LT, :], dAm[:, q % 2, 1, :], start=False, stop=True).then_inc(
                        S("arg_ready"), 1)
                    if q >= 2:
                        pe.wait_ge(*W("sul_ready", 2 * q - 2))
                    pe.matmul(PS[:, 1 + q % 2, 0:P], bct[:, g, c5(ch):c5(ch) + P], bct[:, G + g, c5(ch):c5(ch) + P],
                              start=True, stop=True).then_inc(S("s_ready"), 1)

                scores(0)
                for q in range(len(todo)):
                    if q + 1 < len(todo):
                        scores(q + 1)
                    if q:
                        outputs(q - 1)
                    for s in steps_at(main, q):
                        state_step(*s)
                outputs(len(todo) - 1)
                q = len(todo)
                pe.wait_ge(*W("yd_taken", q))
                pe.wait_ge(*W("o_taken", done["read"]))
                pe.wait_ge(*W("h_ready", done["upd"]))
                def yn_transposes(n):
                    pe.wait_ge(*W("yn_ready", n + 1))
                    if n >= 2:
                        pe.wait_ge(*W("yT_dve", n - 1))
                    for k in range(KD):
                        m = tr(PS[:, 4 + 2 * (n % 2) + k // 4, (k % 4) * P:(k % 4 + 1) * P],
                               Y[:, main[n], k * P:(k + 1) * P], P)
                    m.then_inc(S("ynT_done"), 1)

                def router_rows(n):
                    b = 4 * ((n // 2) % 2)
                    pe.wait_ge(*W("m_taken", n // 2 * 2 + 2))
                    pe.wait_ge(*W("xn2_ready", n + 1))
                    if n % 2:
                        pe.wait_ge(*W("u2_ready", n))
                    for k in range(KD):
                        m = tr(PS[:, b + k // 4, (k % 4) * P:(k % 4 + 1) * P], xn2[:, n, k * P:(k + 1) * P], P)
                    m.then_inc(S("u2T_done"), 1)

                def router_logits(n):
                    pe.wait_ge(*W("u2_ready", n + 1))
                    if n == 0:
                        pe.wait_ge(*W("rw_in", 16))
                    for k in range(KD):
                        m = pe.matmul(logits(n), u2T[:, k, :], rw[:, k, :], start=k == 0, stop=k == KD - 1)
                    m.then_inc(S("logit_ready"), 1)

                n = len(slots)
                for pi, pair in enumerate(pairs(main)):
                    if pi >= 2:
                        pe.wait_ge(*W("lexp_ready", 2 * (pi - 1)))
                    for q in range(KD):
                        if pi == 0 and q == KD // 2:
                            pe.wait_ge(*W("yT_dve", len(main)))
                        for b in range(2):
                            k = 2 * wo_order(q) + b
                            r = 2 * (pi * KD + q) + b
                            if r < KD:
                                if r == 0:
                                    pe.wait_ge(*W("v_ready", KD))
                                wv = weights(n)
                                for ti, t in enumerate(pair):
                                    for h in range(2):
                                        m = pe.matmul(PS[:, 2 * ti + h, :], vT[:, k - KD, c31(t):c31(t) + P],
                                                      wv[:, b * D + h * 512:b * D + (h + 1) * 512],
                                                      start=r == 0, stop=False)
                                m.then_inc(S("wo_used"), 1)
                                continue
                            pe.wait_ge(*W("wol_made", r - KD + 1))
                            if pi == 1 and k >= KD:
                                pe.wait_ge(*W("vlo_made", k - KD + 1))
                            w_hi, w_lo = woh[r % WOH][:], wol[:, n % WS, b * D:(b + 1) * D]
                            for ti, t in enumerate(pair):
                                if k < KD:
                                    hi, lo = yhi[:, t, k, :], ylo[:, t, k, :]
                                else:
                                    hi, lo = vhi[:, k - KD, t * P:(t + 1) * P], vlo[:, k - KD, c31(t):c31(t) + P]
                                for c3, (x_, w_) in enumerate(((hi, w_hi), (hi, w_lo), (lo, w_hi))):
                                    for h in range(2):
                                        m = pe.matmul(PS[:, 4 * (pi % 2) + 2 * ti + h, :], x_, w_[:, h * 512:(h + 1) * 512],
                                                      start=q + b + c3 == 0, stop=q == KD - 1 and b == 1 and c3 == 2)
                            m.then_inc(S("wo_used"), 1)
                        n += 1
                        if pi == 0 and q < KD // 2:
                            for t in range(q * len(main) // 4, (q + 1) * len(main) // 4):
                                yn_transposes(t)
                        if pi and q == 4:
                            router_rows(2 * pi - 2)
                        if pi and q == 5:
                            router_logits(2 * pi - 2)
                            router_rows(2 * pi - 1)
                        if pi and q == 6:
                            router_logits(2 * pi - 1)
                for t in range(len(main) - 2, len(main)):
                    router_rows(t)
                    router_logits(t)
                pe.wait_ge(*W("aff_ready", len(main)))
                for n, t in enumerate(main):
                    dst = PS[0:NE, 4, t * P:(t + 1) * P] if t < NCT else PS[0:NE, 5, (t - NCT) * P:(t - NCT + 1) * P]
                    m = tr(dst, aff[:, n, :], P)
                m.then_inc(S("affT_done"), 1)
                pe.wait_ge(*W("gi_ready", 1))
                for b in range(2):
                    m = tr(PS[0:slot_n, 6, b * NE:(b + 1) * NE], gi[:, b, 0:slot_n], NE)
                m.then_inc(S("giT_done"), 1)

                def sel_transposes():
                    for k in range(KD):
                        m = tr(PS[:, k // 4, (k % 4) * P:(k % 4) * P + slot_n], sel[0:slot_n, k * P:(k + 1) * P], slot_n)
                    m.then_inc(S("selT_done"), 1)

                def product(u, dst, hi, lo, widths, start, stop):
                    slot, _ = slot_turn(u)
                    pe.wait_ge(*W("lo_made", number(u) + 1))
                    for n, (x_, w_) in enumerate(((hi, whi), (hi, wlo), (lo, whi))):
                        for b, (f, w) in enumerate(widths):
                            m = pe.matmul(dst(b, w), x_, w_[:, slot, f:f + w], start=start and n == 0, stop=stop and n == 2)
                    m.then_inc(S("unit_used"), 1)

                def gate_up(e):
                    pe.wait_ge(*W("selT_dve", e + 1))
                    for k in range(KD):
                        for mi in range(2):
                            product(gu(e, 2 * k + mi), lambda b, w: PS[0:slot_n, 3 * mi + b, 0:w], shi[:, k, 0:slot_n],
                                    slo[:, k, 0:slot_n], FB, k == 0, k == KD - 1)

                def down(par, e, lo, hi):
                    for j in range(lo, hi):
                        product(dn(e, j), lambda b, w: PS[0:slot_n, 6 + b, 0:w], hhi[:, par, j, 0:slot_n],
                                hlo[:, par, j, 0:slot_n], [(0, 512), (512, 512)], j == 0, j == JF - 1)

                def h_transposes():
                    hv = hh[0:slot_n, :].rearrange("s (p j) -> s p j", j=JF)
                    for j in range(JF):
                        m = tr(PS[:, 2 + j // 4, (j % 4) * P:(j % 4) * P + slot_n], hv[:, :, j], slot_n)
                    m.then_inc(S("hT_done"), 1)

                def expert(par, e, first=False, last=False):
                    if not first:
                        pe.wait_ge(*W("hT_dve", e))
                    gate_up(e)
                    if not first:
                        pe.wait_ge(*W("dn_free", e))
                        down(1 - par, e - 1, 0, 3)
                    if not last:
                        pe.wait_ge(*W("hs_ready", 3 * e + 2))
                        pe.wait_ge(*W("sel_in", 16 * e + 32))
                    if not first:
                        down(1 - par, e - 1, 3, 4)
                    if not last:
                        sel_transposes()
                    if not first:
                        down(1 - par, e - 1, 4, 7)
                    pe.wait_ge(*W("h_rows", 3 * e + 3))
                    if not first:
                        down(1 - par, e - 1, 7, 8)
                    h_transposes()
                    if not first:
                        down(1 - par, e - 1, 8, JF)

                pe.wait_ge(*W("affT_taken", 1))
                pe.wait_ge(*W("sel_in", 16))
                sel_transposes()
                expert(0, 0, first=True)
                with pe.Fori(1, NE - 3, 2) as e:
                    expert(1, e)
                    expert(0, e + 1)
                for e in range(NE - 3, NE):
                    expert(e % 2, e, last=e == NE - 1)
                pe.wait_ge(*W("hT_dve", NE))
                pe.wait_ge(*W("dn_free", NE))
                down(1, NE - 1, 0, JF)

        @block.scalar
        def _(act):
            def modulation_job(L, n):
                W, jobs = counter(L), LAYERS[L][2]
                kind, i = jobs[n]
                u = n % 4
                if kind == "ada" and i >= 2:
                    if i - 2 in GATES:
                        act.wait_ge(*W("gp_ready", 2))
                    else:
                        act.wait_ge(*W("pe_job", jobs.index(("adaT", i - 2)) + 1))
                act.wait_ge(*W("pe_job", n + 1))
                if kind == "par":
                    ins = act.copy(par[:, 0:P * 3 + 72], PS[:, 2 * u, 0:P * 3 + 72])
                elif kind == "ada":
                    ins = act.copy(arow[:, i % 2, :], unit2(u, 33))
                else:
                    ins = act.copy(modc[:, i, :, :], PS[:, 2 * u, 0:KD * 33].rearrange(
                        "p (k s) -> p s k", s=33)[:, 0:33:32, :])
                ins.then_inc(sem("act_job"), 1)
                if kind == "par" and L == 0:
                    act.wait_ge(*W("act_job", n + 1))
                    act.wait_ge(sem("cstat_zero"), 1)
                    act.activation(cstat[:, :, 0:33:32].rearrange("p k s -> p s k"),
                                   par[:, COL["c"]:COL["c"] + 16].rearrange("p (s k) -> p s k", s=2),
                                   ACT.Silu).then_inc(sem("cstat_ready"), 1)
                    act.wait_ge(sem("eps_set"), 1)

            for n in range(EARLY):
                modulation_job(0, n)
            for L, main, jobs, slots in LAYERS:
                S, W = sem, counter(L)
                slot_n = CL + (CC if main[0] == 0 else 0)
                v0, vw = seg_cols(main, g31)

                def rms(src, junk_, col, stage, n):
                    act.activation(junk_, src, ACT.Square, accum_out=ss[:, col:col + 1]).then_inc(S(f"{stage}_sq"), 1)
                    act.wait_ge(*W(f"{stage}_sq", n + 1))
                    act.activation(ss[:, col + 1:col + 2], ss[:, col:col + 1], ACT.Sqrt, bias=eps[:, 0:1],
                                   scale=1.0 / D).then_inc(S(f"{stage}_rms"), 1)

                def silu5(j):
                    act.wait_ge(*W("taps_done", j + 1))
                    dst = acc5[:, j % 3, :] if j < 8 else bct[:, j - 8, :]
                    act.activation(dst, acc5[:, j % 3, :], ACT.Silu,
                                   bias=par[:, COL["conv_b"] + j:COL["conv_b"] + j + 1]).then_inc(S("conv_done"), 1)

                rows_in = xt if L == 0 else xr
                if L == 0:
                    act.wait_ge(sem("x_in"), 16 * NT)
                for t in range(NT):
                    if L:
                        act.wait_ge(*counter(L - 1)("xf_ready", t + 1))
                    if t:
                        act.wait_ge(*W("x_sq", t))
                    act.activation(junk[:], rows_in[:, t, :], ACT.Square, accum_out=ss[:, t:t + 1]).then_inc(S("x_sq"), 1)
                act.wait_ge(*W("x_sq", NT))
                act.activation(ss[:, 8:8 + NT], ss[:, 0:NT], ACT.Sqrt, bias=eps[:, 0:1], scale=1.0 / D).then_inc(
                    S("x_rms"), 1)
                act.wait_ge(*W("x_rstd", 1))
                for t in range(NT):
                    act.mul(xt[:, t, :], rows_in[:, t, :], rstd[:, t:t + 1]).then_inc(S("xn_ready"), 1)
                for n, (kind, i) in enumerate(jobs):
                    if kind in ("par", "ada", "adaT"):
                        if n >= EARLY:
                            modulation_job(L, n)
                        continue
                    u = n % 4
                    if kind == "norm" and i == 0:
                        act.wait_ge(*W("mod_ready", 1))
                    if kind == "g" and i:
                        act.wait_ge(*W("v_made", i))
                    if kind == "xbc" and i >= 2:
                        act.wait_ge(*W("taps_done", i - 1))
                    if kind == "xbc" and i == 0:
                        act.wait_ge(*W("pads_ready", 1))
                    if kind == "z" and i == main[0]:
                        act.wait_ge(*W("gp_out", 4 * 16))
                    if kind == "mean":
                        for b in range(2):
                            act.wait_ge(*W(f"sz_out{b}", 16 * len(main) // 2))
                    act.wait_ge(*W("pe_job", n + 1))
                    if kind == "norm":
                        st = 0 if i >= NCT else 1
                        for k in range(KD // 2):
                            ins = act.activation(uT[:, k, i * P:(i + 1) * P],
                                                 PS[:, 2 * u + k // 4, (k % 4) * P:(k % 4 + 1) * P],
                                                 ACT.Identity, bias=modc[:, 0, st, k:k + 1], scale=scl[:, 0, st, k:k + 1])
                    elif kind in ("g", "a"):
                        for s in segs(main):
                            dst = (sg if kind == "g" else asb)[:, SEG[s][0]:SEG[s][0] + SEG[s][1]]
                            ins = act.activation(dst, seg_banks(u, s), ACT.Sigmoid if kind == "g" else ACT.Copy)
                    elif kind == "dt":
                        for s in (0, 1):
                            ins = act.copy(dtT[:, SEG[s][0]:SEG[s][0] + SEG[s][1]], PS[0:32, 2 * u + s, 0:SEG[s][1]])
                    elif kind == "z":
                        zi = main.index(i)
                        if zi >= 2:
                            act.wait_ge(*W(f"sz_out{zi % 2}", 16 * (zi // 2)))
                        ins = act.activation(szt[:, zi % 2, :], unit2(u), ACT.Silu)
                    elif kind == "dtT":
                        ins = act.copy(dts[:, D1, :], PS[:, 2 * u, 0:DTN])
                    elif kind == "cum":
                        for b, dst in ((0, EC), (1, ER)):
                            act.activation(dts[:, dst, :], PS[:, 2 * u, b * 256:b * 256 + DTN], ACT.Exp)
                        ins = act.activation(dts[:, ET, :], PS[:, 2 * u + 1, 0:DTN], ACT.Exp)
                    elif kind == "xbc":
                        for s in (0, 1):
                            f = g5 + c5(0 if s == 0 else NCT)
                            ins = act.copy(pre5[:, i % 2, f:f + SEG[s][1]], seg_banks(u, s))
                    elif kind == "xT":
                        dst = xtok[:, :, i * P:(i + 1) * P] if i < 8 else btok[:, :, (i - 8) * P:(i - 7) * P]
                        act.copy(dst[:, 0:4, :], PS[:, 2 * u, :].rearrange("p (t n) -> p t n", n=P))
                        ins = act.copy(dst[:, 4:6, :], PS[:, 2 * u + 1, 0:256].rearrange("p (t n) -> p t n", n=P))
                    elif kind == "mean":
                        for s in segs(main):
                            f = c31(0 if s == 0 else NCT)
                            ins = act.copy(mean[:, f:f + SEG[s][1]], seg_banks(u, s))
                    ins.then_inc(S("act_job"), 1)
                    if kind == "z":
                        act.wait_ge(*W("act_job", n + 1))
                        act.dma_start(sz_d[i * P:(i + 1) * P, :], szt[:, zi % 2, :]).then_inc(S(f"sz_out{zi % 2}"), 16)
                    if kind == "dtT":
                        act.wait_ge(*W("sp_abs", 1))
                        act.activation(dts[:, D3, :], dts[:, D2, :], ACT.Exp, scale=-1.0).then_inc(S("sp_exp"), 1)
                        act.wait_ge(*W("sp_one", 1))
                        act.activation(dts[:, EC, :], dts[:, D2, :], ACT.Ln).then_inc(S("sp_ln"), 1)
                        act.activation(hdrow[:, 3, :], hdrow[:, 1, :], ACT.Exp).then_inc(S("a_exp"), 1)
                    if kind == "xbc" and i >= 1:
                        silu5(i - 1)
                        if i == 15:
                            silu5(15)
                for k in range(KD):
                    act.wait_ge(*W("vc_ready", k + 1))
                    if k >= 2:
                        act.wait_ge(*W("sq_used", k - 1))
                    act.activation(sqb[:, k % 2, v0:v0 + vw], vT[:, k, v0:v0 + vw], ACT.Square).then_inc(S("sq_ready"), 1)
                act.wait_ge(*W("sq_used", KD))
                for s in segs(main):
                    f = c31(0 if s == 0 else NCT)
                    ins = act.activation(rs[:, f:f + SEG[s][1]], seg_banks(0, s), ACT.Sqrt, bias=eps[:, 0:1])
                ins.then_inc(S("var_taken"), 1)
                def finish_v(k):
                    act.wait_ge(*W("vn_ready", k + 1))
                    act.activation(vT[:, k, v0:v0 + vw], vT[:, k, v0:v0 + vw], ACT.Silu,
                                   bias=par[:, COL["ln_b"] + k:COL["ln_b"] + k + 1],
                                   scale=par[:, COL["ln_g"] + k:COL["ln_g"] + k + 1]).then_inc(S("v_ready"), 1)

                for q, (ch, g) in enumerate((ch, g) for ch in main for g in range(G)):
                    act.wait_ge(*W("arg_ready", q + 1))
                    if q >= 2:
                        act.wait_ge(*W("m_ready", q - 1))
                    act.activation(E[:, q % 2, :], PS[:, 0, :], ACT.Exp).then_inc(S("e_ready"), 1)
                    act.wait_ge(*W("sul_ready", 2 * q + 2))
                    for r in range(R):
                        f = ch * 32 + H + g * R + r
                        ins = act.mul(GA[:, q % 2, r * P:(r + 1) * P], SUL[:, q % 2, 1, :], dts[:, DTV, f:f + 1])
                    ins.then_inc(S("ga_ready"), 1)
                    if 1 <= q <= KD:
                        finish_v(q - 1)

                rows_made = [KD]

                def wo_high(count_):
                    for r in range(rows_made[0], min(rows_made[0] + count_, len(main) * KD)):
                        n = len(slots) + r // 2
                        act.wait_ge(*W(f"w_in{n % WS}", 16 * (n // WS + 1)))
                        if r >= KD + WOH:
                            act.wait_ge(*W("wo_used", r - WOH + 1))
                        act.copy(woh[r % WOH][:], wslot[:, n % WS, (r % 2) * D:(r % 2 + 1) * D]).then_inc(S("woh_made"), 1)
                        rows_made[0] = r + 1

                def take_yT(n):
                    act.wait_ge(*W("ynT_done", n + 1))
                    for k in range(KD // 2):
                        ins = act.mul(yT[:, main[n], k, :], PS[:, 4 + 2 * (n % 2) + k // 4, (k % 4) * P:(k % 4 + 1) * P],
                                      par[:, COL["norm_g"] + k:COL["norm_g"] + k + 1])
                    ins.then_inc(S("yT_fa"), 1)
                    act.wait_ge(*W("yT_fa", n + 1))
                    act.copy(yhi[:, main[n], 0:KD // 2, :], yT[:, main[n], 0:KD // 2, :]).then_inc(S("yT_ready"), 1)

                for name, v in (("ga_ready", len(main) * G), ("yd_ready", len(main) * G), ("o_taken", len(reads(main))),
                                ("h_ready", len(UPDATES)), ("xw_ready", len(UPDATES))):
                    act.wait_ge(*W(name, v))
                for n, t in enumerate(main):
                    act.wait_ge(*W("yz_ready", n + 1))
                    if n:
                        act.wait_ge(*W("y_rstd", n))
                    rms(Y[:, t, :], otmp[:], 0, "y", n)
                    act.wait_ge(*W("y_rstd", n + 1))
                    act.mul(Y[:, t, :], Y[:, t, :], rstd[:, n:n + 1]).then_inc(S("yn_ready"), 1)
                    if n:
                        take_yT(n - 1)
                wo_high(WOH)
                take_yT(len(main) - 1)
                wo_high(KD - WOH)

                def take_u2(n):
                    act.wait_ge(*W("u2T_done", n + 1))
                    if n:
                        act.wait_ge(*W("logit_ready", n))
                    st = 0 if main[n] >= NCT else 1
                    for k in range(KD):
                        ins = act.activation(u2T[:, k, :],
                                             PS[:, 4 * ((n // 2) % 2) + k // 4, (k % 4) * P:(k % 4 + 1) * P], ACT.Identity,
                                             bias=modc[:, 3, st, k:k + 1], scale=scl[:, 1, st, k:k + 1])
                    ins.then_inc(S("u2_ready"), 1)

                for n in range(0, len(main), 2):
                    wo_high(WOH)
                    act.wait_ge(*W("wo_used", (n + 2) * KD))
                    if n:
                        act.wait_ge(*W("x1_rstd", n))
                    for r in (n, n + 1):
                        b = 4 * ((r // 2) % 2) + 2 * (r % 2)
                        rms(PS[:, b:b + 2, :].rearrange("p b n -> p (b n)"), xn2[:, r, :], 4 * (r % 2), "m", r)
                    wo_high(2)
                    for r in (n, n + 1):
                        act.wait_ge(*W("x1_ready", r + 1))
                        rms(xres[:, r % 2, :], xn2[:, r, :], 4 * (r % 2) + 2, "x1", r)
                        wo_high(1)
                    for r in (n, n + 1):
                        act.wait_ge(*W("x1_rstd", r + 1))
                        act.mul(xn2[:, r, :], xres[:, r % 2, :], rstd[:, 2 * (r % 2) + 1:2 * (r % 2) + 2]).then_inc(
                            S("xn2_ready"), 1)
                        wo_high(1)
                    for r in (n, n + 1):
                        wo_high(2)
                        take_u2(r)
                    wo_high(2)
                    for r in (n, n + 1):
                        act.wait_ge(*W("lmax_ready", r + 1))
                        act.activation(aff[:, r, :], logits(r), ACT.Exp, bias=sm[:, 0, r:r + 1],
                                       accum_out=sm[:, 1, r:r + 1]).then_inc(S("lexp_ready"), 1)

                def high(u, width):
                    slot, turn = slot_turn(u)
                    act.wait_ge(*W(f"unit_in{slot}", 16 * turn + 16))
                    if not isinstance(turn, int) or turn:
                        act.wait_ge(*W("unit_used", number(u) - RING + 1))
                    act.copy(whi[:, slot, 0:width], wr[:, slot, 0:width]).then_inc(S("hi_made"), 1)

                def take_sel(e):
                    act.wait_ge(*W("selT_done", e + 1))
                    for st, (lo, hi) in enumerate(((0, CL), (CL, slot_n))):
                        for k in range(KD // 2) if hi > lo else ():
                            ins = act.activation(selF[:, k, lo:hi], PS[:, k // 4, (k % 4) * P + lo:(k % 4) * P + hi],
                                                 ACT.Identity, bias=modc[:, 3, st, k:k + 1], scale=scl[:, 1, st, k:k + 1])
                    ins.then_inc(S("selF_act"), 1)
                    act.wait_ge(*W("selF_act", e + 1))
                    act.copy(shi[:, 0:KD // 2, 0:slot_n], selF[:, 0:KD // 2, 0:slot_n]).then_inc(S("selT_act"), 1)

                def down_out(par, e):
                    act.wait_ge(*W("unit_used", number(dn(e, JF - 1)) + 1))
                    act.wait_ge(*W("gate_cur", e + 1))
                    act.wait_ge(*W("scattered", 16 * e + 16))
                    act.mul(ob[0:slot_n, par, :], PS[0:slot_n, 6:8, :].rearrange("p b n -> p (b n)"),
                            gcur[0:slot_n, par:par + 1]).then_inc(S("dn_free"), 1)

                def expert(par, e, first=False, last=False):
                    for i in range(AHEAD, GU):
                        high(gu(e, i), FE)
                    for j in range(7) if not first else ():
                        high(dn(e - 1, j), D)
                    for b, (f, w) in enumerate(FB):
                        if b == 0:
                            act.wait_ge(*W("unit_used", number(gu(e, GU - 1)) + 1))
                        if b or not first:
                            act.wait_ge(*W("h_rows", 3 * e + b))
                        act.activation(hs[0:slot_n, 0:w], PS[0:slot_n, b, 0:w], ACT.Silu).then_inc(S("hs_ready"), 1)
                        if not first:
                            high(dn(e - 1, 7 + b), D)
                    if not last:
                        take_sel(e + 1)
                    if not first:
                        high(dn(e - 1, JF - 1), D)
                        for i in range(AHEAD) if not last else ():
                            high(gu(e + 1, i), FE)
                    act.wait_ge(*W("hT_done", e + 1))
                    for j, n in ((0, 4), (4, 4), (8, 3)):
                        ins = act.copy(hhi[:, par, j:j + n, 0:slot_n],
                                       PS[:, 2 + j // 4, 0:n * P].rearrange("p (j s) -> p j s", s=P)[:, :, 0:slot_n])
                    ins.then_inc(S("hT_act"), 1)
                    if first:
                        for i in range(AHEAD):
                            high(gu(e + 1, i), FE)
                    if not first:
                        down_out(1 - par, e - 1)

                act.wait_ge(*W("affT_taken", 1))
                for i in range(AHEAD):
                    high(gu(0, i), FE)
                take_sel(0)
                expert(0, 0, first=True)
                with act.Fori(1, NE - 3, 2) as e:
                    expert(1, e)
                    expert(0, e + 1)
                for e in range(NE - 3, NE):
                    expert(e % 2, e, last=e == NE - 1)
                for j in range(JF):
                    high(dn(NE - 1, j), D)
                down_out(1, NE - 1)
                for n in range(EARLY) if L < DEPTH - 1 else ():
                    modulation_job(L + 1, n)
                act.wait_ge(*W("yt_in", 16))
                for n, t in enumerate(main):
                    if n:
                        act.wait_ge(*W("f_sq", n))
                    act.activation(junk[:], yt[:, t, :], ACT.Square, accum_out=ss[:, t:t + 1]).then_inc(S("f_sq"), 1)
                act.wait_ge(*W("f_sq", len(main)))
                act.activation(ss[:, 8:8 + NT], ss[:, 0:NT], ACT.Sqrt, bias=eps[:, 0:1], scale=1.0 / D).then_inc(
                    S("f_rms"), 1)

        @block.vector
        def _(dve):
            chained = [0]

            def chain(ins):
                chained[0] += 1
                ins.then_inc(sem("dve_chain"), 1)
                dve.wait_ge(sem("dve_chain"), chained[0])

            def seen(ins, at_name, n):
                ins.then_inc(sem(at_name), 1)
                dve.wait_ge(*counter(L)(at_name, n))

            dve.memset(eps[:, 0:1], EPS).then_inc(sem("eps_set"), 1)
            dve.memset(cstat[:], 0.0).then_inc(sem("cstat_zero"), 1)
            for L, main, jobs, slots in LAYERS:
                S, W = sem, counter(L)
                slot_n = CL + (CC if main[0] == 0 else 0)
                v0, vw = seg_cols(main, g31)
                TT, TS, STT = dve.tensor_tensor, dve.tensor_scalar, dve.scalar_tensor_tensor

                def inv(dst, src):
                    return dve.reciprocal(dst, src)

                dve.wait_ge(*W("x_rms", 1))
                inv(rstd[:, 0:NT], ss[:, 8:8 + NT]).then_inc(S("x_rstd"), 1)
                dtr = lambda i: dts[:, i, :].rearrange("p (t h) -> p t h", t=NT)
                over_t = lambda i: hdrow[:, i, :].unsqueeze(1).to_broadcast([P, NT, 2 * H])

                def dt_quantities():
                    dve.wait_ge(*W("act_job", jobs.index(("dtT", 0)) + 1))
                    chain(TT(dtr(D1), dtr(D1), over_t(0), ALU.add))
                    STT(dts[:, D2, :], dts[:, D1, :], -1.0, dts[:, D1, :], ALU.mult, ALU.max).then_inc(S("sp_abs"), 1)
                    chain(TS(dts[:, D1, :], dts[:, D1, :], 0.0, None, ALU.max))
                    dve.wait_ge(*W("sp_exp", 1))
                    TS(dts[:, D2, :], dts[:, D3, :], 1.0, None, ALU.add).then_inc(S("sp_one"), 1)
                    dve.wait_ge(*W("sp_one", 1))
                    chain(TS(dts[:, WDT, :], dts[:, D2, :], 1.0, 1e-30, ALU.subtract, ALU.max))
                    chain(inv(dts[:, WDT, :], dts[:, WDT, :]))
                    chain(STT(dts[:, DTV, :], dts[:, D2, :], 1.0, dts[:, D3, :], ALU.is_le, ALU.mult))
                    chain(TT(dts[:, DTV, :], dts[:, DTV, :], dts[:, D1, :], ALU.add))
                    chain(TT(dts[:, WDT, :], dts[:, WDT, :], dts[:, D3, :], ALU.mult))
                    dve.wait_ge(*W("sp_ln", 1))
                    chain(TT(dts[:, WDT, :], dts[:, WDT, :], dts[:, EC, :], ALU.mult))
                    chain(TT(dts[:, DTV, :], dts[:, DTV, :], dts[:, WDT, :], ALU.add))
                    dve.wait_ge(*W("a_exp", 1))
                    chain(TT(dtr(DA), dtr(DTV), over_t(3), ALU.mult))
                    TS(dts[:, DA, :], dts[:, DA, :], -1.0, None, ALU.mult).then_inc(S("da_ready"), 1)

                def taps(j):
                    dve.wait_ge(*W("act_job", jobs.index(("xbc", j)) + 1))
                    if j >= 3:
                        if j - 3 < 8:
                            dve.wait_ge(*W("pe_job", jobs.index(("xT", j - 3)) + 1))
                        else:
                            dve.wait_ge(*W("conv_done", j - 2))
                    tap = lambda k: par[:, COL["conv_w"] + k * 16 + j:COL["conv_w"] + k * 16 + j + 1]
                    a = acc5[:, j % 3, :]
                    chain(TS(a, pre5[:, j % 2, 0:W5], tap(0), None, ALU.mult))
                    for k in range(1, K5):
                        ins = STT(a, pre5[:, j % 2, k:k + W5], tap(k), a, ALU.mult, ALU.add)
                        if k < K5 - 1:
                            chain(ins)
                    ins.then_inc(S("taps_done"), 1)

                dve.wait_ge(*W("mod_ready", 1))
                for t in range(NT):
                    st = 0 if t >= NCT else 1
                    n = jobs.index(("norm", t))
                    dve.wait_ge(*W("pe_job", n + 1))
                    for k in range(KD // 2, KD):
                        ins = TS(uT[:, k, t * P:(t + 1) * P], PS[:, 2 * (n % 4) + k // 4, (k % 4) * P:(k % 4 + 1) * P],
                                 scl[:, 0, st, k:k + 1], modc[:, 0, st, k:k + 1], ALU.mult, ALU.add)
                    ins.then_inc(S("norm_dve"), 1)
                early = 2
                first_col = par[:, COL["dw_w"]:COL["dw_w"] + K31 * KD]
                for j in range(KD):
                    if j == (KD - 1 if main[0] == 0 else KD - 2):
                        dt_quantities()
                    if j == KD - 1:
                        for e in range(early):
                            taps(e)
                    dve.wait_ge(*W("v_made", j + 1))
                    tap = lambda k: first_col[:, k * KD + j:k * KD + j + 1]
                    a = cacc[:, j % 2, v0:v0 + vw]
                    chain(TS(a, vT[:, j, v0 + 1:v0 + 1 + vw], tap(1), par[:, COL["dw_b"] + j:COL["dw_b"] + j + 1],
                             ALU.mult, ALU.add))
                    for k in range(2, K31):
                        chain(STT(a, vT[:, j, v0 + k:v0 + k + vw], tap(k), a, ALU.mult, ALU.add))
                    STT(vT[:, j, v0:v0 + vw], vT[:, j, v0:v0 + vw], tap(0), a, ALU.mult, ALU.add).then_inc(S("conf_done"), 1)
                for j in range(early, XBC // P):
                    taps(j)
                dve.wait_ge(*W("act_job", jobs.index(("cum", 0)) + 1))
                for d in range(2):
                    ins = TT(dtr(WDT)[:, :, d * H:(d + 1) * H], dtr(DTV)[:, :, d * H:(d + 1) * H],
                             dts[:, ER, d * 96:(d + 1) * 96].rearrange("p (t h) -> p t h", h=H), ALU.mult)
                ins.then_inc(S("wdt_ready"), 1)
                dve.wait_ge(*W("act_job", len(jobs)))
                for k in range(KD):
                    for s in segs(main):
                        f = c31(0 if s == 0 else NCT)
                        ins = TT(vT[:, k, f:f + SEG[s][1]], vT[:, k, f:f + SEG[s][1]], mean[:, f:f + SEG[s][1]], ALU.subtract)
                    ins.then_inc(S("vc_ready"), 1)
                dve.wait_ge(*W("var_taken", 1))
                for s in segs(main):
                    f = c31(0 if s == 0 else NCT)
                    chain(inv(rs[:, f:f + SEG[s][1]], rs[:, f:f + SEG[s][1]]))
                def normalise(k):
                    for s in segs(main):
                        f = c31(0 if s == 0 else NCT)
                        ins = TT(vT[:, k, f:f + SEG[s][1]], vT[:, k, f:f + SEG[s][1]], rs[:, f:f + SEG[s][1]], ALU.mult)
                    ins.then_inc(S("vn_ready"), 1)

                dve.wait_ge(*W("y_init", len(main)))
                todo = [(ch, g) for ch in main for g in range(G)]

                def add_outputs(q):
                    ch, g = todo[q]
                    dve.wait_ge(*W("yd_ready", q + 1))
                    yv = Y[:, ch, g * 256:(g + 1) * 256].rearrange("p (a b n) -> p a b n", a=2, b=2)
                    pv = PS[:, 3, :].rearrange("p (a c n) -> p a c n", a=2, n=HD)[:, :, 0:4:3, :]
                    return TT(yv, yv, pv, ALU.add).then_inc(S("yd_taken"), 1)

                done = {"read": 0, "upd": 0}

                def state_step(d, n, ch):
                    per_head = lambda buf, f: dts[:, buf, f:f + H].unsqueeze(2).to_broadcast([P, H, HD])
                    ov = otmp[:].rearrange("p (h n) -> p h n", h=H)
                    if (d, n, ch) in reads(main):
                        dve.wait_ge(*W("o_ready", done["read"] + 1))
                        seen(TT(ov, PS[:, 4:6, :].rearrange("p b (h n) -> p (b h) n", n=HD), per_head(EC, d * 96 + ch * H),
                                ALU.mult), "o_taken", done["read"] + 1)
                        done["read"] += 1
                        chain(TT(Y[:, ch, :], Y[:, ch, :], otmp[:], ALU.add))
                    if (d, n, ch) in UPDATES:
                        if n:
                            hv = hst[:, d, :].rearrange("p (h n) -> p h n", h=H)
                            chain(TT(hv, hv, per_head(ET, ch * 32 + d * H), ALU.mult))
                        dve.wait_ge(*W("st_ready", done["upd"] + 1))
                        new = PS[:, 6:8, :].rearrange("p b n -> p (b n)")
                        if n:
                            ins = TT(hst[:, d, :], hst[:, d, :], new, ALU.add)
                        else:
                            ins = dve.tensor_copy(hst[:, d, :], new)
                        done["upd"] += 1
                        seen(ins, "h_ready", done["upd"])

                def mask_scores(q):
                    dve.wait_ge(*W("s_ready", q + 1))
                    if q >= 2:
                        dve.wait_ge(*W("ga_ready", q - 1))
                    for b, mk in enumerate((LE, GE)):
                        TT(SUL[:, q % 2, b, :], PS[:, 1 + q % 2, 0:P], masks[:, mk, :], ALU.mult).then_inc(
                            S("sul_ready"), 1)

                mask_scores(0)
                for q, (ch, g) in enumerate(todo):
                    if q + 1 < len(todo):
                        mask_scores(q + 1)
                    dve.wait_ge(*W("ga_ready", q + 1))
                    if q >= 2:
                        dve.wait_ge(*W("yd_ready", q - 1))
                    for r in range(R):
                        f = ch * 32 + g * R + r
                        ins = STT(GB[:, q % 2, r * P:(r + 1) * P], SUL[:, q % 2, 0, :], dts[:, DTV, f:f + 1],
                                  GA[:, q % 2, r * P:(r + 1) * P], ALU.mult, ALU.add)
                    chain(ins)
                    dve.wait_ge(*W("e_ready", q + 1))
                    TT(GB[:, q % 2, :], GB[:, q % 2, :], E[:, q % 2, :], ALU.mult).then_inc(S("m_ready"), 1)
                    if q:
                        add_outputs(q - 1)
                    if q < KD:
                        normalise(q)
                    for s in steps_at(main, q):
                        if q:
                            dve.wait_ge(*W("yd_taken", q))
                        state_step(*s)
                add_outputs(len(todo) - 1)
                dve.wait_ge(*W("yd_taken", len(todo)))
                rows_made = [KD]

                def wo_low(count_):
                    for r in range(rows_made[0], min(rows_made[0] + count_, len(main) * KD)):
                        n = len(slots) + r // 2
                        dve.wait_ge(*W("woh_made", r - KD + 1))
                        half = slice((r % 2) * D, (r % 2 + 1) * D)
                        TT(wol[:, n % WS, half], wslot[:, n % WS, half], woh[r % WOH][:].bitcast(F32), ALU.subtract).then_inc(
                            S("wol_made"), 1)
                        rows_made[0] = r + 1

                def v_low(k):
                    dve.wait_ge(*W("vhi_made", k + 1))
                    for s in segs(main):
                        f, t0 = c31(0 if s == 0 else NCT), SEG[s][0]
                        ins = TT(vlo[:, k, f:f + SEG[s][1]], vT[:, k, f:f + SEG[s][1]],
                                 vhi[:, k, t0:t0 + SEG[s][1]].bitcast(F32), ALU.subtract)
                    ins.then_inc(S("vlo_made"), 1)

                def take_yT(n):
                    dve.wait_ge(*W("ynT_done", n + 1))
                    for k in range(KD // 2, KD):
                        ins = TS(yT[:, main[n], k, :], PS[:, 4 + 2 * (n % 2) + k // 4, (k % 4) * P:(k % 4 + 1) * P],
                                 par[:, COL["norm_g"] + k:COL["norm_g"] + k + 1], None, ALU.mult)
                    seen(ins, "yT_fd", n + 1)
                    seen(dve.tensor_copy(yhi[:, main[n], KD // 2:KD, :], yT[:, main[n], KD // 2:KD, :]), "yhi_dve", n + 1)
                    dve.wait_ge(*W("yT_ready", n + 1))
                    TT(ylo[:, main[n], :, :], yT[:, main[n], :, :], yhi[:, main[n], :, :].bitcast(F32), ALU.subtract).then_inc(
                        S("yT_dve"), 1)

                for n, t in enumerate(main):
                    dve.wait_ge(*W(f"szl_in{n % 2}", 16 * (n // 2 + 1)))
                    TT(Y[:, t, :], Y[:, t, :], szl[:, n % 2, :], ALU.mult).then_inc(S("yz_ready"), 1)
                    dve.wait_ge(*W("y_rms", n + 1))
                    inv(rstd[:, n:n + 1], ss[:, 1:2]).then_inc(S("y_rstd"), 1)
                    if n:
                        take_yT(n - 1)
                take_yT(len(main) - 1)
                dve.wait_ge(*W("wo_used", KD))
                for k in range(KD):
                    wo_low(1)
                    v_low(k)
                for n in range(0, len(main), 2):
                    wo_low(WOH)
                    for r in (n, n + 1):
                        st = 0 if main[r] >= NCT else 1
                        b = 4 * ((r // 2) % 2) + 2 * (r % 2)
                        c = 2 * (r % 2)
                        dve.wait_ge(*W("m_rms", r + 1))
                        chain(inv(rstd[:, c:c + 1], ss[:, 2 * c + 1:2 * c + 2]))
                        if r == 0:
                            dve.wait_ge(*W("gpb_in", 32))
                        seen(STT(xn2[:, r, :], PS[:, b:b + 2, :].rearrange("p b n -> p (b n)"), rstd[:, c:c + 1],
                                 gpb[:, st, :], ALU.mult, ALU.mult), "m_taken", r + 1)
                        dve.wait_ge(*W(f"xres_in{r % 2}", 16 * (r // 2 + 1)))
                        TT(xres[:, r % 2, :], xres[:, r % 2, :], xn2[:, r, :], ALU.add).then_inc(S("x1_ready"), 1)
                        wo_low(1)
                    for r in (n, n + 1):
                        c = 2 * (r % 2)
                        dve.wait_ge(*W("x1_rms", r + 1))
                        inv(rstd[:, c + 1:c + 2], ss[:, 2 * c + 3:2 * c + 4]).then_inc(S("x1_rstd"), 1)
                        wo_low(1)
                    wo_low(6)
                    for r in (n, n + 1):
                        dve.wait_ge(*W("logit_ready", r + 1))
                        chain(dve.reduce_max(sm[:, 2, r:r + 1], logits(r), AX_X))
                        TS(sm[:, 0, r:r + 1], sm[:, 2, r:r + 1], -1.0, None, ALU.mult).then_inc(S("lmax_ready"), 1)
                        if r == n:
                            wo_low(2)
                    for r in (n, n + 1):
                        dve.wait_ge(*W("lexp_ready", r + 1))
                        chain(inv(sm[:, 3, r:r + 1], sm[:, 1, r:r + 1]))
                        TS(aff[:, r, :], aff[:, r, :], sm[:, 3, r:r + 1], None, ALU.mult).then_inc(S("aff_ready"), 1)
                npt = 48 if main[0] == 0 else NE
                for i in range(2):
                    dve.wait_ge(*W(f"xn_out{i}", 16 * len(main) // 2))
                dve.wait_ge(*W("affT_done", 1))
                chain(dve.memset(affT[:], -1.0))
                if main[0] == 0:
                    dve.tensor_copy(affT[32:32 + NE, 0:CTX], PS[0:NE, 4, 0:CTX])
                seen(dve.tensor_copy(affT[0:NE, :], PS[0:NE, 5, :]), "affT_taken", 1)
                for r in range(CL // 8):
                    c8 = slice(8 * r, 8 * r + 8)
                    chain(dve.max(topv[0:npt, c8], affT[0:npt, :]))
                    dve.max_index(topi_u[0:npt, c8], topv[0:npt, c8], affT[0:npt, :])
                    chain(dve.match_replace(affT[0:npt, :], topv[0:npt, c8], affT[0:npt, :], -1.0))
                if main[0] == 0:
                    dve.tensor_copy(gi[:, 0, CL:SL], topv[32:32 + NE, 0:CC])
                    dve.tensor_copy(gi[:, 1, CL:SL], topi_u[32:32 + NE, 0:CC])
                dve.tensor_copy(gi[:, 0, 0:CL], topv[0:NE, :])
                chain(dve.tensor_copy(gi[:, 1, 0:CL], topi_u[0:NE, :]))
                TS(gi[:, 1, 0:CL], gi[:, 1, 0:CL], float(CTX), None, ALU.add).then_inc(S("gi_ready"), 1)
                dve.wait_ge(*W("giT_done", 1))
                chain(dve.tensor_copy(gateT[0:slot_n, :], PS[0:slot_n, 6, 0:NE]))
                seen(dve.tensor_copy(idxT_u[0:slot_n, :], PS[0:slot_n, 6, NE:2 * NE]), "dn_free", 1)

                def next_rows(e):
                    dve.tensor_copy(idg_u[0:slot_n, :], idxT_u[0:slot_n, bass.ds(e, 1)]).then_inc(S("idg_ready"), 1)

                def low(u, width):
                    slot, _ = slot_turn(u)
                    dve.wait_ge(*W("hi_made", number(u) + 1))
                    TT(wlo[:, slot, 0:width], wr[:, slot, 0:width], whi[:, slot, 0:width].bitcast(F32), ALU.subtract).then_inc(
                        S("lo_made"), 1)

                def take_sel(e):
                    half = slice(KD // 2, KD)
                    dve.wait_ge(*W("selT_done", e + 1))
                    for st, (lo, hi) in enumerate(((0, CL), (CL, slot_n))):
                        for k in range(KD // 2, KD) if hi > lo else ():
                            ins = TS(selF[:, k, lo:hi], PS[:, k // 4, (k % 4) * P + lo:(k % 4) * P + hi],
                                     scl[:, 1, st, k:k + 1], modc[:, 3, st, k:k + 1], ALU.mult, ALU.add)
                    ins.then_inc(S("selF_dve"), 1)
                    dve.wait_ge(*W("selF_dve", e + 1))
                    dve.tensor_copy(shi[:, half, 0:slot_n], selF[:, half, 0:slot_n]).then_inc(S("shi_dve"), 1)
                    dve.wait_ge(*W("shi_dve", e + 1))
                    dve.wait_ge(*W("selT_act", e + 1))
                    TT(slo[:, :, 0:slot_n], selF[:, :, 0:slot_n], shi[:, :, 0:slot_n].bitcast(F32), ALU.subtract).then_inc(
                        S("selT_dve"), 1)

                def scatter_rows(par, e):
                    dve.wait_ge(*W("scattered", 16 * e + 16))
                    dve.tensor_copy(ids_u[0:slot_n, par:par + 1], idxT_u[0:slot_n, bass.ds(e, 1)])
                    dve.tensor_copy(gcur[0:slot_n, par:par + 1], gateT[0:slot_n, bass.ds(e, 1)]).then_inc(S("gate_cur"), 1)

                def expert(par, e, first=False, nxt=True, last=False):
                    for i in range(AHEAD, GU):
                        low(gu(e, i), FE)
                    for j in range(7) if not first else ():
                        low(dn(e - 1, j), D)
                    for b, (f, w) in enumerate(FB):
                        dve.wait_ge(*W("hs_ready", 3 * e + b + 1))
                        if b == 0 and not first:
                            dve.wait_ge(*W("hT_done", e))
                        TT(hh[0:slot_n, f:f + w], hs[0:slot_n, 0:w], PS[0:slot_n, 3 + b, 0:w], ALU.mult).then_inc(
                            S("h_rows"), 1)
                        if not first:
                            low(dn(e - 1, 7 + b), D)
                    if not last:
                        take_sel(e + 1)
                        if nxt:
                            next_rows(e + 2)
                    if not first:
                        low(dn(e - 1, JF - 1), D)
                        for i in range(AHEAD) if not last else ():
                            low(gu(e + 1, i), FE)
                        scatter_rows(1 - par, e - 1)
                    dve.wait_ge(*W("hT_act", e + 1))
                    for j, n in ((0, 4), (4, 4), (8, 3)):
                        ins = TT(hlo[:, par, j:j + n, 0:slot_n],
                                 PS[:, 2 + j // 4, 0:n * P].rearrange("p (j s) -> p j s", s=P)[:, :, 0:slot_n],
                                 hhi[:, par, j:j + n, 0:slot_n].bitcast(F32), ALU.subtract)
                    ins.then_inc(S("hT_dve"), 1)
                    if first:
                        for i in range(AHEAD):
                            low(gu(e + 1, i), FE)

                next_rows(0)
                take_sel(0)
                next_rows(1)
                dve.wait_ge(*W("lo_made", AHEAD))
                expert(0, 0, first=True)
                with dve.Fori(1, NE - 3, 2) as e:
                    expert(1, e)
                    expert(0, e + 1)
                for e in range(NE - 3, NE):
                    expert(e % 2, e, nxt=e + 2 < NE, last=e == NE - 1)
                for j in range(JF):
                    low(dn(NE - 1, j), D)
                scatter_rows(1, NE - 1)
                dve.wait_ge(*W("f_rms", 1))
                chain(inv(rstd[:, 0:NT], ss[:, 8:8 + NT]))
                dve.wait_ge(*W("gpb2_in", 32))
                dve.wait_ge(*W("xr_in", 16))
                for n, t in enumerate(main):
                    st = 0 if t >= NCT else 1
                    chain(STT(yt[:, t, :], yt[:, t, :], rstd[:, t:t + 1], gpb2[:, st, :], ALU.mult, ALU.mult))
                    TT(xr[:, t, :], xr[:, t, :], yt[:, t, :], ALU.add).then_inc(S("xf_ready"), 1)

        @block.gpsimd
        def _(pool):
            chained = [0]

            def chain(ins):
                chained[0] += 1
                ins.then_inc(sem("pool_chain"), 1)
                pool.wait_ge(sem("pool_chain"), chained[0])

            pool.memset(ones[:], 1.0)
            pool.memset(masks[:, AVG, :], 1.0 / D)
            chain(pool.memset(masks[:, 0:AVG, :], 1.0))
            for mk, op, b, cm, st in ((IDN, ALU.is_equal, 0, 1, -1), (LE, ALU.is_ge, 0, -1, 1), (GE, ALU.is_ge, 0, 1, -1),
                                      (GT, ALU.is_ge, -1, 1, -1), (LT, ALU.is_ge, -1, -1, 1)):
                ins = pool.affine_select(out=masks[:, mk, :], in_=masks[:, mk, :], compare_op=op, fill=0.0, base=b,
                                         pattern=[[st, P]], channel_multiplier=cm)
            ins.then_inc(sem("consts"), 1)
            for L, main, jobs, slots in LAYERS:
                S, W = sem, counter(L)
                slot_n = CL + (CC if main[0] == 0 else 0)
                TT = pool.tensor_tensor
                bcol = par[:, COL["ada_b"]:COL["ada_b"] + 48].rearrange("p (s k) -> p s k", k=KD)
                pool.wait_ge(*W("act_job", jobs.index(("par", 0)) + 1))
                for s in range(6):
                    if s in GATES:
                        gi_ = GATES.index(s)
                        pool.wait_ge(*W("act_job", jobs.index(("ada", s)) + 1))
                        if gi_ == 0:
                            pool.wait_ge(*W("brow_in", 8 * 16))
                        for r in (0, 32):
                            row = arow[r:r + 1, s % 2, :]
                            chain(TT(row, row, brow[r:r + 1, 2 * gi_, :], ALU.add))
                            TT(brow[r:r + 1, 2 * gi_ + 1, :], row, brow[r:r + 1, 2 * gi_ + 1, :], ALU.mult).then_inc(
                                S("gp_ready"), 1)
                            pool.wait_ge(*W("gp_ready", 2 * gi_ + r // 32 + 1))
                            pool.dma_start(gp_d[L, gi_, r // 32:r // 32 + 1, :], brow[r:r + 1, 2 * gi_ + 1, :]).then_inc(
                                S("gp_out"), 16)
                        continue
                    pool.wait_ge(*W("act_job", jobs.index(("adaT", s)) + 1))
                    chain(TT(modc[:, s, :, :], modc[:, s, :, :], bcol[:, s, :].unsqueeze(1).to_broadcast([P, 2, KD]), ALU.add))
                    if s in (1, 4):
                        chain(pool.tensor_scalar(scl[:, s // 4, :, :], modc[:, s, :, :], 1.0, None, ALU.add))
                        gain = par[:, COL["pre_g" if s == 1 else "moe_g"]:][:, 0:KD]
                        ins = TT(scl[:, s // 4, :, :], scl[:, s // 4, :, :], gain.unsqueeze(1).to_broadcast([P, 2, KD]), ALU.mult)
                        ins.then_inc(S("mod_ready"), 1)
                pool.wait_ge(*W("pe_job", jobs.index(("norm", NT - 1)) + 1))
                for j in range(KD):
                    for f in (0, g31 + CTX, 2 * g31 + T):
                        pool.memset(vT[:, j, f:f + g31], 0.0)
                for b in range(2):
                    for f in (0, g5 + CTX, 2 * g5 + T):
                        ins = pool.memset(pre5[:, b, f:f + g5], 0.0)
                ins.then_inc(S("pads_ready"), 1)
                for j in range(KD):
                    pool.wait_ge(*W("act_job", jobs.index(("a", j)) + 1))
                    for s in segs(main):
                        f = g31 + c31(0 if s == 0 else NCT)
                        w = slice(SEG[s][0], SEG[s][0] + SEG[s][1])
                        ins = TT(vT[:, j, f:f + SEG[s][1]], asb[:, w], sg[:, w], ALU.mult)
                    ins.then_inc(S("v_made"), 1)
                pool.wait_ge(*W("pe_job", jobs.index(("xT", 11)) + 1))
                pool.wait_ge(*W("act_job", jobs.index(("xT", 11)) + 1))
                pool.wait_ge(*W("pe_job", jobs.index(("xbc", 15)) + 1))
                heads = lambda ap: ap.rearrange("p (h n) -> p h n", h=H)
                for ch in main:
                    TT(heads(Y[:, ch, :]), heads(xtok[:, ch, :]), hdrow[:, 2, 0:H].unsqueeze(2).to_broadcast([P, H, HD]),
                       ALU.mult).then_inc(S("y_init"), 1)
                pool.wait_ge(*W("conv_done", 2 * KD))
                pool.wait_ge(*W("act_job", len(jobs)))
                def load_gates(ns):
                    for n in ns:
                        if n == 0:
                            pool.wait_ge(*W("vn_ready", KD))
                            for i in range(2):
                                pool.wait_ge(*W(f"sz_out{i}", 16 * len(main) // 2))
                        if n >= 2:
                            pool.wait_ge(*W("yz_ready", n - 1))
                        t = main[n]
                        pool.dma_start(szl[:, n % 2, :], sz_d[t * P:(t + 1) * P, :]).then_inc(S(f"szl_in{n % 2}"), 16)

                pool.wait_ge(*W("wdt_ready", 1))
                nupd = 0
                todo = [(ch, g) for ch in main for g in range(G)]

                def masked_da(q):
                    ch, g = todo[q]
                    if q >= 2:
                        pool.wait_ge(*W("arg_ready", q - 1))
                    for d, mk in ((0, LE), (1, GE)):
                        f = ch * 32 + d * H + g * R
                        ins = TT(dAm[:, q % 2, d, :].rearrange("p (r n) -> p r n", r=R),
                                 masks[:, mk, :].unsqueeze(1).to_broadcast([P, R, P]),
                                 dts[:, DA, f:f + R].unsqueeze(2).to_broadcast([P, R, P]), ALU.mult)
                    ins.then_inc(S("dam_ready"), 1)

                masked_da(0)
                for q in range(len(todo)):
                    if q + 1 < len(todo):
                        masked_da(q + 1)
                    for d, n, at_ in steps_at(main, q):
                        if (d, n, at_) in UPDATES:
                            if nupd:
                                pool.wait_ge(*W("st_ready", nupd))
                            f = at_ * 32 + d * H
                            TT(heads(xw[:]), heads(xtok[:, at_, :]), dts[:, WDT, f:f + H].unsqueeze(2).to_broadcast(
                                [P, H, HD]), ALU.mult).then_inc(S("xw_ready"), 1)
                            nupd += 1
                    if q == 2 * G - 1:
                        load_gates(range(2))
                for n in range(2, len(main)):
                    load_gates([n])
                pool.wait_ge(*W("yd_ready", len(todo)))
                pool.wait_ge(*W("v_ready", KD))
                for k in range(KD):
                    for s in segs(main):
                        f, t0 = c31(0 if s == 0 else NCT), SEG[s][0]
                        ins = pool.tensor_copy(vhi[:, k, t0:t0 + SEG[s][1]], vT[:, k, f:f + SEG[s][1]])
                    ins.then_inc(S("vhi_made"), 1)
                pool.wait_ge(*W("yn_ready", len(main)))
                for st in range(2):
                    pool.dma_start(gpb[:, st, :], gp_d[L, 0, st, :].partition_broadcast(P)).then_inc(S("gpb_in"), 16)
                pool.dma_start(rw[:], router_w[L].rearrange("(k p) e -> p k e", p=P)).then_inc(S("rw_in"), 16)
                if L:
                    pool.wait_ge(*counter(L - 1)("out_stored", 16 * NT))
                for n, t in enumerate(main):
                    if n >= 2:
                        pool.wait_ge(*W(f"x1_out{n % 2}", 16 * (n // 2)))
                        pool.wait_ge(*W("xn2_ready", n - 1))
                    pool.dma_start(xres[:, n % 2, :], src_rows(L, t)).then_inc(S(f"xres_in{n % 2}"), 16)
                    if n:
                        store_x1(pool, L, main, n - 1)
                store_x1(pool, L, main, len(main) - 1)
                for i in range(2):
                    pool.wait_ge(*W(f"x1_out{i}", 16 * len(main) // 2))
                    pool.wait_ge(*W(f"xn_out{i}", 16 * len(main) // 2))

                pool.wait_ge(*W("logit_ready", len(main)))
                chain(pool.memset(zro[:], 0.0))
                made = 0
                for i in range(2):
                    pool.dma_start(y_d[i * T // 2:(i + 1) * T // 2, :].rearrange("(t p) n -> p t n", p=P),
                                   zro[:].unsqueeze(1).to_broadcast([P, NT // 2, D])).then_inc(S("scattered"), 16)
                    while made < AHEAD * (i + 1) // 2:
                        pool.wait_ge(*W("hi_made", made + 1))
                        TT(wlo[:, made, :], wr[:, made, :], whi[:, made, :].bitcast(F32), ALU.subtract).then_inc(
                            S("lo_made"), 1)
                        made += 1
                    pool.wait_ge(*W("scattered", 16 * (i + 1)))

                def settle(n):
                    if L or not isinstance(n, int) or n:
                        pool.wait_ge(*W("settled", n))
                    TT(eps[:, 1:2], masks[:, IDN, 0:1], masks[:, IDN, 0:1], ALU.add).then_inc(S("settled"), 1)

                def gather(e, n):
                    pool.wait_ge(*W("idg_ready", e + 1))
                    settle(n)
                    pool.indirect_dma_start(out=sel[0:slot_n, :], out_offset=None, in_=xn_d,
                                            in_offset=bass.IndirectOffsetOnAxis(idg_u[0:slot_n, 0:1], 0)).then_inc(
                        S("sel_in"), 16)

                def scatter(par, e, n):
                    pool.wait_ge(*W("dn_free", e + 2))
                    pool.wait_ge(*W("scattered", 16 * e + 32))
                    settle(n)
                    pool.indirect_dma_start(out=y_d, out_offset=bass.IndirectOffsetOnAxis(ids_u[0:slot_n, par:par + 1], 0),
                                            in_=ob[0:slot_n, par, :], in_offset=None, compute_op=ALU.add).then_inc(
                        S("scattered"), 16)

                for e in range(3):
                    gather(e, e)
                with pool.Fori(1, NE - 3, 2) as e:
                    gather(e + 2, 2 * e + 1)
                    scatter(0, e - 1, 2 * e + 2)
                    gather(e + 3, 2 * e + 3)
                    scatter(1, e, 2 * e + 4)
                gather(NE - 1, 2 * NE - 5)
                for e in range(NE - 4, NE):
                    scatter(e % 2, e, NE + e)
                rows = lambda d: d.rearrange("(t p) n -> p t n", p=P)[:, main[0]:NT, :]
                pool.wait_ge(*W("unit_used", UNITS * NE))
                for st in range(2):
                    pool.dma_start(gpb2[:, st, :], gp_d[L, 1, st, :].partition_broadcast(P)).then_inc(S("gpb2_in"), 16)
                pool.dma_start(xr[:, main[0]:NT, :], rows(x1_d)).then_inc(S("xr_in"), 16)
                pool.wait_ge(*W("scattered", 32 + 16 * NE))
                pool.dma_start(yt[:, main[0]:NT, :], rows(y_d)).then_inc(S("yt_in"), 16)
                for n in range(len(main)):
                    store_out(pool, L, main, n)
            pool.wait_ge(*counter(DEPTH - 1)("out_stored", 16 * len(main)))


_INS = ["x", "c", "ctx", "c_ctx", "ada_w", "ada_b", "mix_pre_g", "w_in", "conv_w", "conv_b", "dt_bias", "a_log",
        "d_skip", "ssd_norm_g", "cm_dw_w", "cm_dw_b", "cm_ln_g", "cm_ln_b", "w_out", "mix_post_g", "moe_pre_g",
        "router_w", "exp_w_gate", "exp_w_up", "exp_w_down", "moe_post_g"]


def kernel(**inputs):
    import concourse.bacc as bacc
    from concourse.bass_utils import run_bass_kernel_spmd

    nc = bacc.Bacc("TRN2", target_bir_lowering=False, num_devices=1)
    arrays, aps = {}, {}
    for name in _INS:
        a = np.ascontiguousarray(inputs[name])
        arrays[f"in_{name}"] = a
        aps[name] = nc.dram_tensor(f"in_{name}", a.shape, mybir.dt.from_np(a.dtype), kind="ExternalInput").ap()
    out = nc.dram_tensor("out_x", (1, SEQ, D), F32, kind="ExternalOutput").ap()
    build(nc, out=out, **aps)
    r = run_bass_kernel_spmd(nc, [arrays], core_ids=[0])
    return r.results[0]["out_x"]
```
